# Optimizing a Trainium2 kernel written in Bass

```python
import math
import jax, jax.numpy as jnp
from jax import lax
import numpy as np

D_MODEL = 1024
BATCH = 1
SEQ = 256
DEPTH = 2

N_MEM = 256
HEAD_DIM = 64
SWA_HEADS = 8
SWA_KV_HEADS = 2
SWA_GROUP = SWA_HEADS // SWA_KV_HEADS
WINDOW = 128
SB_HEADS = 8
SB_BLOCK = 128
HGRN_HEAD_DIM = 128
HGRN_HEADS = D_MODEL // HGRN_HEAD_DIM
HGRN_CHUNK = 32
XA_HEADS = 4
XA_HEAD_DIM = D_MODEL // XA_HEADS
D_FF = 128 * ((8 * D_MODEL // 3 + 127) // 128)
CONV_WIDTH = 3
ROPE_THETA = 10000.0
EPS = 1e-6
N_EVEN = (DEPTH + 1) // 2
N_ODD = DEPTH // 2
SWA_Q_W = SWA_HEADS * HEAD_DIM
SWA_KV_W = SWA_KV_HEADS * HEAD_DIM
SB_W = SB_HEADS * HEAD_DIM
AB_IN = SWA_Q_W + 2 * SWA_KV_W + 3 * SB_W
AB_OUT = SWA_Q_W + SB_W


def rms_norm(x, gain):
    x32 = x.astype(jnp.float32)
    y = x32 * lax.rsqrt(jnp.mean(x32 * x32, axis=-1, keepdims=True) + EPS)
    return (y * gain.astype(jnp.float32)).astype(x.dtype)

def rope(x, positions):
    d = x.shape[-1]
    inv_freq = ROPE_THETA ** (-jnp.arange(0, d, 2, dtype=jnp.float32) / d)
    ang = positions.astype(jnp.float32)[..., None] * inv_freq
    cos, sin = jnp.cos(ang)[:, :, None, :], jnp.sin(ang)[:, :, None, :]
    x1, x2 = x[..., : d // 2], x[..., d // 2:]
    return jnp.concatenate([x1 * cos - x2 * sin, x2 * cos + x1 * sin], axis=-1)

def sliding_window_attention(q, k, v, sinks):
    B, S = q.shape[:2]
    nb = S // WINDOW
    qb = q.reshape(B, nb, WINDOW, SWA_KV_HEADS, SWA_GROUP, HEAD_DIM)

    def band(t):
        prev = jnp.pad(t, ((0, 0), (WINDOW, 0), (0, 0), (0, 0)))[:, :S]
        return jnp.concatenate([prev.reshape(B, nb, WINDOW, SWA_KV_HEADS, HEAD_DIM),
                                t.reshape(B, nb, WINDOW, SWA_KV_HEADS, HEAD_DIM)], axis=2)

    kb, vb = band(k), band(v)
    s = jnp.einsum('bnqhgd,bnkhd->bnhgqk', qb, kb) * (HEAD_DIM ** -0.5)
    i = jnp.arange(WINDOW)[:, None]
    j = jnp.arange(2 * WINDOW)[None, :]
    blk = jnp.arange(nb)[:, None, None]
    mask = (j > i) & (j <= i + WINDOW) & (blk * WINDOW - WINDOW + j >= 0)
    s = jnp.where(mask[None, :, None, None], s, -jnp.inf)
    sink = sinks.astype(jnp.float32).reshape(SWA_KV_HEADS, SWA_GROUP)[None, None, :, :, None, None]
    m = jnp.maximum(jnp.max(s, axis=-1, keepdims=True), sink)
    p = jnp.exp(s - m)
    p = p / (jnp.sum(p, axis=-1, keepdims=True) + jnp.exp(sink - m))
    o = jnp.einsum('bnhgqk,bnkhd->bnqhgd', p, vb)
    return o.reshape(B, S, SWA_Q_W)

def stick_breaking_attention(q, k, v):
    B, S = q.shape[:2]
    outs = []
    for n in range(S // SB_BLOCK):
        t0, t1 = n * SB_BLOCK, (n + 1) * SB_BLOCK
        z = jnp.einsum('bqhd,bkhd->bhqk', q[:, t0:t1], k[:, :t1]) * (HEAD_DIM ** -0.5)
        causal = jnp.arange(t1)[None, :] < (t0 + jnp.arange(SB_BLOCK))[:, None]
        log_fail = jnp.where(causal, -jax.nn.softplus(z), 0.0)
        log_after = lax.cumsum(log_fail, axis=3, reverse=True) - log_fail
        a = jnp.where(causal, jnp.exp(jax.nn.log_sigmoid(z) + log_after), 0.0)
        outs.append(jnp.einsum('bhqk,bkhd->bqhd', a, v[:, :t1]))
    return jnp.concatenate(outs, axis=1).reshape(B, S, SB_W)

def hgrn2_chunkwise(q, k, v, log_f):
    B, S, H, dk = q.shape
    dv = v.shape[-1]
    nc = S // HGRN_CHUNK

    def chunks(t):
        return t.reshape(B, nc, HGRN_CHUNK, H, t.shape[-1]).transpose(1, 0, 3, 2, 4)

    qc, kc, vc = chunks(q), chunks(k), chunks(v)
    bc = jnp.cumsum(chunks(log_f), axis=3)
    tril = jnp.tril(jnp.ones((HGRN_CHUNK, HGRN_CHUNK), dtype=bool))

    def step(state, inp):
        qi, ki, vi, bi = inp
        b_last = bi[:, :, -1:, :]
        rel = jnp.where(tril[None, None, :, :, None],
                        bi[:, :, :, None, :] - bi[:, :, None, :, :], -jnp.inf)
        scores = jnp.einsum('bhtd,bhsd,bhtsd->bhts', qi, ki, jnp.exp(rel))
        o = (jnp.einsum('bhts,bhse->bhte', scores, vi)
             + jnp.einsum('bhtd,bhde->bhte', qi * jnp.exp(bi), state))
        state = (jnp.exp(b_last)[:, :, 0, :, None] * state
                 + jnp.einsum('bhsd,bhse->bhde', ki * jnp.exp(b_last - bi), vi))
        return state, o

    s0 = jnp.zeros((B, H, dk, dv), jnp.float32)
    _, o = lax.scan(step, s0, (qc, kc, vc, bc))
    return o.transpose(1, 0, 3, 2, 4).reshape(B, S, H, dv)

def swa_sb_mixer(h, positions, w_in, w_out, q_norm, k_norm, sinks):
    B, S, _ = h.shape
    f32 = jnp.float32
    cuts = (SWA_Q_W, SWA_Q_W + SWA_KV_W, SWA_Q_W + 2 * SWA_KV_W,
            SWA_Q_W + 2 * SWA_KV_W + SB_W, SWA_Q_W + 2 * SWA_KV_W + 2 * SB_W)
    qa, ka, va, qb, kb, vb = jnp.split((h @ w_in).astype(f32), cuts, axis=-1)
    qa = rope(rms_norm(qa.reshape(B, S, SWA_HEADS, HEAD_DIM), q_norm), positions)
    ka = rope(rms_norm(ka.reshape(B, S, SWA_KV_HEADS, HEAD_DIM), k_norm), positions)
    va = va.reshape(B, S, SWA_KV_HEADS, HEAD_DIM)
    out_a = sliding_window_attention(qa, ka, va, sinks)
    heads_b = lambda t: t.reshape(B, S, SB_HEADS, HEAD_DIM)
    out_b = stick_breaking_attention(heads_b(qb), heads_b(kb), heads_b(vb))
    return jnp.concatenate([out_a, out_b], axis=-1).astype(h.dtype) @ w_out

def hgrn2_mixer(h, w_in, w_out, o_norm, lower_bound):
    B, S, _ = h.shape
    f32 = jnp.float32
    q, f_logit, i_in, g = jnp.split((h @ w_in).astype(f32), 4, axis=-1)
    lb = lower_bound.astype(f32)
    log_f = jnp.log(lb + (1.0 - lb) * jax.nn.sigmoid(f_logit))
    k = (1.0 - lb) * jax.nn.sigmoid(-f_logit)
    heads = lambda t: t.reshape(B, S, HGRN_HEADS, HGRN_HEAD_DIM)
    o = hgrn2_chunkwise(heads(q), heads(k), heads(i_in), heads(log_f))
    o = rms_norm(o, o_norm) * jax.nn.silu(heads(g))
    return o.reshape(B, S, HGRN_HEADS * HGRN_HEAD_DIM).astype(h.dtype) @ w_out

def memory_cross_attention(h, mem_n, w_q, w_kv, w_o, q_norm, k_norm):
    B, S, _ = h.shape
    M = mem_n.shape[1]
    f32 = jnp.float32
    q = rms_norm((h @ w_q).astype(f32).reshape(B, S, XA_HEADS, XA_HEAD_DIM), q_norm)
    kv = (mem_n @ w_kv).astype(f32).reshape(B, M, 2, XA_HEADS, XA_HEAD_DIM)
    k = rms_norm(kv[:, :, 0], k_norm)
    v = kv[:, :, 1]
    s = jnp.einsum('bshd,bmhd->bhsm', q, k) * (XA_HEAD_DIM ** -0.5)
    p = jax.nn.softmax(s, axis=-1)
    o = jnp.einsum('bhsm,bmhd->bshd', p, v).reshape(B, S, D_MODEL)
    return o.astype(h.dtype) @ w_o

def conv_ffn(h, w_up, conv_w, conv_b, w_down):
    S = h.shape[1]
    u = h @ w_up
    shift = lambda t, n: jnp.pad(t, ((0, 0), (n, 0), (0, 0)))[:, :S]
    u = sum(conv_w[CONV_WIDTH - 1 - n] * shift(u, n) for n in range(CONV_WIDTH)) + conv_b
    gate, up = jnp.split(u, 2, axis=-1)
    return (jax.nn.silu(gate) * up) @ w_down

def first_inputs(seed: int = 0) -> dict:
    key = jax.random.key(seed)
    ks = jax.random.split(key, 24)
    f32 = jnp.float32

    def dense(k, shape):
        return jax.random.normal(k, shape, f32) * (shape[-2] ** -0.5)

    def gain(k, shape):
        return 1.0 + 0.02 * jax.random.normal(k, shape, f32)

    x = jax.random.normal(ks[0], (BATCH, SEQ, D_MODEL), f32)
    mem = jax.random.normal(ks[1], (BATCH, N_MEM, D_MODEL), f32)
    positions = (jax.random.randint(ks[2], (BATCH, 1), 0, 1024, dtype=jnp.int32)
                 + jnp.arange(SEQ, dtype=jnp.int32)[None, :])
    return {
        "x": x,
        "mem": mem,
        "positions": positions,
        "norm_mix": gain(ks[3], (DEPTH, D_MODEL)),
        "norm_cross": gain(ks[4], (DEPTH, D_MODEL)),
        "norm_mem": gain(ks[5], (DEPTH, D_MODEL)),
        "norm_ffn": gain(ks[6], (DEPTH, D_MODEL)),
        "ab_w_in": dense(ks[7], (N_EVEN, D_MODEL, AB_IN)),
        "ab_w_out": dense(ks[8], (N_EVEN, AB_OUT, D_MODEL)),
        "swa_q_norm": gain(ks[9], (N_EVEN, HEAD_DIM)),
        "swa_k_norm": gain(ks[10], (N_EVEN, HEAD_DIM)),
        "swa_sinks": 0.5 * jax.random.normal(ks[11], (N_EVEN, SWA_HEADS), f32),
        "hgrn_w_in": dense(ks[12], (N_ODD, D_MODEL, 4 * HGRN_HEADS * HGRN_HEAD_DIM)),
        "hgrn_w_out": dense(ks[13], (N_ODD, HGRN_HEADS * HGRN_HEAD_DIM, D_MODEL)),
        "hgrn_o_norm": gain(ks[14], (N_ODD, HGRN_HEAD_DIM)),
        "hgrn_lb": jax.random.normal(ks[15], (DEPTH, HGRN_HEADS * HGRN_HEAD_DIM), f32),
        "xa_w_q": dense(ks[16], (DEPTH, D_MODEL, D_MODEL)),
        "xa_w_kv": dense(ks[17], (DEPTH, D_MODEL, 2 * D_MODEL)),
        "xa_w_o": dense(ks[18], (DEPTH, D_MODEL, D_MODEL)),
        "xa_q_norm": gain(ks[19], (DEPTH, XA_HEAD_DIM)),
        "xa_k_norm": gain(ks[20], (DEPTH, XA_HEAD_DIM)),
        "ffn_w_up": dense(ks[21], (DEPTH, D_MODEL, 2 * D_FF)),
        "ffn_conv_w": jax.random.normal(ks[22], (DEPTH, CONV_WIDTH, 2 * D_FF), f32) * (CONV_WIDTH ** -0.5),
        "ffn_conv_b": 0.02 * jax.random.normal(jax.random.fold_in(ks[22], 1), (DEPTH, 2 * D_FF), f32),
        "ffn_w_down": dense(ks[23], (DEPTH, D_FF, D_MODEL)),
    }

def first_block(x, mem, positions, norm_mix, norm_cross, norm_mem, norm_ffn,
              ab_w_in, ab_w_out, swa_q_norm, swa_k_norm, swa_sinks,
              hgrn_w_in, hgrn_w_out, hgrn_o_norm, hgrn_lb,
              xa_w_q, xa_w_kv, xa_w_o, xa_q_norm, xa_k_norm,
              ffn_w_up, ffn_conv_w, ffn_conv_b, ffn_w_down):
    p_lb = jax.nn.softmax(hgrn_lb.astype(jnp.float32), axis=0)
    lower_bounds = jnp.cumsum(p_lb, axis=0) - p_lb[0]
    for l in range(DEPTH):
        h = rms_norm(x, norm_mix[l])
        if l % 2 == 0:
            e = l // 2
            x = x + swa_sb_mixer(h, positions, ab_w_in[e], ab_w_out[e],
                                 swa_q_norm[e], swa_k_norm[e], swa_sinks[e])
        else:
            o = l // 2
            x = x + hgrn2_mixer(h, hgrn_w_in[o], hgrn_w_out[o], hgrn_o_norm[o], lower_bounds[l])
        mem_n = rms_norm(mem, norm_mem[l])
        x = x + memory_cross_attention(rms_norm(x, norm_cross[l]), mem_n, xa_w_q[l], xa_w_kv[l],
                                       xa_w_o[l], xa_q_norm[l], xa_k_norm[l])
        x = x + conv_ffn(rms_norm(x, norm_ffn[l]), ffn_w_up[l], ffn_conv_w[l], ffn_conv_b[l], ffn_w_down[l])
    return x


N_MIXERS = 2
POOL_WINDOWS = (2, 4, 8, 16)
POOL_GROUPS = len(POOL_WINDOWS)
POOL_GROUP_DIM = D_MODEL // POOL_GROUPS
N_HEADS = 16
N_KV_GROUPS = 4
HEADS_PER_GROUP = N_HEADS // N_KV_GROUPS
HEAD_DIM_2 = D_MODEL // N_HEADS
Q_DIM = N_HEADS * HEAD_DIM_2
KV_DIM = N_KV_GROUPS * HEAD_DIM_2
N_BRANCHES = 3
IN_PROJ_DIM = Q_DIM + 2 * N_BRANCHES * KV_DIM + N_BRANCHES * N_HEADS
CMP_STRIDE = 16
CMP_BLOCK = 2 * CMP_STRIDE
CMP_HIDDEN = 2 * HEAD_DIM_2
SEL_BLOCK = 64
SEL_TOP_N = 16
WINDOW_2 = 512
Q_BLOCK = 64
FORCE_BONUS = 1.0e3
NEG_INF = -1.0e30
ATTN_SCALE = HEAD_DIM_2 ** -0.5
D_FF_2 = 2816
N_EXPERTS = 8
TOP_K = 2
D_FF_EXPERT = 3584
LN_EPS = 1e-5
ALPHA = (2 * DEPTH) ** 0.25
BETA = (8 * DEPTH) ** -0.25


def layer_norm(x, g, b):
    xf = x.astype(jnp.float32)
    mu = jnp.mean(xf, axis=-1, keepdims=True)
    var = jnp.mean(jnp.square(xf - mu), axis=-1, keepdims=True)
    return ((xf - mu) * lax.rsqrt(var + LN_EPS) * g.astype(jnp.float32) + b.astype(jnp.float32)).astype(x.dtype)

def rope_2(x, pos):
    half = x.shape[-1] // 2
    freqs = jnp.power(ROPE_THETA, -jnp.arange(half, dtype=jnp.float32) / half)
    ang = pos.astype(jnp.float32)[:, None] * freqs[None, :]
    cos = jnp.cos(ang)[None, :, None, :]
    sin = jnp.sin(ang)[None, :, None, :]
    xf = x.astype(jnp.float32)
    x1, x2 = xf[..., :half], xf[..., half:]
    return jnp.concatenate([x1 * cos - x2 * sin, x1 * sin + x2 * cos], axis=-1).astype(x.dtype)

def pool_mixer(x, w_grp, scale):
    B, S, _ = x.shape
    xg = x.reshape(B, S, POOL_GROUPS, POOL_GROUP_DIM)
    c = jnp.concatenate([jnp.zeros((B, 1, POOL_GROUPS, POOL_GROUP_DIM), jnp.float32),
                         jnp.cumsum(xg.astype(jnp.float32), axis=1)], axis=1)
    t1 = jnp.arange(1, S + 1)
    pooled = []
    for gi, w in enumerate(POOL_WINDOWS):
        cg = c[:, :, gi]
        lo = cg[:, jnp.maximum(t1 - w, 0)]
        cnt = jnp.minimum(t1, w).astype(jnp.float32)
        pooled.append((cg[:, 1:] - lo) / cnt[None, :, None])
    pooled = jnp.stack(pooled, axis=2).astype(x.dtype)
    y = jnp.einsum('bsgc,gcd->bsgd', pooled - xg, w_grp).reshape(B, S, D_MODEL)
    return y * scale

def compress(k, pe, w1, w2):
    B, S, G, D = k.shape
    ch = k.reshape(B, S // CMP_STRIDE, CMP_STRIDE, G, D)
    blk = jnp.concatenate([ch[:, :-1], ch[:, 1:]], axis=2)
    blk = blk + pe[None, None, :, None, :]
    nc = blk.shape[1]
    blk = blk.transpose(0, 1, 3, 2, 4).reshape(B, nc, G, CMP_BLOCK * D)
    return jax.nn.silu(blk @ w1) @ w2

def nsa_mixer(x, w_in, pe_k, w1_k, w2_k, pe_v, w1_v, w2_v, w_out):
    B, S, _ = x.shape
    G, HG, D = N_KV_GROUPS, HEADS_PER_GROUP, HEAD_DIM_2
    proj = x @ w_in
    splits = [Q_DIM + i * KV_DIM for i in range(2 * N_BRANCHES + 1)]
    q, kc_raw, vc_raw, ks, vs, kw, vw, g_logits = jnp.split(proj, splits, axis=-1)
    pos = jnp.arange(S)
    q = rope_2(q.reshape(B, S, N_HEADS, D), pos)
    q = q.reshape(B, S, G, HG, D).transpose(0, 2, 3, 1, 4)
    kv = lambda a: a.reshape(B, S, G, D)
    ks = rope_2(kv(ks), pos)
    kw = rope_2(kv(kw), pos)
    vs, vw = kv(vs), kv(vw)
    kc = compress(kv(kc_raw), pe_k, w1_k, w2_k)
    vc = compress(kv(vc_raw), pe_v, w1_v, w2_v)
    nc = kc.shape[1]
    cend = CMP_STRIDE * jnp.arange(nc) + CMP_BLOCK - 1
    kc = rope_2(kc, cend)
    gates = jax.nn.sigmoid(g_logits.astype(jnp.float32)).astype(x.dtype).reshape(B, S, N_HEADS, N_BRANCHES)

    nsel = S // SEL_BLOCK
    n_top = min(SEL_TOP_N, nsel)
    ks_blk = ks.reshape(B, nsel, SEL_BLOCK, G, D).transpose(0, 3, 1, 2, 4)
    vs_blk = vs.reshape(B, nsel, SEL_BLOCK, G, D).transpose(0, 3, 1, 2, 4)
    kw_pad = jnp.pad(kw, ((0, 0), (WINDOW_2, 0), (0, 0), (0, 0)))
    vw_pad = jnp.pad(vw, ((0, 0), (WINDOW_2, 0), (0, 0), (0, 0)))
    cstart = CMP_STRIDE * jnp.arange(nc)
    sstart = SEL_BLOCK * jnp.arange(nsel)
    overlap = ((cstart[:, None] <= sstart[None, :] + SEL_BLOCK - 1) &
               (cstart[:, None] + CMP_BLOCK - 1 >= sstart[None, :])).astype(jnp.float32)
    bi = jnp.arange(B)[:, None, None, None]
    gi = jnp.arange(G)[None, :, None, None]
    jsel = jnp.arange(nsel)

    def query_block(i):
        t0 = i * Q_BLOCK
        t = t0 + jnp.arange(Q_BLOCK)
        qb = lax.dynamic_slice_in_dim(q, t0, Q_BLOCK, axis=3)
        sc = jnp.einsum('bghtd,bngd->bghtn', qb, kc).astype(jnp.float32) * ATTN_SCALE
        cvalid = cend[None, :] <= t[:, None]
        pc = jax.nn.softmax(jnp.where(cvalid, sc, NEG_INF), axis=-1)
        pc = pc * jnp.any(cvalid, axis=-1).astype(jnp.float32)[:, None]
        o_c = jnp.einsum('bghtn,bngd->btghd', pc.astype(vc.dtype), vc)
        imp = jnp.einsum('bghtn,nj->bgtj', pc, overlap)
        blk_t = t // SEL_BLOCK
        bvalid = jsel[None, :] <= blk_t[:, None]
        forced = (jsel[None, :] == 0) | (jsel[None, :] == blk_t[:, None]) | (jsel[None, :] == blk_t[:, None] - 1)
        score = jnp.where(bvalid, imp + FORCE_BONUS * forced.astype(jnp.float32), -1.0)
        _, idx = lax.top_k(score, n_top)
        sel_valid = idx <= blk_t[None, None, :, None]
        kg = ks_blk[bi, gi, idx]
        vg = vs_blk[bi, gi, idx]
        ss = jnp.einsum('bghtd,bgtnld->bghtnl', qb, kg).astype(jnp.float32) * ATTN_SCALE
        kpos = idx[..., None] * SEL_BLOCK + jnp.arange(SEL_BLOCK)
        ms = (kpos <= t[None, None, :, None, None]) & sel_valid[..., None]
        ss = jnp.where(ms[:, :, None], ss, NEG_INF)
        ps = jax.nn.softmax(ss.reshape(ss.shape[:4] + (n_top * SEL_BLOCK,)), axis=-1).reshape(ss.shape)
        o_s = jnp.einsum('bghtnl,bgtnld->btghd', ps.astype(vg.dtype), vg)
        kwb = lax.dynamic_slice_in_dim(kw_pad, t0, Q_BLOCK + WINDOW_2, axis=1)
        vwb = lax.dynamic_slice_in_dim(vw_pad, t0, Q_BLOCK + WINDOW_2, axis=1)
        kpos_w = t0 - WINDOW_2 + jnp.arange(Q_BLOCK + WINDOW_2)
        mw = (kpos_w[None, :] <= t[:, None]) & (kpos_w[None, :] > t[:, None] - WINDOW_2) & (kpos_w[None, :] >= 0)
        sw = jnp.einsum('bghtd,bkgd->bghtk', qb, kwb).astype(jnp.float32) * ATTN_SCALE
        pw = jax.nn.softmax(jnp.where(mw, sw, NEG_INF), axis=-1)
        o_w = jnp.einsum('bghtk,bkgd->btghd', pw.astype(vwb.dtype), vwb)
        gb = lax.dynamic_slice_in_dim(gates, t0, Q_BLOCK, axis=1).reshape(B, Q_BLOCK, G, HG, N_BRANCHES)
        return gb[..., 0:1] * o_c + gb[..., 1:2] * o_s + gb[..., 2:3] * o_w

    out = lax.map(query_block, jnp.arange(S // Q_BLOCK))
    out = out.transpose(1, 0, 2, 3, 4, 5).reshape(B, S, Q_DIM)
    return out @ w_out

def swiglu(x, w_gu, w_down):
    g, u = jnp.split(x @ w_gu, 2, axis=-1)
    return (jax.nn.silu(g) * u) @ w_down

def moe_ffn(x, router, w_gu, w_down):
    B, S, D = x.shape
    xt = x.reshape(B * S, D)
    logits = (xt @ router).astype(jnp.float32)
    top_v, top_i = lax.top_k(logits, TOP_K)
    w = jax.nn.softmax(top_v, axis=-1)
    combine = jnp.einsum('tk,tke->te', w, jax.nn.one_hot(top_i, N_EXPERTS, dtype=jnp.float32)).astype(x.dtype)
    y = jnp.zeros_like(xt)
    for e in range(N_EXPERTS):
        y = y + combine[:, e:e + 1] * swiglu(xt, w_gu[e], w_down[e])
    return y.reshape(B, S, D)

def second_inputs(seed: int = 0) -> dict:
    key = jax.random.key(seed)
    keys = iter(jax.random.split(key, 32))
    nrm = lambda shape, s: jax.random.normal(next(keys), shape, jnp.float32) * s
    na = (DEPTH + 1) // 2
    nb = DEPTH // 2
    return {
        "x": nrm((BATCH, SEQ, D_MODEL), 1.0),
        "ln_g": 1.0 + nrm((DEPTH, 2, D_MODEL), 0.05),
        "ln_b": nrm((DEPTH, 2, D_MODEL), 0.02),
        "pool_w": nrm((na, POOL_GROUPS, POOL_GROUP_DIM, POOL_GROUP_DIM), BETA * POOL_GROUP_DIM ** -0.5),
        "pool_scale": 1.0 + nrm((na, D_MODEL), 0.1),
        "nsa_w_in": nrm((nb, D_MODEL, IN_PROJ_DIM), D_MODEL ** -0.5),
        "nsa_pe_k": nrm((nb, CMP_BLOCK, HEAD_DIM_2), 0.1),
        "nsa_w1_k": nrm((nb, CMP_BLOCK * HEAD_DIM_2, CMP_HIDDEN), (CMP_BLOCK * HEAD_DIM_2) ** -0.5),
        "nsa_w2_k": nrm((nb, CMP_HIDDEN, HEAD_DIM_2), CMP_HIDDEN ** -0.5),
        "nsa_pe_v": nrm((nb, CMP_BLOCK, HEAD_DIM_2), 0.1),
        "nsa_w1_v": nrm((nb, CMP_BLOCK * HEAD_DIM_2, CMP_HIDDEN), (CMP_BLOCK * HEAD_DIM_2) ** -0.5),
        "nsa_w2_v": nrm((nb, CMP_HIDDEN, HEAD_DIM_2), CMP_HIDDEN ** -0.5),
        "nsa_w_out": nrm((nb, Q_DIM, D_MODEL), BETA * Q_DIM ** -0.5),
        "ffn_w_gu": nrm((na, D_MODEL, 2 * D_FF_2), D_MODEL ** -0.5),
        "ffn_w_down": nrm((na, D_FF_2, D_MODEL), BETA * D_FF_2 ** -0.5),
        "moe_router": nrm((nb, D_MODEL, N_EXPERTS), D_MODEL ** -0.5),
        "moe_w_gu": nrm((nb, N_EXPERTS, D_MODEL, 2 * D_FF_EXPERT), D_MODEL ** -0.5),
        "moe_w_down": nrm((nb, N_EXPERTS, D_FF_EXPERT, D_MODEL), BETA * D_FF_EXPERT ** -0.5),
    }

def second_block(x, ln_g, ln_b, pool_w, pool_scale, nsa_w_in, nsa_pe_k, nsa_w1_k, nsa_w2_k,
              nsa_pe_v, nsa_w1_v, nsa_w2_v, nsa_w_out, ffn_w_gu, ffn_w_down,
              moe_router, moe_w_gu, moe_w_down):
    for i in range(DEPTH):
        j = i // N_MIXERS
        if i % N_MIXERS == 0:
            h = pool_mixer(x, pool_w[j], pool_scale[j])
        else:
            h = nsa_mixer(x, nsa_w_in[j], nsa_pe_k[j], nsa_w1_k[j], nsa_w2_k[j],
                          nsa_pe_v[j], nsa_w1_v[j], nsa_w2_v[j], nsa_w_out[j])
        x = layer_norm(ALPHA * x + h, ln_g[i, 0], ln_b[i, 0])
        if i % 2 == 0:
            f = swiglu(x, ffn_w_gu[j], ffn_w_down[j])
        else:
            f = moe_ffn(x, moe_router[j], moe_w_gu[j], moe_w_down[j])
        x = layer_norm(ALPHA * x + f, ln_g[i, 1], ln_b[i, 1])
    return x


def setup_inputs(seed=0):
    out = dict(first_inputs(seed))
    for name, value in second_inputs(seed + 1).items():
        if name != "x":
            out[name + "_2"] = value
    return out


def reference(
    x, mem, positions, norm_mix, norm_cross, norm_mem, norm_ffn, ab_w_in, ab_w_out, swa_q_norm,
    swa_k_norm, swa_sinks, hgrn_w_in, hgrn_w_out, hgrn_o_norm, hgrn_lb, xa_w_q, xa_w_kv, xa_w_o,
    xa_q_norm, xa_k_norm, ffn_w_up, ffn_conv_w, ffn_conv_b, ffn_w_down, ln_g_2, ln_b_2,
    pool_w_2, pool_scale_2, nsa_w_in_2, nsa_pe_k_2, nsa_w1_k_2, nsa_w2_k_2, nsa_pe_v_2,
    nsa_w1_v_2, nsa_w2_v_2, nsa_w_out_2, ffn_w_gu_2, ffn_w_down_2, moe_router_2, moe_w_gu_2,
    moe_w_down_2,
):
    x = first_block(
        x, mem, positions, norm_mix, norm_cross, norm_mem, norm_ffn, ab_w_in, ab_w_out,
        swa_q_norm, swa_k_norm, swa_sinks, hgrn_w_in, hgrn_w_out, hgrn_o_norm, hgrn_lb, xa_w_q,
        xa_w_kv, xa_w_o, xa_q_norm, xa_k_norm, ffn_w_up, ffn_conv_w, ffn_conv_b, ffn_w_down,
    )
    return second_block(
        x, ln_g_2, ln_b_2, pool_w_2, pool_scale_2, nsa_w_in_2, nsa_pe_k_2, nsa_w1_k_2,
        nsa_w2_k_2, nsa_pe_v_2, nsa_w1_v_2, nsa_w2_v_2, nsa_w_out_2, ffn_w_gu_2, ffn_w_down_2,
        moe_router_2, moe_w_gu_2, moe_w_down_2,
    )


_drawn_inputs = setup_inputs


def setup_inputs(seed=0):
    import zlib

    import numpy as np

    out = dict(_drawn_inputs(seed))
    spreads = {}
    factors = {'norm_cross': 8.0,
     'norm_mem': 5.31,
     'swa_q_norm': 5.954,
     'swa_k_norm': 7.579,
     'hgrn_o_norm': 3.441,
     'xa_q_norm': 8.0,
     'xa_k_norm': 7.681,
     'nsa_pe_k_2': 23.017,
     'nsa_pe_v_2': 3.737,
     'swa_sinks': 8.0}
    for name, (base, spread) in spreads.items():
        noise = np.random.default_rng([zlib.crc32(name.encode()), seed]).standard_normal(out[name].shape)
        drawn = base * np.exp(spread * noise) if base else spread * noise
        out[name] = __import__('jax').numpy.asarray(drawn.astype(out[name].dtype))
    for name, factor in factors.items():
        out[name] = (out[name] * factor).astype(out[name].dtype)
    return out
```

```python
from contextlib import ExitStack

import concourse.bass as bass
import numpy as np
from concourse import mybir

F32 = mybir.dt.float32
F32R = mybir.dt.float32r
I32 = mybir.dt.int32
U32 = mybir.dt.uint32
ALU = mybir.AluOpType
ACT = mybir.ActivationFunctionType
AX = mybir.AxisListType.X

P = 128
T = 256
D = 1024
NB = D // P
BLK = T
SLOT = 16 * P
DEPTH = 3
FF = 22
MOE_FF = 28
EXPERTS = 8
HALF = MOE_FF // 2
ALPHA = 4.0 ** 0.25
NCMP = 15
MASKED = -1.0e30
HG_LEVELS = 7
ROUND = 1.5 * 2.0 ** 23
_C1 = 6.28125
_C2 = round((2.0 * np.pi - _C1) * 2.0 ** 20) / 2.0 ** 20
TWO_PI = (_C1, _C2, 2.0 * np.pi - _C1 - _C2)
PI = 3.1415925


class Phase:

    def __init__(self, name, kind, n, g, e, a):
        self.name, self.kind, self.n, self.g, self.e, self.a = name, kind, n, g, e, a


def plan():
    phases, g, e, a = {}, 0, 0, 0
    ffn = [("gu", HALF), ("down", HALF // 2), ("gu", FF - HALF), ("down", (FF - HALF) // 2)]
    order = [("ab_in", "proj", 9), ("ab_out", "proj", 4)]
    for layer in range(2):
        if layer == 1:
            order += [("hg_in", "proj", 16), ("hg_out", "proj", 4)]
        order += [(f"kv{layer}", "proj", 8), (f"q{layer}", "proj", 4), (f"o{layer}", "proj", 4)]
        order += [(f"ffn{layer}_{i}", k, n) for i, (k, n) in enumerate(ffn)]
    order += [("pool", "pool", 1)]
    order += [(f"ffn2_{i}", k, n) for i, (k, n) in enumerate(ffn)]
    order += [("nsa_in", "proj", 10), ("nsa_out", "proj", 4)]
    order += [("moe_gu", "gu", HALF), ("moe_down", "down", HALF // 2)]
    for name, kind, n in order:
        phases[name] = Phase(name, kind, n, g, e, a)
        g += n
        if kind != "down":
            e += n
        if kind == "gu":
            a += n
    per_half = HALF + HALF // 2
    total = phases["moe_gu"].g + 2 * EXPERTS * per_half
    return phases, per_half, total


PHASES, PER_HALF, SLOTS = plan()
STREAM = SLOTS + DEPTH

CONST = {}
_at = 0
for _name, _n in [("ident", 128), ("ones", 128), ("ones64", 128), ("rot", 128), ("dup0", 128), ("dup1", 128),
                  ("ge", 128), ("invf", 1), ("eps6", 1), ("eps5", 1), ("cend_cos", 15), ("cend_sin", 15), ("cmp_mask", 30),
                  ("cmp_any", 2), ("iota8", 8)]:
    CONST[_name] = (_at, _n)
    _at += _n
N_CONST = _at
STAGE = {"attn": 0, "hgrn": 1, "pool": 2, "nsa": 3}
PARAM = {}
_at = 0
for _name, _n in [("norm_mix", 16), ("norm_cross", 16), ("norm_mem", 16), ("norm_ffn", 16), ("swa_q", 1),
                  ("swa_k", 1), ("sinks", 8), ("o_norm", 1), ("lb", 16), ("xa_q", 4), ("xa_k", 4),
                  ("conv_w", 264), ("conv_b", 88), ("ln_g", 32), ("ln_b", 32), ("pool_scale", 8),
                  ("router", 64), ("pe_k", 16), ("pe_v", 16), ("w2_k", 128), ("w2_v", 64)]:
    PARAM[_name] = (_at, _n)
    _at += _n
N_PARAM = _at


def build(nc, stream, x_in, mem_in, pos_in, params, consts, stage_consts, w1_in, out):
    ctx = ExitStack()
    with ctx:
        def sb(name, cols, dt=F32):
            return ctx.enter_context(nc.sbuf_tensor(name, [P, cols], dt))

        def sem(name):
            return ctx.enter_context(nc.semaphore(name))

        raw = [sb(f"raw{i}", SLOT) for i in range(DEPTH)]
        whi = [sb(f"whi{i}", SLOT, F32R) for i in range(DEPTH)]
        wlo = [sb(f"wlo{i}", SLOT, F32R) for i in range(DEPTH)]
        x = sb("x", NB * BLK)
        hh = sb("hh", NB * BLK, F32R)
        hl = sb("hl", NB * BLK, F32R)
        ahi = sb("ahi", HALF * BLK, F32R)
        alo = sb("alo", HALF * BLK, F32R)
        hf = sb("hf", NB * BLK)
        rstd = sb("rstd", BLK)
        const = sb("const", N_CONST)
        par = sb("par", N_PARAM)
        stage = sb("stage", 1024)
        zero = sb("zero", P, F32R)
        small = sb("small", 640)
        idx = sb("idx", 16, U32)
        work = sb("work", 60 * BLK)
        ps = ctx.enter_context(nc.psum_tensor("ps", [P, 8, 512], F32))

        def C(name, a=0, n=None):
            at, size = CONST[name]
            return const[:, at + a:at + (size if n is None else a + n)]

        def R(name, a=0, n=1):
            return par[:, PARAM[name][0] + a:PARAM[name][0] + a + n]

        def W(block, n=1):
            return work[:, block * BLK:(block + n) * BLK]

        def Wc(col, n):
            return work[:, col:col + n]

        def xb(b, n=1):
            return x[:, b * BLK:(b + n) * BLK]

        def banks(b, n=2):
            return ps[:, b:b + n, :].rearrange("p b c -> p (b c)")

        def r3(ap, b):
            return ap.rearrange("p (b c) -> p b c", b=b)

        raw_loaded = [sem(f"raw_loaded{i}") for i in range(DEPTH)]
        hi_ready = sem("hi_ready")
        lo_ready = sem("lo_ready")
        slot_used = sem("slot_used")
        banks_drained = sem("banks_drained")
        gate_act = sem("gate_act")
        act_ready = sem("act_ready")
        acc_ready = sem("acc_ready")
        acc_drained = sem("acc_drained")
        dve_step = sem("dve_step")
        act_step = sem("act_step")
        params_loaded = sem("params_loaded")
        x_loaded = sem("x_loaded")
        positions_loaded = sem("positions_loaded")
        stage_loaded = sem("stage_loaded")
        mem_loaded = sem("mem_loaded")
        w1_loaded = sem("w1_loaded")
        angles_ready = sem("angles_ready")
        sines_ready = sem("sines_ready")
        zero_ready = sem("zero_ready")
        out_stored = sem("out_stored")
        squares_ready = sem("squares_ready")
        sums_ready = sem("sums_ready")
        rstd_ready = sem("rstd_ready")
        mean_ready = sem("mean_ready")
        x_ready = sem("x_ready")
        h_ready = sem("h_ready")
        head_sq = sem("head_sq")
        head_sums = sem("head_sums")
        head_rstd = sem("head_rstd")
        rope_in = sem("rope_in")
        rope_rot = sem("rope_rot")
        heads_ready = sem("heads_ready")
        dup_ready = sem("dup_ready")
        dup_copied = sem("dup_copied")
        v_turned = sem("v_turned")
        v_copied = sem("v_copied")
        scores_ready = sem("scores_ready")
        scores_masked = sem("scores_masked")
        negmax_ready = sem("negmax_ready")
        exp_done = sem("exp_done")
        probs_ready = sem("probs_ready")
        pt_ready = sem("pt_ready")
        pt_copied = sem("pt_copied")
        pv_done = sem("pv_done")
        o_drained = sem("o_drained")
        z_ready = sem("z_ready")
        z_masked = sem("z_masked")
        soft_ready = sem("soft_ready")
        sp_ready = sem("sp_ready")
        cs_ready = sem("cs_ready")
        d_ready = sem("d_ready")
        a_ready = sem("a_ready")
        sb_pv_done = sem("sb_pv_done")
        hg_lb = sem("hg_lb")
        hg_lb_exp = sem("hg_lb_exp")
        hg_sig = sem("hg_sig")
        hg_kf = sem("hg_kf")
        hg_log = sem("hg_log")
        hg_d = sem("hg_d")
        hg_e = sem("hg_e")
        hg_x = sem("hg_x")
        hg_s = sem("hg_s")
        hg_a = sem("hg_a")
        hg_o = sem("hg_o")
        hg_osq = sem("hg_osq")
        hg_osum = sem("hg_osum")
        hg_orstd = sem("hg_orstd")
        gates_ps = sem("gates_ps")
        gates_ready = sem("gates_ready")
        cmp_dup = sem("cmp_dup")
        cmp_cols = sem("cmp_cols")
        cmp_hidden = sem("cmp_hidden")
        cmp_bias = sem("cmp_bias")
        cmp_silu = sem("cmp_silu")
        cmp_kv = sem("cmp_kv")
        cmp_kv_copied = sem("cmp_kv_copied")
        cmp_rot = sem("cmp_rot")
        cmp_roped = sem("cmp_roped")
        cmp_scores = sem("cmp_scores")
        cmp_shifted = sem("cmp_shifted")
        cmp_exp = sem("cmp_exp")
        cmp_probs = sem("cmp_probs")
        cmp_turned = sem("cmp_turned")
        cmp_ready = sem("cmp_ready")
        logits_ps = sem("logits_ps")
        top2_diff = sem("top2_diff")
        top2_exp = sem("top2_exp")
        cw_diag = sem("cw_diag")
        cw_ps = sem("cw_ps")
        cw_ready = sem("cw_ready")

        block = ctx.enter_context(nc.Block())

        SWA_U, XA_U, NSA_U = 0, (4, 6), 8
        SWA_O, SB_O, XA_O, NSA_O = 0, 4, (8, 10), 12
        PROBS = [Wc(10752 + 1024 * i, 1024) for i in range(2)]
        PT = [Wc(12800 + 1024 * i, 1024) for i in range(2)]
        ROPED = (0, 2, 4, 6, 12, 16)
        PCT = (2048, 8192)
        SB_T = [Wc(4608 + 1024 * i, 1024) for i in range(2)]

        def place(kind, h):
            return h if kind == "xa" else (h % 2) * 2 + h // 2

        def units(kind):
            if kind == "swa":
                return [(g, qt, 0) for g in range(2) for qt in range(2)]
            if kind == "nsa":
                return [(g, qt, br) for g in range(4) for qt in range(2) for br in range(2)]
            return [(0, qt, 0) for qt in range(2)]

        def slot_loop(eng, ph, body, n=None, peel=0):
            n = ph.n if n is None else n
            rounds = n // DEPTH
            for i in range(min(peel, rounds)):
                for k in range(DEPTH):
                    body(i, k, DEPTH * i + k)
            if rounds - peel > 1:
                with eng.Fori(peel, rounds) as i:
                    for k in range(DEPTH):
                        body(i, k, i * DEPTH + k)
            elif rounds - peel == 1:
                for k in range(DEPTH):
                    body(peel, k, DEPTH * peel + k)
            for s in range(DEPTH * rounds, n):
                body(rounds, s - DEPTH * rounds, s)

        def at_least(eng, s, value):
            if not (isinstance(value, int) and value <= 0):
                eng.wait_ge(s, value)

        @block.sync
        def _(sp):
            sp.dma_start(x[:, :], x_in).then_inc(x_loaded, 16)
            sp.dma_start(const[:, :], consts).then_inc(params_loaded, 16)
            sp.dma_start(par[:, :], params).then_inc(params_loaded, 16)
            sp.dma_start(Wc(10752, 256).bitcast(I32), pos_in).then_inc(positions_loaded, 16)
            for k in range(DEPTH):
                sp.dma_start(raw[k][:, :], stream[k]).then_inc(raw_loaded[k], 16)

            def load(i, k, s):
                sp.wait_ge(lo_ready, s + 1)
                sp.dma_start(raw[k][:, :], stream[s + DEPTH]).then_inc(raw_loaded[k], 16)

            slot_loop(sp, None, load, n=STREAM - DEPTH)
            sp.wait_ge(x_ready, 4)
            sp.dma_start(out, x[:, :]).then_inc(out_stored, 16)
            sp.wait_ge(out_stored, 16)

        @block.gpsimd
        def _(pool):
            def split_lo(i, k, s):
                pool.wait_ge(hi_ready, s + 1)
                nc.gpsimd.tensor_tensor(wlo[k][:, :], raw[k][:, :], whi[k][:, :].bitcast(F32),
                                        ALU.subtract).then_inc(lo_ready, 1)

            slot_loop(pool, None, split_lo, n=STREAM)

        @block.scalar
        def _(act):
            chain = [0]

            def link(ins):
                chain[0] += 1
                ins.then_inc(act_step, 1)
                act.wait_ge(act_step, chain[0])

            def split_hi(ph, i, k, s, off=0):
                p = (ph.g + k) % DEPTH
                act.wait_ge(raw_loaded[p], i * 16 + (16 * ((ph.g + k) // DEPTH + 2) + off * 16))
                act.wait_ge(slot_used, s + (ph.g + 1) + off * DEPTH)
                nc.scalar.activation(whi[p][:, :], raw[p][:, :], ACT.Copy).then_inc(hi_ready, 1)

            def split_phase(name):
                ph = PHASES[name]
                slot_loop(act, ph, lambda i, k, s: split_hi(ph, i, k, s))

            def norm_act(n, count, eps):
                act.wait_ge(sums_ready, n + 1)
                link(nc.scalar.activation(rstd[:, :], ps[:, 7, 0:BLK], ACT.Ln, scale=1.0 / count, bias=eps_ap(eps)))
                nc.scalar.activation(rstd[:, :], rstd[:, :], ACT.Exp, scale=-0.5).then_inc(rstd_ready, 1)

            def eps_ap(eps):
                return C("eps6") if eps == 1e-6 else C("eps5")

            def softmax_act(kind, u0):
                us = units(kind)
                for step in range(len(us) + 1):
                    if step < len(us):
                        u = u0 + step
                        act.wait_ge(negmax_ready, u + 1)
                        probs, par2 = PROBS[u % 2], 32 * (u % 2)
                        if kind == "swa":
                            nc.scalar.activation(small[:, par2 + 12:par2 + 16], small[:, par2 + 8:par2 + 12], ACT.Exp)
                        for h in range(4):
                            ins = nc.scalar.activation(probs[:, h * 256:(h + 1) * 256], probs[:, h * 256:(h + 1) * 256],
                                                       ACT.Exp, bias=small[:, par2 + h:par2 + h + 1],
                                                       accum_out=small[:, par2 + 4 + h:par2 + 5 + h])
                        ins.then_inc(exp_done, 1)
                    if step >= 1:
                        u = u0 + step - 1
                        act.wait_ge(pt_ready, u + 1)
                        at_least(act, pv_done, u - 1)
                        nc.scalar.activation(PT[u % 2], banks(2), ACT.Copy).then_inc(pt_copied, 1)

            def ffn_act(layer, conv):
                for i in range(4):
                    ph = PHASES[f"ffn{layer}_{i}"]
                    if ph.kind == "down":
                        split_phase(ph.name)
                        continue

                    def body(i, k, s, ph=ph):
                        if conv:
                            gate = Wc(512 * ((ph.g + k) % DEPTH), BLK)
                            act.wait_ge(banks_drained, s + (ph.e + 1))
                            nc.scalar.activation(gate, gate, ACT.Silu).then_inc(gate_act, 1)
                        else:
                            silu_gate(ph, k, s)
                        split_hi(ph, i, k, s)

                    slot_loop(act, ph, body)

            def silu_gate(ph, k, s, off_g=0, off_a=0):
                bank = (ph.g + k) % DEPTH
                act.wait_ge(slot_used, s + (ph.g + 1) + off_g)
                act.wait_ge(act_ready, s + (ph.a - 2) + off_a)
                nc.scalar.activation(Wc(512 * bank, BLK), ps[:, bank, 0:BLK], ACT.Silu).then_inc(gate_act, 1)

            def xa_act(layer):
                act.wait_ge(h_ready, 2 + 6 * layer)
                act.dma_start(W(24, 8), mem_in).then_inc(mem_loaded, 16)
                norm_act(layer * 4 + 1, D, 1e-6)
                split_phase(f"kv{layer}")
                norm_act(layer * 4 + 2, D, 1e-6)
                split_phase(f"q{layer}")
                act.wait_ge(head_sums, 2 + layer)
                link(nc.scalar.activation(W(42, 8), banks(0, 4), ACT.Ln, scale=1.0 / 256, bias=C("eps6")))
                nc.scalar.activation(W(42, 8), W(42, 8), ACT.Exp, scale=-0.5).then_inc(head_rstd, 1)
                softmax_act("xa", XA_U[layer])
                split_phase(f"o{layer}")

            for k in range(DEPTH):
                act.wait_ge(raw_loaded[k], 16)
                nc.scalar.activation(whi[k][:, :], raw[k][:, :], ACT.Copy).then_inc(hi_ready, 1)
            act.dma_start(stage[:, :], stage_consts[STAGE["attn"]]).then_inc(stage_loaded, 16)
            act.wait_ge(angles_ready, 1)
            nc.scalar.activation(W(33, 2), W(33, 2), ACT.Sin).then_inc(sines_ready, 1)
            norm_act(0, D, 1e-6)
            split_phase("ab_in")
            act.wait_ge(head_sums, 1)
            link(nc.scalar.activation(W(23, 5), banks(0, 3)[:, 0:5 * BLK], ACT.Ln, scale=1.0 / 64, bias=C("eps6")))
            nc.scalar.activation(W(23, 5), W(23, 5), ACT.Exp, scale=-0.5).then_inc(head_rstd, 1)
            softmax_act("swa", SWA_U)
            for u in range(4):
                act.wait_ge(z_masked, u + 1)
                link(nc.scalar.activation(SB_T[u % 2], PROBS[u % 2], ACT.Abs))
                link(nc.scalar.activation(SB_T[u % 2], SB_T[u % 2], ACT.Exp, scale=-1.0))
                nc.scalar.activation(SB_T[u % 2], SB_T[u % 2], ACT.Ln, bias=1.0).then_inc(soft_ready, 1)
                act.wait_ge(d_ready, u + 1)
                at_least(act, sb_pv_done, u - 1)
                nc.scalar.activation(PT[u % 2], PROBS[u % 2], ACT.Exp).then_inc(a_ready, 1)
            split_phase("ab_out")
            xa_act(0)
            norm_act(3, D, 1e-6)
            ffn_act(0, True)
            act.dma_start(stage[:, :], stage_consts[STAGE["hgrn"]]).then_inc(stage_loaded, 16)
            norm_act(4, D, 1e-6)
            act.wait_ge(hg_lb, 1)
            nc.scalar.activation(small[:, 416:432], small[:, 400:416], ACT.Exp).then_inc(hg_lb_exp, 1)
            split_phase("hg_in")
            act.wait_ge(banks_drained, PHASES["hg_in"].e + PHASES["hg_in"].n)
            nc.scalar.activation(W(32, 8), W(8, 8), ACT.Sigmoid, scale=-1.0)
            nc.scalar.activation(W(8, 8), W(8, 8), ACT.Sigmoid).then_inc(hg_sig, 1)
            nc.scalar.activation(W(24, 8), W(24, 8), ACT.Silu)
            act.wait_ge(hg_kf, 1)
            nc.scalar.activation(W(8, 8), W(8, 8), ACT.Ln).then_inc(hg_log, 1)
            for lv in range(HG_LEVELS + 1):
                act.wait_ge(hg_d, lv + 1)
                if lv:
                    link(nc.scalar.activation(W(16, 8), W(16, 8), ACT.Abs))
                nc.scalar.activation(W(16, 8), W(16, 8), ACT.Exp, scale=-1.0 if lv else 1.0).then_inc(hg_e, 1)
            act.wait_ge(hg_osum, 1)
            link(nc.scalar.activation(W(8, 8), banks(4, 4), ACT.Ln, scale=1.0 / 128, bias=C("eps6")))
            nc.scalar.activation(W(8, 8), W(8, 8), ACT.Exp, scale=-0.5).then_inc(hg_orstd, 1)
            act.dma_start(stage[:, :], stage_consts[STAGE["pool"]]).then_inc(stage_loaded, 16)
            split_phase("hg_out")
            xa_act(1)
            norm_act(7, D, 1e-6)
            ffn_act(1, True)
            split_phase("pool")
            norm_act(8, D, 1e-5)
            act.dma_start(stage[:, :], stage_consts[STAGE["nsa"]]).then_inc(stage_loaded, 16)
            ffn_act(2, False)
            norm_act(9, D, 1e-5)
            act.dma_start(Wc(8192, 4480), w1_in).then_inc(w1_loaded, 16)
            split_phase("nsa_in")
            act.wait_ge(gates_ps, 1)
            nc.scalar.activation(small[:, 64:160], ps[:, 7, 0:96], ACT.Sigmoid).then_inc(gates_ready, 1)
            act.wait_ge(cmp_bias, 1)
            for br in range(2):
                ins = nc.scalar.activation(small[:, 160 + 60 * br:220 + 60 * br], ps[:, 6, 64 * br:64 * br + 60],
                                           ACT.Silu, bias=small[:, 280 + br:281 + br])
            ins.then_inc(cmp_silu, 1)
            act.wait_ge(cmp_shifted, 1)
            nc.scalar.activation(Wc(10240, 480), Wc(10240, 480), ACT.Exp).then_inc(cmp_exp, 1)
            softmax_act("nsa", NSA_U)
            split_phase("nsa_out")
            norm_act(10, D, 1e-5)
            act.wait_ge(top2_diff, 1)
            nc.scalar.activation(small[:, 504:506], small[:, 504:506], ACT.Exp).then_inc(top2_exp, 1)
            gu, down = PHASES["moe_gu"], PHASES["moe_down"]
            with act.Fori(0, EXPERTS) as e:
                with act.Fori(0, 2) as part:
                    half = e * 2 + part
                    rounds = half * (PER_HALF // DEPTH)

                    def body(i, k, s):
                        silu_gate(gu, k, s, half * PER_HALF, half * HALF)
                        split_hi(gu, i, k, s, rounds)

                    slot_loop(act, gu, body)
                    slot_loop(act, down, lambda i, k, s: split_hi(down, i, k, s, rounds))
            norm_act(11, D, 1e-5)

        @block.tensor
        def _(pe):
            mm = nc.tensor.matmul

            def split_mm(out_ap, hi_w, lo_w, hi_x, lo_x, start, stop, **kw):
                mm(out_ap, hi_w, hi_x, start=start, stop=False, **kw)
                mm(out_ap, hi_w, lo_x, start=False, stop=False, **kw)
                return mm(out_ap, lo_w, hi_x, start=False, stop=stop, **kw)

            def proj_slot(ph, k, s, off_g=0, off_e=0):
                p = (ph.g + k) % DEPTH
                pe.wait_ge(lo_ready, s + (ph.g + 1) + off_g)
                at_least(pe, banks_drained, s + (ph.e - 2) + off_e)
                for b in range(2):
                    for c in range(NB):
                        w = slice((b * NB + c) * P, (b * NB + c + 1) * P)
                        m = slice(c * BLK, (c + 1) * BLK)
                        last = split_mm(ps[:, p, b * BLK:(b + 1) * BLK], whi[p][:, w], wlo[p][:, w],
                                        hh[:, m], hl[:, m], c == 0, c == NB - 1)
                last.then_inc(slot_used, 1)

            def proj_pe(name, h):
                ph = PHASES[name]
                pe.wait_ge(h_ready, h)
                slot_loop(pe, ph, lambda i, k, s: proj_slot(ph, k, s), peel=1 if ph.g == 0 else 0)

            def down_slot(ph, k, s, act_at, off_g=0):
                p = (ph.g + k) % DEPTH
                pe.wait_ge(lo_ready, s + (ph.g + 1) + off_g)
                for c in range(2):
                    m = bass.ds(s * (2 * BLK) + c * BLK, BLK)
                    if isinstance(s, int):
                        m = slice((2 * s + c) * BLK, (2 * s + c + 1) * BLK)
                    pe.wait_ge(act_ready, act_at(s, c))
                    for b in range(NB):
                        w = slice((c * NB + b) * P, (c * NB + b + 1) * P)
                        last = split_mm(ps[:, 3 + b // 2, (b % 2) * BLK:(b % 2 + 1) * BLK], whi[p][:, w],
                                        wlo[p][:, w], ahi[:, m], alo[:, m], False, False, skip_group_check=True)
                last.then_inc(slot_used, 1)

            def acc_zero(start, stop):
                for b in range(4):
                    last = mm(ps[:, 3 + b, :], zero[:, :], zero[:, :].unsqueeze(1).to_broadcast([P, 4, P]), start=start, stop=stop,
                              skip_group_check=True)
                return last

            def sums_pe(src):
                for b in range(NB):
                    last = mm(ps[:, 7, 0:BLK], C("ones"), src[:, b * BLK:(b + 1) * BLK], start=(b == 0), stop=(b == NB - 1))
                return last

            def norm_pe(n):
                pe.wait_ge(squares_ready, n + 1)
                sums_pe(hf).then_inc(sums_ready, 1)

            def layer_norm_pe(i, drained, count):
                pe.wait_ge(drained, count)
                sums_pe(x).then_inc(mean_ready, 1)
                norm_pe(8 + i)

            def ffn_pe(layer, h):
                pe.wait_ge(h_ready, h)
                at_least(pe, acc_drained, layer)
                for i in range(4):
                    ph = PHASES[f"ffn{layer}_{i}"]
                    if ph.kind == "gu":
                        slot_loop(pe, ph, lambda i, k, s: proj_slot(ph, k, s))
                        a0 = ph.a
                    else:
                        if i == 1:
                            acc_zero(True, False)
                        slot_loop(pe, ph, lambda i, k, s: down_slot(ph, k, s, lambda s, c: s * 2 + (a0 + c + 1)))
                acc_zero(False, True).then_inc(acc_ready, 1)

            def turn(dst, src):
                return nc.tensor.transpose(dst, src, C("ident"))

            def softmax_pe(kind, u0, o0, q_at, k_at, v_at, cmp=None):
                us = units(kind)
                branches = 2 if kind == "nsa" else 1
                for step in range(len(us) + 2):
                    if step < len(us):
                        u = u0 + step
                        g, qt, br = us[step]
                        at_least(pe, scores_masked, u)
                        for h in range(4):
                            for last_c, (q, kk) in zip((False, True) if kind == "xa" else (True,), zip(q_at(g, h, qt), k_at(g, h, br))):
                                at = place(kind, h)
                                last = mm(ps[:, at // 2, (at % 2) * 256:(at % 2 + 1) * 256], q, kk,
                                          start=(not last_c or kind != "xa"), stop=last_c)
                        last.then_inc(scores_ready, 1)
                    if 1 <= step <= len(us):
                        u = u0 + step - 1
                        pe.wait_ge(probs_ready, u + 1)
                        at_least(pe, pt_copied, u)
                        for h in range(4):
                            for kt in range(2):
                                n = h * 2 + kt
                                last = turn(ps[:, 2 + n // 4, (n % 4) * P:(n % 4 + 1) * P],
                                            PROBS[u % 2][:, h * 256 + kt * P:h * 256 + (kt + 1) * P])
                        last.then_inc(pt_ready, 1)
                    if step >= 2:
                        u = u0 + step - 2
                        g, qt, br = us[step - 2]
                        o = o0 + (step - 2) // branches
                        pe.wait_ge(pt_copied, u + 1)
                        if br == 0:
                            at_least(pe, o_drained, o - 1)
                        bank = 4 + 2 * (o % 2)
                        pt = PT[u % 2]
                        for h in range(4):
                            at = 2 * place(kind, h)
                            if kind == "xa":
                                for eb in range(2):
                                    n = 2 * h + eb
                                    for kt in range(2):
                                        last = mm(ps[:, bank + n // 4, (n % 4) * P:(n % 4 + 1) * P], v_at(g, h, kt, eb),
                                                  pt[:, (at + kt) * P:(at + kt + 1) * P], start=(kt == 0), stop=(kt == 1))
                                continue
                            half = 64 * (h % 2)
                            dst = ps[half:half + 64, bank, (h // 2) * P:(h // 2 + 1) * P]
                            fresh = h < 2
                            if cmp is not None and br == 0:
                                vc, pc = cmp(g, h, qt)
                                mm(dst, vc, pc, start=fresh, stop=False, skip_group_check=True)
                                fresh = False
                            for kt in range(2):
                                last = mm(dst, v_at(g, h, kt, br), pt[:, (at + kt) * P:(at + kt + 1) * P],
                                          start=(fresh and kt == 0 and br == 0), stop=(kt == 1 and br == branches - 1),
                                          skip_group_check=True)
                        last.then_inc(pv_done, 1)

            def xa_pe(layer, h):
                norm_pe(layer * 4 + 1)
                proj_pe(f"kv{layer}", h)
                norm_pe(layer * 4 + 2)
                proj_pe(f"q{layer}", h + 1)
                pe.wait_ge(head_sq, 2 + layer)
                for n in range(8):
                    for b in range(2):
                        last = mm(ps[:, n // 2, (n % 2) * 256:(n % 2 + 1) * 256], C("ones"), W(24 + 2 * n + b),
                                  start=(b == 0), stop=(b == 1))
                last.then_inc(head_sums, 1)
                for tt in range(2):
                    for b in range(8):
                        n = tt * 8 + b
                        last = turn(ps[:, 4 + n // 4, (n % 4) * P:(n % 4 + 1) * P], W(8 + b)[:, tt * P:(tt + 1) * P])
                last.then_inc(v_turned, 1)
                pe.wait_ge(v_copied, 2 + 2 * layer)
                pe.wait_ge(heads_ready, 2 + layer)
                softmax_pe("xa", XA_U[layer], XA_O[layer],
                           lambda g, h, qt: [W(16 + 2 * h + c)[:, qt * P:(qt + 1) * P] for c in range(2)],
                           lambda g, h, br: [W(2 * h + c) for c in range(2)],
                           lambda g, h, kt, eb: Wc(6144 + kt * 1024 + (2 * h + eb) * P, P))
                proj_pe(f"o{layer}", h + 2)

            pe.wait_ge(params_loaded, 32)
            pe.wait_ge(zero_ready, 1)
            norm_pe(0)
            proj_pe("ab_in", 1)
            pe.wait_ge(head_sq, 1)
            for b in range(5):
                last = mm(ps[:, b // 2, (b % 2) * 256:(b % 2 + 1) * 256], C("ones64"), W(18 + b), start=True, stop=True)
            last.then_inc(head_sums, 1)
            for tt in range(2):
                turn(ps[:, 4, tt * P:(tt + 1) * P], W(5)[:, tt * P:(tt + 1) * P])
                for b in range(4):
                    last = turn(ps[:, 5 + tt, b * P:(b + 1) * P], W(14 + b)[:, tt * P:(tt + 1) * P])
            last.then_inc(v_turned, 1)
            pe.wait_ge(rope_in, 1)
            for b in range(5):
                last = mm(ps[:, b // 2, (b % 2) * 256:(b % 2 + 1) * 256], C("rot"), W(b), start=True, stop=True)
            last.then_inc(rope_rot, 1)
            pe.wait_ge(heads_ready, 1)
            for g in range(2):
                last = mm(ps[:, 3, g * 256:(g + 1) * 256], C(f"dup{g}"), W(4), start=True, stop=True)
            last.then_inc(dup_ready, 1)
            pe.wait_ge(dup_copied, 1)
            softmax_pe("swa", SWA_U, SWA_O,
                       lambda g, h, qt: [W(2 * g + h // 2)[64 * (h % 2):64 * (h % 2) + 64, qt * P:(qt + 1) * P]],
                       lambda g, h, br: [W(35 + g)[64 * (h % 2):64 * (h % 2) + 64, :]],
                       lambda g, h, kt, br: Wc(9472 + kt * P + g * 64, 64))
            for u in range(4):
                if u == 0:
                    pe.wait_ge(o_drained, 4)
                at_least(pe, z_masked, u)
                for h in range(2):
                    rows = slice(64 * h, 64 * h + 64)
                    for kt in range(2):
                        last = mm(ps[:, h, kt * 256:(kt + 1) * 256], W(10 + u)[rows, kt * P:(kt + 1) * P], W(6 + u)[rows, :],
                                  start=True, stop=True)
                last.then_inc(z_ready, 1)
                pe.wait_ge(sp_ready, u + 1)
                sp_t = SB_T[u % 2]
                for h in range(2):
                    lo_t, hi_t = sp_t[:, h * 512:h * 512 + 256], sp_t[:, h * 512 + 256:h * 512 + 512]
                    mm(ps[:, 2 + h, 0:256], C("ge"), lo_t, start=True, stop=False)
                    mm(ps[:, 2 + h, 0:256], C("ones"), hi_t, start=False, stop=True)
                    last = mm(ps[:, 2 + h, 256:512], C("ge"), hi_t, start=True, stop=True)
                last.then_inc(cs_ready, 1)
                pe.wait_ge(a_ready, u + 1)
                o = SB_O + u
                at_least(pe, o_drained, o - 1)
                for h in range(2):
                    for kt in range(2):
                        last = mm(ps[64 * h:64 * h + 64, 4 + 2 * (o % 2), 0:256], Wc(9728 + kt * 512 + (2 * u + h) * 64, 64),
                                  PT[u % 2][:, h * 512 + kt * 256:h * 512 + (kt + 1) * 256], start=(kt == 0), stop=(kt == 1))
                last.then_inc(sb_pv_done, 1)
            proj_pe("ab_out", 2)
            xa_pe(0, 3)
            norm_pe(3)
            ffn_pe(0, 6)
            norm_pe(4)
            proj_pe("hg_in", 7)
            pe.wait_ge(banks_drained, PHASES["hg_in"].e + PHASES["hg_in"].n)
            for tt in range(2):
                for b in range(8):
                    n = tt * 8 + b
                    last = turn(ps[:, 4 + n // 4, (n % 4) * P:(n % 4 + 1) * P], W(16 + b)[:, tt * P:(tt + 1) * P])
            last.then_inc(v_turned, 1)

            def hg_scores(lhs, rhs, tiles):
                for h in range(8):
                    for n, tt in enumerate(tiles):
                        col = h * len(tiles) + n
                        last = mm(ps[:, col // 4, (col % 4) * P:(col % 4 + 1) * P], lhs(h, tt[0]), rhs(h, tt[1]), start=True, stop=True)
                last.then_inc(hg_s, 1)

            pe.wait_ge(hg_kf, 1)
            hg_scores(lambda h, t: W(32 + h)[:, t * P:(t + 1) * P], lambda h, t: W(h)[:, t * P:(t + 1) * P], [(0, 0), (1, 1)])
            for lv in range(HG_LEVELS + 1):
                pe.wait_ge(hg_x, lv + 1)
                pe.wait_ge(hg_a, lv + 1)
                both = lambda h, t: hf[:, h * BLK + t * P:h * BLK + (t + 1) * P]
                hg_scores(both, both, [(0, 1)] if lv == 0 else [(0, 0), (1, 1)])
            pe.wait_ge(hg_a, HG_LEVELS + 2)
            pe.wait_ge(v_copied, 3)
            A = lambda h, n: Wc(10240 + h * 384 + n * P, P)
            V = lambda h, t: Wc(13312 + t * 1024 + h * P, P)
            for h in range(8):
                o = lambda t: ps[:, h // 2, (h % 2) * 256 + t * P:(h % 2) * 256 + (t + 1) * P]
                mm(o(0), V(h, 0), A(h, 0), start=True, stop=True)
                mm(o(1), V(h, 0), A(h, 1), start=True, stop=False)
                last = mm(o(1), V(h, 1), A(h, 2), start=False, stop=True)
            last.then_inc(hg_o, 1)
            pe.wait_ge(hg_osq, 1)
            for h in range(8):
                last = mm(ps[:, 4 + h // 2, (h % 2) * 256:(h % 2 + 1) * 256], C("ones"), hf[:, h * BLK:(h + 1) * BLK],
                          start=True, stop=True)
            last.then_inc(hg_osum, 1)
            proj_pe("hg_out", 8)
            xa_pe(1, 9)
            norm_pe(7)
            ffn_pe(1, 12)
            ph = PHASES["pool"]
            pe.wait_ge(h_ready, 13)
            pe.wait_ge(lo_ready, ph.g + 1)
            p = ph.g % DEPTH
            pe.wait_ge(banks_drained, ph.e)
            for g in range(4):
                for b in range(2):
                    for c in range(2):
                        w = slice(((g * 2 + b) * 2 + c) * P, ((g * 2 + b) * 2 + c + 1) * P)
                        m = slice((2 * g + c) * BLK, (2 * g + c + 1) * BLK)
                        last = split_mm(ps[:, g, b * BLK:(b + 1) * BLK], whi[p][:, w], wlo[p][:, w], hh[:, m], hl[:, m],
                                        c == 0, c == 1)
            last.then_inc(slot_used, 1)

            layer_norm_pe(0, banks_drained, ph.e + 1)
            ffn_pe(2, 14)
            layer_norm_pe(1, acc_drained, 3)
            proj_pe("nsa_in", 15)
            pe.wait_ge(w1_loaded, 16)
            for tt in range(2):
                for c in range(NB):
                    last = mm(ps[:, 7, tt * 48:(tt + 1) * 48], x[:, c * BLK + tt * P:c * BLK + (tt + 1) * P],
                              Wc(12288 + c * 48, 48), start=(c == 0), stop=(c == NB - 1))
            last.then_inc(gates_ps, 1)
            pe.wait_ge(banks_drained, PHASES["nsa_in"].e + PHASES["nsa_in"].n)
            for n, b0 in enumerate(ROPED):
                for b in range(2):
                    last = mm(ps[:, n, b * 256:(b + 1) * 256], C("rot"), W(b0 + b), start=True, stop=True)
            last.then_inc(rope_rot, 1)
            pe.wait_ge(heads_ready, 4)
            for br in range(2):
                for g in range(4):
                    last = mm(ps[:, g // 2 + 2 * br, (g % 2) * 256:(g % 2 + 1) * 256], C(f"dup{g % 2}"),
                              W(8 + 2 * br + g // 2), start=True, stop=True)
            last.then_inc(cmp_dup, 1)
            pe.wait_ge(cmp_cols, 1)
            for br, pe_name in enumerate(("pe_k", "pe_v")):
                for j in range(16):
                    cols = W(20 + 4 * br, 2).rearrange("p (g m) -> p g m", g=4)[:, :, j:j + 8 * (NCMP - 1) + 1:8]
                    mm(ps[:, 6, 64 * br:64 * br + 60], Wc(8192 + 2048 * br + j * P, P), cols, start=(j == 0), stop=(j == 15))
                for j in range(16):
                    last = mm(ps[:, 5, br:br + 1], Wc(8192 + 2048 * br + j * P, P), R(pe_name, j), start=(j == 0), stop=(j == 15))
            last.then_inc(cmp_hidden, 1)
            pe.wait_ge(cmp_silu, 1)
            mm(ps[:, 1, 0:60], R("w2_k", 0, 128), small[:, 160:220], start=True, stop=True)
            for g in range(4):
                last = mm(ps[0:NCMP, 2, g * 64:(g + 1) * 64], small[:, 220 + g * NCMP:220 + (g + 1) * NCMP], R("w2_v", 0, 64),
                          start=True, stop=True)
            last.then_inc(cmp_kv, 1)
            pe.wait_ge(cmp_kv_copied, 1)
            mm(ps[:, 3, 0:60], C("rot"), small[:, 288:348], start=True, stop=True).then_inc(cmp_rot, 1)
            pe.wait_ge(cmp_roped, 1)
            for qt in range(2):
                for h in range(16):
                    g, rows = h // 4, slice(64 * (h % 2), 64 * (h % 2) + 64)
                    at = (qt * 8 + h // 2) * NCMP
                    last = mm(ps[:, 4 + h % 2, at:at + NCMP], W(h // 2)[rows, qt * P:(qt + 1) * P],
                              small[rows, 288 + g * 15:288 + g * 15 + 15], start=True, stop=True)
            last.then_inc(cmp_scores, 1)
            pe.wait_ge(gates_ready, 1)
            for n, b0 in enumerate((12, 16)):
                for g in range(4):
                    last = mm(ps[:, 2 * n + g // 2, (g % 2) * 256:(g % 2 + 1) * 256], C(f"dup{g % 2}"), W(b0 + g // 2),
                              start=True, stop=True)
            last.then_inc(dup_ready, 1)
            for n, b0 in enumerate((14, 18)):
                for tt in range(2):
                    for b in range(2):
                        last = turn(ps[:, 6 + n, (tt * 2 + b) * P:(tt * 2 + b + 1) * P], W(b0 + b)[:, tt * P:(tt + 1) * P])
            last.then_inc(v_turned, 1)
            pe.wait_ge(cmp_probs, 1)
            pe.wait_ge(dup_copied, 2)
            pe.wait_ge(v_copied, 5)
            for n in range(4):
                for h in range(8):
                    head = (n // 2) * 8 + h
                    last = turn(ps[0:NCMP, 2 * n + h // 4, (h % 4) * P:(h % 4 + 1) * P],
                                Wc(10240 + ((head % 2) * 16 + (n % 2) * 8 + head // 2) * NCMP, NCMP))
            last.then_inc(cmp_turned, 1)
            pe.wait_ge(cmp_ready, 1)
            softmax_pe("nsa", NSA_U, NSA_O,
                       lambda g, h, qt: [W(2 * g + h // 2)[64 * (h % 2):64 * (h % 2) + 64, qt * P:(qt + 1) * P]],
                       lambda g, h, br: [W(20 + 4 * br + g)[64 * (h % 2):64 * (h % 2) + 64, :]],
                       lambda g, h, kt, br: Wc(7168 + 512 * br + kt * 256 + g * 64, 64),
                       cmp=lambda g, h, qt: (rstd[0:NCMP, g * 64:(g + 1) * 64],
                                             Wc(PCT[g // 2] + ((g % 2) * 4 + h) * 256 + qt * P, P)[0:NCMP, :]))
            proj_pe("nsa_out", 16)
            layer_norm_pe(2, banks_drained, PHASES["nsa_out"].e + PHASES["nsa_out"].n)
            pe.wait_ge(x_ready, 3)
            for tt in range(2):
                for c in range(NB):
                    last = mm(ps[:, 0, tt * 8:(tt + 1) * 8], x[:, c * BLK + tt * P:c * BLK + (tt + 1) * P],
                              R("router", c * 8, 8), start=(c == 0), stop=(c == NB - 1))
            last.then_inc(logits_ps, 1)
            pe.wait_ge(cw_diag, 1)
            for n in range(4):
                last = mm(ps[:, 1 + n, :], C("ones"), Wc(n * 512, 512), start=True, stop=True)
            last.then_inc(cw_ps, 1)
            gu, down = PHASES["moe_gu"], PHASES["moe_down"]
            pe.wait_ge(h_ready, 17)
            pe.wait_ge(cw_ready, 1)
            acc_zero(True, False)
            with pe.Fori(0, EXPERTS) as e:
                with pe.Fori(0, 2) as part:
                    half = e * 2 + part
                    slot_loop(pe, gu, lambda i, k, s: proj_slot(gu, k, s, half * PER_HALF, half * HALF))
                    slot_loop(pe, down, lambda i, k, s: down_slot(
                        down, k, s, lambda s, c: s * 2 + (gu.a + c + 1) + half * HALF, half * PER_HALF))
            acc_zero(False, True).then_inc(acc_ready, 1)
            layer_norm_pe(3, acc_drained, 4)

        @block.vector
        def _(dve):
            chain = [0]
            V = nc.vector

            def step(ins):
                chain[0] = chain[0] + 1
                ins.then_inc(dve_step, 1)

            def sync():
                dve.wait_ge(dve_step, chain[0])

            def link(ins):
                step(ins)
                sync()

            def drain(ph, k, s, write, off_g=0):
                dve.wait_ge(slot_used, s + (ph.g + 1) + off_g)
                write((ph.g + k) % DEPTH, s).then_inc(banks_drained, 1)

            def proj_copy(name, b0):
                ph = PHASES[name]

                def write(bank, s):
                    at = bass.ds(s * 512 + b0 * BLK, 512) if not isinstance(s, int) else slice(s * 512 + b0 * BLK, s * 512 + b0 * BLK + 512)
                    return V.tensor_copy(work[:, at], ps[:, bank, :])

                slot_loop(dve, ph, lambda i, k, s: drain(ph, k, s, write))
                dve.wait_ge(banks_drained, ph.e + ph.n)

            def proj_add(name, alpha=1.0):
                ph = PHASES[name]
                slot_loop(dve, ph, lambda i, k, s: drain(ph, k, s, lambda bank, s: (
                    V.scalar_tensor_tensor(out=xs(s), in0=xs(s), scalar=alpha, in1=ps[:, bank, :], op0=ALU.mult, op1=ALU.add))))
                dve.wait_ge(banks_drained, ph.e + ph.n)

            def xs(s):
                return x[:, bass.ds(s * 512, 512)] if not isinstance(s, int) else x[:, s * 512:s * 512 + 512]

            def split_h(src):
                link(V.tensor_copy(hh[:, :], src))
                V.tensor_tensor(hl[:, :], src, hh[:, :].bitcast(F32), ALU.subtract).then_inc(h_ready, 1)

            def rms_norm(n, src, gain, at):
                V.tensor_tensor(hf[:, :], src, src, ALU.mult).then_inc(squares_ready, 1)
                dve.wait_ge(rstd_ready, n + 1)
                for b in range(NB):
                    step(V.scalar_tensor_tensor(out=hf[:, b * BLK:(b + 1) * BLK], in0=src[:, b * BLK:(b + 1) * BLK],
                                                scalar=R(gain, at + b), in1=rstd[:, :], op0=ALU.mult, op1=ALU.mult))
                sync()
                split_h(hf[:, :])

            def layer_norm(i, g_at, last=False):
                dve.wait_ge(mean_ready, i + 1)
                for b in range(NB):
                    step(V.scalar_tensor_tensor(out=xb(b), in0=ps[:, 7, 0:BLK], scalar=-1.0 / D, in1=xb(b),
                                                op0=ALU.mult, op1=ALU.add))
                sync()
                V.tensor_tensor(hf[:, :], x[:, :], x[:, :], ALU.mult).then_inc(squares_ready, 1)
                dve.wait_ge(rstd_ready, 9 + i)
                for b in range(NB):
                    step(V.scalar_tensor_tensor(out=xb(b), in0=xb(b), scalar=R("ln_g", g_at + b), in1=rstd[:, :],
                                                op0=ALU.mult, op1=ALU.mult))
                sync()
                for b in range(NB):
                    ins = V.tensor_scalar(xb(b), xb(b), R("ln_b", g_at + b), None, ALU.add)
                    if b < NB - 1:
                        step(ins)
                ins.then_inc(x_ready, 1)
                dve.wait_ge(x_ready, i + 1)
                if not last:
                    split_h(x[:, :])

            def softmax_dve(kind, u0, o0, scale, mask, o_blocks):
                us = units(kind)
                branches = 2 if kind == "nsa" else 1
                for st in range(len(us) + 2):
                    if st < len(us):
                        u = u0 + st
                        g, qt, br = us[st]
                        pr, s0 = PROBS[u % 2], 32 * (u % 2)
                        dve.wait_ge(scores_ready, u + 1)
                        at_least(dve, pt_ready, u - 1)
                        if mask is None:
                            V.tensor_scalar(pr, banks(0), scale, None, ALU.mult).then_inc(scores_masked, 1)
                        else:
                            V.scalar_tensor_tensor(out=r3(pr, 4), in0=r3(banks(0), 4), scalar=scale,
                                                   in1=mask(qt).unsqueeze(1).to_broadcast([P, 4, 256]),
                                                   op0=ALU.mult, op1=ALU.add).then_inc(scores_masked, 1)
                        dve.wait_ge(scores_masked, u + 1)
                        link(V.tensor_reduce(small[:, s0:s0 + 4], r3(pr, 4), AX, ALU.max))
                        if kind == "swa":
                            link(V.tensor_tensor(small[:, s0:s0 + 4], small[:, s0:s0 + 4], R("sinks", 4 * g, 4), ALU.max))
                            link(V.tensor_tensor(small[:, s0 + 8:s0 + 12], R("sinks", 4 * g, 4), small[:, s0:s0 + 4], ALU.subtract))
                        V.tensor_scalar(small[:, s0:s0 + 4], small[:, s0:s0 + 4], -1.0, None, ALU.mult).then_inc(negmax_ready, 1)
                    if 1 <= st <= len(us):
                        u = u0 + st - 1
                        g, qt, br = us[st - 1]
                        pr, s0 = PROBS[u % 2], 32 * (u % 2)
                        dve.wait_ge(exp_done, u + 1)
                        if kind == "swa":
                            link(V.tensor_tensor(small[:, s0 + 4:s0 + 8], small[:, s0 + 4:s0 + 8], small[:, s0 + 12:s0 + 16], ALU.add))
                        link(V.reciprocal(small[:, s0 + 16:s0 + 20], small[:, s0 + 4:s0 + 8]))
                        if kind == "nsa":
                            at = 64 + qt * 48 + g * 12
                            coef = small[:, s0 + 16:s0 + 20].rearrange("p (par j) -> p par j", par=2)
                            link(V.tensor_tensor(coef, coef, small[:, at:at + 12].rearrange(
                                "p (j par b) -> p par j b", j=2, par=2)[:, :, :, br + 1], ALU.mult))
                        for h in range(4):
                            ins = V.tensor_scalar(pr[:, h * 256:(h + 1) * 256], pr[:, h * 256:(h + 1) * 256],
                                                  small[:, s0 + 16 + h:s0 + 17 + h], None, ALU.mult)
                        ins.then_inc(probs_ready, 1)
                    if st >= 2:
                        u = u0 + st - 2
                        g, qt, br = us[st - 2]
                        if br == branches - 1:
                            o = o0 + (st - 2) // branches
                            dve.wait_ge(pv_done, u + 1)
                            evacuate(o, o_blocks(g), qt * P, 4 + 2 * (o % 2))

            def evacuate(o, blocks, col, bank, width=P):
                b0, n = blocks
                view = lambda t: t[:, :].rearrange("p (b c) -> p b c", b=NB)[:, b0:b0 + n, col:col + width]
                src = banks(bank)[:, 0:n * width].rearrange("p (b c) -> p b c", b=n)
                link(V.tensor_copy(view(hh), src))
                V.tensor_tensor(view(hl), src, view(hh).bitcast(F32), ALU.subtract).then_inc(o_drained, 1)

            def conv_ffn(layer, l, alpha):
                conv = l is not None
                for i in range(4):
                    ph = PHASES[f"ffn{layer}_{i}"]
                    if ph.kind == "down":
                        continue
                    c0 = chain[0]
                    first = 0 if i == 0 else HALF

                    def body(i, k, s, ph=ph, c0=c0, first=first):
                        bank = (ph.g + k) % DEPTH
                        buf = Wc(512 * bank, 512)
                        f = Wc(1536 + 256 * bank, 256)
                        chain[0] = s * steps + c0
                        dve.wait_ge(slot_used, s + (ph.g + 1))
                        if conv:
                            for b in range(2):
                                p0 = b * FF + first
                                step(V.tensor_scalar(buf[:, b * BLK:(b + 1) * BLK], ps[:, bank, b * BLK:(b + 1) * BLK],
                                                     Rd("conv_w", l * 132 + 88 + p0, s), Rd("conv_b", l * 44 + p0, s), ALU.mult, ALU.add))
                            sync()
                            for tap in (1, 2):
                                for b in range(2):
                                    p0 = b * FF + first
                                    o = buf[:, b * BLK + tap:(b + 1) * BLK]
                                    ins = V.scalar_tensor_tensor(out=o, in0=ps[:, bank, b * BLK:(b + 1) * BLK - tap],
                                                                 scalar=Rd("conv_w", l * 132 + (2 - tap) * 44 + p0, s), in1=o,
                                                                 op0=ALU.mult, op1=ALU.add)
                                    if (tap, b) != (2, 1):
                                        step(ins)
                                if tap == 1:
                                    sync()
                            ins.then_inc(banks_drained, 1)
                            dve.wait_ge(banks_drained, s + (ph.e + 1))
                            dve.wait_ge(gate_act, s + (ph.a + 1))
                            link(V.tensor_tensor(f, buf[:, 0:BLK], buf[:, BLK:2 * BLK], ALU.mult))
                        else:
                            dve.wait_ge(gate_act, s + (ph.a + 1))
                            V.tensor_tensor(f, buf[:, 0:BLK], ps[:, bank, BLK:2 * BLK], ALU.mult).then_inc(banks_drained, 1)
                            dve.wait_ge(banks_drained, s + (ph.e + 1))
                        split_act(s, f)

                    steps = 7 if conv else 1
                    slot_loop(dve, ph, body)
                    chain[0] = c0 + steps * ph.n
                dve.wait_ge(acc_ready, layer + 1)
                for b in range(4):
                    ins = V.scalar_tensor_tensor(out=xs(b), in0=xs(b), scalar=alpha, in1=ps[:, 3 + b, :], op0=ALU.mult, op1=ALU.add)
                ins.then_inc(acc_drained, 1)
                dve.wait_ge(acc_drained, layer + 1)

            def Rd(name, a, s):
                at = PARAM[name][0] + a
                return par[:, at + s:at + s + 1] if isinstance(s, int) else par[:, bass.ds(s + at, 1)]

            def split_act(s, f):
                at = slice(s * BLK, (s + 1) * BLK) if isinstance(s, int) else bass.ds(s * BLK, BLK)
                link(V.tensor_copy(ahi[:, at], f))
                V.tensor_tensor(alo[:, at], f, ahi[:, at].bitcast(F32), ALU.subtract).then_inc(act_ready, 1)

            def xa(layer):
                dve.wait_ge(mem_loaded, 16 * (layer + 1))
                rms_norm(layer * 4 + 1, W(24, 8), "norm_mem", layer * 8)
                proj_copy(f"kv{layer}", 0)
                rms_norm(layer * 4 + 2, x[:, :], "norm_cross", layer * 8)
                proj_copy(f"q{layer}", 16)
                step(V.tensor_tensor(W(24, 8), W(16, 8), W(16, 8), ALU.mult))
                V.tensor_tensor(W(32, 8), W(0, 8), W(0, 8), ALU.mult).then_inc(head_sq, 1)
                dve.wait_ge(head_rstd, 2 + layer)
                for h in range(8):
                    for c in range(2):
                        blk = W(16 + 2 * h + c) if h < 4 else W(2 * (h - 4) + c)
                        ins = V.scalar_tensor_tensor(out=blk, in0=blk, scalar=R("xa_q" if h < 4 else "xa_k", 2 * layer + c),
                                                     in1=W(42 + h), op0=ALU.mult, op1=ALU.mult)
                        if (h, c) == (7, 1):
                            ins.then_inc(heads_ready, 1)
                dve.wait_ge(heads_ready, 2 + layer)
                dve.wait_ge(v_turned, 2 + 2 * layer)
                V.tensor_copy(W(24, 8), banks(4, 4)).then_inc(v_copied, 1)
                softmax_dve("xa", XA_U[layer], XA_O[layer], 256 ** -0.5, None, lambda g: (0, 8))
                attention_whole(XA_O[layer] + 2)
                proj_add(f"o{layer}")

            def attention_whole(outputs):
                dve.wait_ge(o_drained, outputs)
                V.memset(small[:, 639:640], 0.0).then_inc(h_ready, 1)

            def rope(dst, rot_ps, n, cos, sin, tmp):
                wide = lambda t: t.unsqueeze(1).to_broadcast([P, n, t.shape[-1]])
                link(V.tensor_tensor(r3(tmp, n), r3(rot_ps, n), wide(sin), ALU.mult))
                link(V.tensor_tensor(r3(dst, n), r3(dst, n), wide(cos), ALU.mult))
                return V.tensor_tensor(dst, dst, tmp, ALU.add)

            V.memset(zero[:, :].bitcast(F32), 0.0).then_inc(zero_ready, 1)
            dve.wait_ge(params_loaded, 32)
            dve.wait_ge(positions_loaded, 16)
            ang, turns, pos = W(43), W(44), W(42)
            link(V.tensor_copy(ang, pos.bitcast(I32)))
            link(V.tensor_scalar(ang, ang, C("invf"), None, ALU.mult))
            link(V.tensor_scalar(turns, ang, float(1.0 / (2.0 * np.pi)), ROUND, ALU.mult, ALU.add))
            link(V.tensor_scalar(turns, turns, ROUND, None, ALU.subtract))
            for part in TWO_PI:
                link(V.scalar_tensor_tensor(out=ang, in0=turns, scalar=-part, in1=ang, op0=ALU.mult, op1=ALU.add))
            link(V.tensor_scalar(W(33), ang, PI, -PI, ALU.min, ALU.max))
            link(V.tensor_scalar(ang, ang, float(np.pi / 2), None, ALU.add))
            link(V.tensor_scalar(turns, ang, PI, float(-2 * np.pi), ALU.is_gt, ALU.mult))
            link(V.tensor_tensor(ang, ang, turns, ALU.add))
            V.tensor_scalar(W(34), ang, PI, -PI, ALU.min, ALU.max).then_inc(angles_ready, 1)
            dve.wait_ge(x_loaded, 16)
            rms_norm(0, x[:, :], "norm_mix", 0)
            proj_copy("ab_in", 0)
            V.tensor_tensor(W(18, 5), W(0, 5), W(0, 5), ALU.mult).then_inc(head_sq, 1)
            step(V.tensor_scalar(W(6, 4), W(6, 4), 64 ** -0.5, None, ALU.mult))
            dve.wait_ge(head_rstd, 1)
            step(V.scalar_tensor_tensor(out=W(0, 4), in0=W(0, 4), scalar=R("swa_q"), in1=W(23, 4), op0=ALU.mult, op1=ALU.mult))
            V.scalar_tensor_tensor(out=W(4), in0=W(4), scalar=R("swa_k"), in1=W(27), op0=ALU.mult, op1=ALU.mult).then_inc(rope_in, 1)
            dve.wait_ge(rope_in, 1)
            dve.wait_ge(v_turned, 1)
            step(V.tensor_copy(W(37), ps[:, 4, 0:256]))
            V.tensor_copy(W(38, 4), banks(5)).then_inc(v_copied, 1)
            dve.wait_ge(rope_rot, 1)
            dve.wait_ge(sines_ready, 1)
            rope(W(0, 5), banks(0, 3)[:, 0:5 * BLK], 5, W(34), W(33), W(28, 5)).then_inc(heads_ready, 1)
            dve.wait_ge(dup_ready, 1)
            V.tensor_copy(W(35, 2), ps[:, 3, :]).then_inc(dup_copied, 1)
            dve.wait_ge(stage_loaded, 16)
            softmax_dve("swa", SWA_U, SWA_O, 64 ** -0.5, lambda qt: stage[:, qt * 256:(qt + 1) * 256], lambda g: (2 * g, 2))
            for u in range(4):
                z, t = PROBS[u % 2], SB_T[u % 2]
                dve.wait_ge(z_ready, u + 1)
                V.tensor_tensor(r3(z, 2), r3(banks(0), 2), stage[:, 512:1024].unsqueeze(1).to_broadcast([P, 2, 512]),
                                ALU.add).then_inc(z_masked, 1)
                dve.wait_ge(soft_ready, u + 1)
                V.scalar_tensor_tensor(out=t, in0=z, scalar=0.0, in1=t, op0=ALU.max, op1=ALU.add).then_inc(sp_ready, 1)
                dve.wait_ge(cs_ready, u + 1)
                V.tensor_tensor(z, z, banks(2), ALU.subtract).then_inc(d_ready, 1)
                dve.wait_ge(sb_pv_done, u + 1)
                o = SB_O + u
                evacuate(o, (4 + u, 1), 0, 4 + 2 * (o % 2), BLK)
            attention_whole(SB_O + 4)
            proj_add("ab_out")
            xa(0)
            rms_norm(3, x[:, :], "norm_ffn", 0)
            conv_ffn(0, 0, 1.0)
            rms_norm(4, x[:, :], "norm_mix", 8)
            link(V.tensor_tensor(small[:, 408:416], R("lb", 0, 8), R("lb", 8, 8), ALU.max))
            step(V.tensor_tensor(small[:, 400:408], R("lb", 0, 8), small[:, 408:416], ALU.subtract))
            V.tensor_tensor(small[:, 408:416], R("lb", 8, 8), small[:, 408:416], ALU.subtract).then_inc(hg_lb, 1)
            dve.wait_ge(hg_lb_exp, 1)
            link(V.tensor_tensor(small[:, 440:448], small[:, 416:424], small[:, 424:432], ALU.add))
            link(V.reciprocal(small[:, 440:448], small[:, 440:448]))
            link(V.tensor_tensor(small[:, 432:440], small[:, 424:432], small[:, 440:448], ALU.mult))
            link(V.tensor_scalar(small[:, 440:448], small[:, 432:440], -1.0, 1.0, ALU.mult, ALU.add))
            proj_copy("hg_in", 0)
            dve.wait_ge(hg_sig, 1)
            for h in range(8):
                step(V.tensor_scalar(W(32 + h), W(32 + h), small[:, 440 + h:441 + h], None, ALU.mult))
                ins = V.tensor_scalar(W(8 + h), W(8 + h), small[:, 440 + h:441 + h], small[:, 432 + h:433 + h], ALU.mult, ALU.add)
                if h < 7:
                    step(ins)
            ins.then_inc(hg_kf, 1)
            dve.wait_ge(v_turned, 3)
            V.tensor_copy(W(52, 8), banks(4, 4)).then_inc(v_copied, 1)
            link(V.memset(hf[:, :], 1.0))
            link(V.memset(hf[:, 0:NB * BLK:P], 0.0))
            step(V.memset(W(40, 12), 0.0))
            dve.wait_ge(hg_log, 1)
            link(V.tensor_tensor_scan(W(8, 8), hf[:, :], W(8, 8), 0.0, ALU.mult, ALU.add))
            dve.wait_ge(stage_loaded, 32)
            A = W(40, 12).rearrange("p (h n t) -> p h n t", h=8, n=3)
            tiles = lambda t: t.rearrange("p (h n t) -> p h n t", h=8, n=2)
            b, d, e_, q, key, xk = W(8, 8), W(16, 8), W(16, 8), W(0, 8), W(32, 8), hf[:, :]

            def keep(lv, n):
                dve.wait_ge(hg_s, n)
                mask = stage[:, lv * P:(lv + 1) * P].bitcast(I32)
                for tt in range(2):
                    ins = V.copy_predicated(A[:, :, 2 * tt, :], mask.unsqueeze(1).to_broadcast([P, 8, P]),
                                            tiles(banks(0, 4))[:, :, tt, :])
                    if tt == 0:
                        step(ins)
                ins.then_inc(hg_a, 1)
                dve.wait_ge(hg_a, n)

            keep(0, 1)
            for lv in range(HG_LEVELS + 1):
                if lv == 0:
                    step(V.tensor_tensor(tiles(d)[:, :, 0, :], tiles(b)[:, :, 0, P - 1:P].to_broadcast([P, 8, P]),
                                         tiles(b)[:, :, 0, :], ALU.subtract))
                    V.tensor_copy(tiles(d)[:, :, 1, :], tiles(b)[:, :, 1, :]).then_inc(hg_d, 1)
                    half = P
                else:
                    half = P >> lv
                    cut = lambda t: t.rearrange("p (n t) -> p n t", t=2 * half)
                    V.tensor_tensor(cut(d), cut(b), cut(b)[:, :, half - 1:half].to_broadcast([P, NB * BLK // (2 * half), 2 * half]),
                                    ALU.subtract).then_inc(hg_d, 1)
                cut = lambda t: t.rearrange("p (n t) -> p n t", t=2 * half)
                dve.wait_ge(hg_e, lv + 1)
                dve.wait_ge(hg_s, lv + 1)
                step(V.tensor_tensor(cut(xk)[:, :, 0:half], cut(e_)[:, :, 0:half], cut(key)[:, :, 0:half], ALU.mult))
                V.tensor_tensor(cut(xk)[:, :, half:2 * half], cut(e_)[:, :, half:2 * half], cut(q)[:, :, half:2 * half],
                                ALU.mult).then_inc(hg_x, 1)
                if lv == 0:
                    dve.wait_ge(hg_s, 2)
                    V.tensor_copy(A[:, :, 1, :], r3(banks(0), 8)).then_inc(hg_a, 1)
                    dve.wait_ge(hg_a, 2)
                else:
                    keep(lv, lv + 2)
            dve.wait_ge(hg_o, 1)
            link(V.tensor_copy(W(16, 8), banks(0, 4)))
            V.tensor_tensor(hf[:, :], W(16, 8), W(16, 8), ALU.mult).then_inc(hg_osq, 1)
            dve.wait_ge(hg_orstd, 1)
            link(V.tensor_tensor(W(16, 8), W(16, 8), W(8, 8), ALU.mult))
            link(V.scalar_tensor_tensor(out=W(16, 8), in0=W(16, 8), scalar=R("o_norm"), in1=W(24, 8), op0=ALU.mult, op1=ALU.mult))
            split_h(W(16, 8))
            proj_add("hg_out")
            xa(1)
            rms_norm(7, x[:, :], "norm_ffn", 8)
            conv_ffn(1, 1, 1.0)
            pad = 16
            sums = [Wc(4352 * i, NB * (pad + BLK)).rearrange("p (b t) -> p b t", b=NB) for i in range(2)]
            for i in range(2):
                step(V.memset(sums[i][:, :, 0:pad], 0.0))
            link(V.tensor_copy(sums[0][:, :, pad:], x[:, :].rearrange("p (b t) -> p b t", b=NB)))
            dve.wait_ge(stage_loaded, 48)
            for g in range(4):
                old, new, back = sums[g % 2], sums[(g + 1) % 2], 1 << g
                link(V.tensor_tensor(new[:, 2 * g:, pad:], old[:, 2 * g:, pad:], old[:, 2 * g:, pad - back:pad + BLK - back], ALU.add))
                count = stage[:, g * BLK:(g + 1) * BLK].unsqueeze(1).to_broadcast([P, 2, BLK])
                step(V.tensor_tensor(r3(hf[:, 2 * g * BLK:(2 * g + 2) * BLK], 2), new[:, 2 * g:2 * g + 2, pad:], count, ALU.mult))
            sync()
            link(V.tensor_tensor(hf[:, :], hf[:, :], x[:, :], ALU.subtract))
            split_h(hf[:, :])
            dve.wait_ge(h_ready, 13)
            step(V.tensor_scalar(hf[:, :], x[:, :], ALPHA, None, ALU.mult))
            dve.wait_ge(slot_used, PHASES["pool"].g + 1)
            sync()
            for c in range(NB):
                ins = V.scalar_tensor_tensor(out=xb(c), in0=ps[:, c // 2, (c % 2) * BLK:(c % 2 + 1) * BLK], scalar=R("pool_scale", c),
                                             in1=hf[:, c * BLK:(c + 1) * BLK], op0=ALU.mult, op1=ALU.add)
            ins.then_inc(banks_drained, 1)
            layer_norm(0, 0)
            conv_ffn(2, None, ALPHA)
            layer_norm(1, 8)
            proj_copy("nsa_in", 0)
            dve.wait_ge(rope_rot, 2)
            dve.wait_ge(stage_loaded, 64)
            for n, b0 in enumerate(ROPED):
                ins = rope(W(b0, 2), ps[:, n, :], 2, stage[:, 512:768], stage[:, 768:1024], W(50 + 2 * (n % 2), 2))
                if n < 5:
                    step(ins)
            ins.then_inc(heads_ready, 1)
            dve.wait_ge(cmp_dup, 1)
            for br in range(2):
                for odd in range(2):
                    rows = slice(64 * odd, 64 * odd + 64)
                    ins = V.tensor_copy(W(20 + 4 * br, 2)[rows, :].rearrange("p (g m) -> p g m", g=4),
                                        banks(2 * br)[rows, :].rearrange("p (g m two) -> p g m two", g=4, two=2)[:, :, :, odd])
                    if (br, odd) != (1, 1):
                        step(ins)
            ins.then_inc(cmp_cols, 1)
            dve.wait_ge(cmp_hidden, 1)
            V.tensor_copy(small[:, 280:282], ps[:, 5, 0:2]).then_inc(cmp_bias, 1)
            dve.wait_ge(cmp_kv, 1)
            step(V.tensor_copy(rstd[0:NCMP, :], ps[0:NCMP, 2, 0:256]))
            V.tensor_copy(small[:, 288:348], ps[:, 1, 0:60]).then_inc(cmp_kv_copied, 1)
            dve.wait_ge(cmp_rot, 1)
            dve.wait_ge(cmp_kv_copied, 1)
            rope(small[:, 288:348], ps[:, 3, 0:60], 4, C("cend_cos"), C("cend_sin"), small[:, 348:408]).then_inc(cmp_roped, 1)
            dve.wait_ge(cmp_scores, 1)
            rows_of = lambda t: t.rearrange("p (h n) -> p h n", n=NCMP)
            wide = lambda t: t.unsqueeze(2).to_broadcast([P, 32, NCMP])
            pc = Wc(10240, 480)
            for n in range(4):
                odd, qt = n // 2, n % 2
                step(V.scalar_tensor_tensor(out=rows_of(pc[:, n * 120:(n + 1) * 120]),
                                            in0=rows_of(ps[:, 4 + odd, qt * 120:(qt + 1) * 120]), scalar=64 ** -0.5,
                                            in1=C("cmp_mask", qt * 15, 15).unsqueeze(1).to_broadcast([P, 8, NCMP]),
                                            op0=ALU.mult, op1=ALU.add))
            sync()
            link(V.tensor_reduce(small[:, 512:544], rows_of(pc), AX, ALU.max))
            V.tensor_tensor(rows_of(pc), rows_of(pc), wide(small[:, 512:544]), ALU.subtract).then_inc(cmp_shifted, 1)
            dve.wait_ge(cmp_exp, 1)
            link(V.tensor_reduce(small[:, 544:576], rows_of(pc), AX, ALU.add))
            link(V.reciprocal(small[:, 544:576], small[:, 544:576]))
            dve.wait_ge(gates_ready, 1)
            for n in range(4):
                odd, qt = n // 2, n % 2
                rows = small[:, 544 + 8 * n:552 + 8 * n]
                step(V.scalar_tensor_tensor(out=rows, in0=rows, scalar=C("cmp_any", qt, 1),
                                            in1=small[:, 64 + qt * 48 + odd * 3:64 + qt * 48 + odd * 3 + 43:6],
                                            op0=ALU.mult, op1=ALU.mult))
            sync()
            V.tensor_tensor(rows_of(pc), rows_of(pc), wide(small[:, 544:576]), ALU.mult).then_inc(cmp_probs, 1)
            dve.wait_ge(dup_ready, 2)
            V.tensor_copy(W(20, 8), banks(0, 4)).then_inc(dup_copied, 1)
            dve.wait_ge(v_turned, 5)
            V.tensor_copy(W(28, 4), banks(6, 2)).then_inc(v_copied, 1)
            dve.wait_ge(cmp_turned, 1)
            for n in range(4):
                ins = V.tensor_copy(r3(Wc(PCT[n // 2], 2048)[0:NCMP, :], 8)[:, :, (n % 2) * P:(n % 2 + 1) * P],
                                    banks(2 * n)[0:NCMP, :].rearrange("p (h t) -> p h t", h=8))
                if n < 3:
                    step(ins)
            ins.then_inc(cmp_ready, 1)
            softmax_dve("nsa", NSA_U, NSA_O, 64 ** -0.5, lambda qt: stage[:, qt * 256:(qt + 1) * 256], lambda g: (2 * g, 2))
            attention_whole(NSA_O + 8)
            proj_add("nsa_out", ALPHA)
            layer_norm(2, 16)
            dve.wait_ge(logits_ps, 1)
            link(V.tensor_copy(small[:, 448:464], ps[:, 0, 0:16]))
            for tt in range(2):
                step(V.max(small[:, 464 + 8 * tt:472 + 8 * tt], small[:, 448 + 8 * tt:456 + 8 * tt]))
            sync()
            for tt in range(2):
                step(V.max_index(idx[:, 8 * tt:8 * tt + 8], small[:, 464 + 8 * tt:472 + 8 * tt], small[:, 448 + 8 * tt:456 + 8 * tt]))
            sync()
            step(V.tensor_copy(small[:, 480:496], idx[:, :]))
            V.tensor_tensor(small[:, 504:506], small[:, 465:474:8], small[:, 464:473:8], ALU.subtract).then_inc(top2_diff, 1)
            sync()
            dve.wait_ge(top2_exp, 1)
            link(V.tensor_scalar(small[:, 506:508], small[:, 504:506], 1.0, None, ALU.add))
            link(V.reciprocal(small[:, 506:508], small[:, 506:508]))
            link(V.tensor_tensor(small[:, 508:510], small[:, 504:506], small[:, 506:508], ALU.mult))
            for tt in range(2):
                link(V.tensor_scalar(small[:, 576 + 8 * tt:584 + 8 * tt], C("iota8"), small[:, 480 + 8 * tt:481 + 8 * tt],
                                     small[:, 506 + tt:507 + tt], ALU.is_equal, ALU.mult))
                link(V.tensor_scalar(small[:, 592 + 8 * tt:600 + 8 * tt], C("iota8"), small[:, 481 + 8 * tt:482 + 8 * tt],
                                     small[:, 508 + tt:509 + tt], ALU.is_equal, ALU.mult))
            link(V.tensor_tensor(small[:, 576:592], small[:, 576:592], small[:, 592:608], ALU.add))
            for tt in range(2):
                ins = V.tensor_tensor(r3(Wc(tt * 1024, 1024), 8), C("ident").unsqueeze(1).to_broadcast([P, 8, P]),
                                      small[:, 576 + 8 * tt:584 + 8 * tt].unsqueeze(2).to_broadcast([P, 8, P]), ALU.mult)
                if tt == 0:
                    step(ins)
            ins.then_inc(cw_diag, 1)
            dve.wait_ge(cw_ps, 1)
            cw = W(16, 8)
            for tt in range(2):
                ins = V.tensor_copy(r3(cw, 8)[:, :, tt * P:(tt + 1) * P], r3(banks(1 + 2 * tt), 8))
                if tt == 0:
                    step(ins)
            ins.then_inc(cw_ready, 1)
            dve.wait_ge(cw_ready, 1)
            gu = PHASES["moe_gu"]
            c0 = chain[0]
            with dve.Fori(0, EXPERTS) as e:
                with dve.Fori(0, 2) as part:
                    half = e * 2 + part

                    def body(i, k, s):
                        bank = (gu.g + k) % DEPTH
                        f = Wc(1536 + 256 * bank, 256)
                        chain[0] = s * 2 + c0 + half * (2 * HALF)
                        dve.wait_ge(gate_act, s + (gu.a + 1) + half * HALF)
                        V.tensor_tensor(f, Wc(512 * bank, BLK), ps[:, bank, BLK:2 * BLK], ALU.mult).then_inc(banks_drained, 1)
                        dve.wait_ge(banks_drained, s + (gu.e + 1) + half * HALF)
                        link(V.tensor_tensor(f, f, work[:, bass.ds(e * BLK + 16 * BLK, BLK)], ALU.mult))
                        split_act(s, f)

                    slot_loop(dve, gu, body)
            chain[0] = c0 + 2 * EXPERTS * 2 * HALF
            dve.wait_ge(acc_ready, 4)
            for c in range(4):
                ins = V.scalar_tensor_tensor(out=xs(c), in0=xs(c), scalar=ALPHA, in1=ps[:, 3 + c, :], op0=ALU.mult, op1=ALU.add)
            ins.then_inc(acc_drained, 1)
            dve.wait_ge(acc_drained, 4)
            layer_norm(3, 24, last=True)


SINK_ORDER = [0, 2, 1, 3, 4, 6, 5, 7]


def _block_slots(m):
    k, n = m.shape
    b = m.reshape(k // P, P, n // P, P).transpose(1, 2, 0, 3)
    return b.reshape(P, n // P // 2, SLOT).transpose(1, 0, 2)


def _gu_slots(m):
    k, n = m.shape
    b = m.reshape(k // P, P, 2, n // P // 2, P).transpose(3, 1, 2, 0, 4)
    return b.reshape(n // P // 2, P, SLOT)


def _down_slots(m):
    k, n = m.shape
    b = m.reshape(k // P // 2, 2, P, n // P, P).transpose(0, 2, 1, 3, 4)
    return b.reshape(k // P // 2, P, SLOT)


def _ffn_slots(gu, down):
    g, d = _gu_slots(gu), _down_slots(down)
    parts = []
    for a in range(0, g.shape[0], HALF):
        b = min(a + HALF, g.shape[0])
        parts += [g[a:b], d[a // 2:b // 2]]
    return parts


def _columns(v):
    return v.reshape(-1, P).T


def _channel_major(a):
    return a.reshape(T, NB, P).transpose(2, 1, 0).reshape(P, NB * T)


def _constants():
    i = np.arange(P)
    freq = (np.float32(10000.0) ** (-np.arange(0, 64, 2, dtype=np.float32) / np.float32(64))).astype(np.float32)
    lane = freq[i % 32][:, None]
    rot = np.zeros((P, P), np.float32)
    first = (i % 64) < 32
    rot[i[first] + 32, i[first]] = -1.0
    rot[i[~first] - 32, i[~first]] = 1.0
    cend = 16 * np.arange(NCMP, dtype=np.float32) + 31
    t = np.arange(T)
    cmp_valid = (16 * np.arange(NCMP)[None] + 31) <= t[:, None]
    c = {
        "ident": np.eye(P), "ones": np.ones((P, P)), "ones64": (i[:, None] // 64 == i[None] // 64), "rot": rot,
        "dup0": i[:, None] == (i[None] % 64), "dup1": i[:, None] == 64 + (i[None] % 64),
        "ge": i[:, None] >= i[None], "invf": lane, "eps6": np.full((P, 1), 1e-6), "eps5": np.full((P, 1), 1e-5),
        "cend_cos": np.cos(lane * cend[None]), "cend_sin": np.sin(lane * cend[None]),
        "cmp_mask": np.where(cmp_valid, 0.0, MASKED).reshape(2, P, NCMP).transpose(1, 0, 2).reshape(P, 30),
        "cmp_any": cmp_valid.any(1).reshape(2, P).T, "iota8": np.broadcast_to(np.arange(8), (P, 8)),
    }
    consts = np.concatenate([np.asarray(c[n], np.float32) for n in CONST], 1)
    q, k = t[:, None], t[None]
    swa = (k <= q) & (k + P > q)
    by_query = lambda m: np.where(m, 0.0, MASKED).reshape(2, P, T).transpose(1, 0, 2).reshape(P, 512)
    attn = np.concatenate([by_query(swa), by_query(k > q)], 1)
    levels = [np.eye(P)]
    for lv in range(1, HG_LEVELS + 1):
        half = P >> lv
        s_, t_ = i[:, None], i[None]
        levels.append((s_ // (2 * half) == t_ // (2 * half)) & (s_ % (2 * half) < half) & (t_ % (2 * half) >= half))
    pool = np.concatenate([np.broadcast_to(1.0 / np.minimum(t + 1, w), (P, T)) for w in (2, 4, 8, 16)], 1)
    ang = lane * t[None].astype(np.float32)
    nsa = np.concatenate([by_query(k <= q), np.cos(ang), np.sin(ang)], 1)
    stages = [attn, np.concatenate(levels, 1), pool, nsa]
    return consts, np.stack([np.asarray(s, np.float32) for s in stages])


def _stream(v):
    parts = [_block_slots(v["ab_w_in"][0]), _block_slots(v["ab_w_out"][0])]
    for layer in range(2):
        if layer == 1:
            parts += [_block_slots(v["hgrn_w_in"][0]), _block_slots(v["hgrn_w_out"][0])]
        parts += [_block_slots(v["xa_w_kv"][layer]), _block_slots(v["xa_w_q"][layer]), _block_slots(v["xa_w_o"][layer])]
        parts += _ffn_slots(v["ffn_w_up"][layer], v["ffn_w_down"][layer])
    parts += [v["pool_w_2"][0].reshape(4, 2, P, 2, P).transpose(2, 0, 3, 1, 4).reshape(1, P, SLOT)]
    parts += _ffn_slots(v["ffn_w_gu_2"][0], v["ffn_w_down_2"][0])
    parts += [_block_slots(v["nsa_w_in_2"][0][:, :20 * P]), _block_slots(v["nsa_w_out_2"][0])]
    for e in range(EXPERTS):
        parts += _ffn_slots(v["moe_w_gu_2"][0, e], v["moe_w_down_2"][0, e])
    parts += [np.zeros((DEPTH, P, SLOT), np.float32)]
    return np.concatenate(parts)


def kernel(**inputs):
    import concourse.bacc as bacc
    from concourse.bass_utils import run_bass_kernel_spmd

    v = {k: np.asarray(a) for k, a in inputs.items()}
    stream = _stream(v)
    twice = lambda a: np.concatenate([a, a], -1)
    p = {
        "norm_mix": _columns(v["norm_mix"]), "norm_cross": _columns(v["norm_cross"]), "norm_mem": _columns(v["norm_mem"]),
        "norm_ffn": _columns(v["norm_ffn"]), "swa_q": _columns(twice(v["swa_q_norm"][0])), "swa_k": _columns(twice(v["swa_k_norm"][0])),
        "sinks": np.broadcast_to(v["swa_sinks"][0][SINK_ORDER], (P, 8)), "o_norm": _columns(v["hgrn_o_norm"][0]), "lb": _columns(v["hgrn_lb"]),
        "xa_q": _columns(v["xa_q_norm"]), "xa_k": _columns(v["xa_k_norm"]), "conv_w": _columns(v["ffn_conv_w"]),
        "conv_b": _columns(v["ffn_conv_b"]), "ln_g": _columns(v["ln_g_2"]), "ln_b": _columns(v["ln_b_2"]),
        "pool_scale": _columns(v["pool_scale_2"][0]),
        "router": v["moe_router_2"][0].reshape(NB, P, 8).transpose(1, 0, 2).reshape(P, 64),
        "pe_k": _columns(v["nsa_pe_k_2"][0]), "pe_v": _columns(v["nsa_pe_v_2"][0]),
        "w2_k": twice(v["nsa_w2_k_2"][0]), "w2_v": v["nsa_w2_v_2"][0],
    }
    params = np.concatenate([p[n] for n in PARAM], 1)
    w1 = [v[n][0].reshape(16, P, P).transpose(1, 0, 2).reshape(P, 2048) for n in ("nsa_w1_k_2", "nsa_w1_v_2")]
    gates = v["nsa_w_in_2"][0][:, 20 * P:].reshape(NB, P, 48).transpose(1, 0, 2).reshape(P, 384)
    consts, stages = _constants()
    arrays = {
        "stream": stream, "x_in": _channel_major(v["x"][0]), "mem_in": _channel_major(v["mem"][0]),
        "pos_in": np.broadcast_to(v["positions"][0], (P, T)), "params": params, "consts": consts, "stage_consts": stages,
        "w1_in": np.concatenate(w1 + [gates], 1),
    }
    arrays = {k: np.ascontiguousarray(a) for k, a in arrays.items()}
    nc = bacc.Bacc("TRN2", target_bir_lowering=False, num_devices=1)
    args = [nc.dram_tensor(k, a.shape, mybir.dt.from_np(a.dtype), kind="ExternalInput").ap() for k, a in arrays.items()]
    out = nc.dram_tensor("out", (P, NB * T), F32, kind="ExternalOutput").ap()
    build(nc, *args, out)
    r = run_bass_kernel_spmd(nc, [arrays], core_ids=[0])
    got = r.results[0]["out"]
    return got.reshape(P, NB, T).transpose(2, 1, 0).reshape(1, T, D)
```

```python
from contextlib import ExitStack

import concourse.bass as bass
import numpy as np
from concourse import mybir

F32 = mybir.dt.float32
F32R = mybir.dt.float32r
I32 = mybir.dt.int32
U32 = mybir.dt.uint32
ALU = mybir.AluOpType
ACT = mybir.ActivationFunctionType
AX = mybir.AxisListType.X

P = 128
T = 256
D = 1024
NB = D // P
BLK = T
SLOT = 16 * P
QUARTERS = 4
DEPTH = 3
FF = 22
MOE_FF = 28
EXPERTS = 8
HALF = MOE_FF // 2
ALPHA = 4.0 ** 0.25
NCMP = 15
MASKED = -1.0e30
HG_LEVELS = 7
ROUND = 1.5 * 2.0 ** 23
_C1 = 6.28125
_C2 = round((2.0 * np.pi - _C1) * 2.0 ** 20) / 2.0 ** 20
TWO_PI = (_C1, _C2, 2.0 * np.pi - _C1 - _C2)
PI = 3.1415925


class Phase:

    def __init__(self, name, kind, n, g, e, a):
        self.name, self.kind, self.n, self.g, self.e, self.a = name, kind, n, g, e, a


def plan():
    phases, g, e, a = {}, 0, 0, 0
    ffn = [("gu", HALF), ("down", HALF // 2), ("gu", FF - HALF), ("down", (FF - HALF) // 2)]
    order = [("ab_in", "proj", 9), ("ab_out", "proj", 4)]
    for layer in range(2):
        if layer == 1:
            order += [("hg_in", "proj", 16), ("hg_out", "proj", 4)]
        order += [(f"kv{layer}", "proj", 8), (f"q{layer}", "proj", 4), (f"o{layer}", "proj", 4)]
        order += [(f"ffn{layer}_{i}", k, n) for i, (k, n) in enumerate(ffn)]
    order += [("pool", "pool", 1)]
    order += [(f"ffn2_{i}", k, n) for i, (k, n) in enumerate(ffn)]
    order += [("nsa_in", "proj", 10), ("nsa_out", "proj", 4)]
    order += [("moe_gu", "gu", HALF), ("moe_down", "down", HALF // 2)]
    for name, kind, n in order:
        phases[name] = Phase(name, kind, n, g, e, a)
        g += n
        if kind != "down":
            e += n
        if kind == "gu":
            a += n
    per_half = HALF + HALF // 2
    total = phases["moe_gu"].g + 2 * EXPERTS * per_half
    return phases, per_half, total


PHASES, PER_HALF, SLOTS = plan()
STREAM = SLOTS + DEPTH

CONST = {}
_at = 0
for _name, _n in [("ident", 128), ("ones", 128), ("ones64", 128), ("rot", 128), ("dup0", 128), ("dup1", 128),
                  ("ge", 128), ("invf", 1), ("eps6", 1), ("eps5", 1), ("cend_cos", 15), ("cend_sin", 15), ("cmp_mask", 30),
                  ("cmp_any", 2), ("iota8", 8), ("places", 128)]:
    CONST[_name] = (_at, _n)
    _at += _n
N_CONST = _at
STAGE = {"attn": 0, "hgrn": 1, "pool": 2, "nsa": 3}
PARAM = {}
_at = 0
for _name, _n in [("norm_mix", 16), ("norm_cross", 16), ("norm_mem", 16), ("norm_ffn", 16), ("swa_q", 1),
                  ("swa_k", 1), ("sinks", 8), ("o_norm", 1), ("lb", 16), ("xa_q", 4), ("xa_k", 4),
                  ("conv_w", 264), ("conv_b", 88), ("ln_g", 32), ("ln_b", 32), ("pool_scale", 8),
                  ("router", 64), ("pe_k", 16), ("pe_v", 16), ("w2_k", 128), ("w2_v", 64)]:
    PARAM[_name] = (_at, _n)
    _at += _n
N_PARAM = _at


def build(nc, stream, x_in, mem_in, pos_in, params, consts, stage_consts, w1_in, out):
    ctx = ExitStack()
    with ctx:
        def sb(name, cols, dt=F32):
            return ctx.enter_context(nc.sbuf_tensor(name, [P, cols], dt))

        def sem(name):
            return ctx.enter_context(nc.semaphore(name))

        raw = [sb(f"raw{i}", SLOT) for i in range(DEPTH)]
        whi = [sb(f"whi{i}", SLOT, F32R) for i in range(DEPTH)]
        wlo = [sb(f"wlo{i}", SLOT, F32R) for i in range(DEPTH)]
        x = sb("x", NB * BLK)
        hh = sb("hh", NB * BLK, F32R)
        hl = sb("hl", NB * BLK, F32R)
        ahi = sb("ahi", HALF * BLK, F32R)
        alo = sb("alo", HALF * BLK, F32R)
        hf = sb("hf", NB * BLK)
        rstd = sb("rstd", BLK)
        const = sb("const", N_CONST)
        par = sb("par", N_PARAM)
        stage = sb("stage", 1024)
        zero = sb("zero", P, F32R)
        small = sb("small", 640)
        idx = sb("idx", 16, U32)
        few = sb("few", 1, I32)
        work = sb("work", 60 * BLK)
        ps = ctx.enter_context(nc.psum_tensor("ps", [P, 8, 512], F32))

        def C(name, a=0, n=None):
            at, size = CONST[name]
            return const[:, at + a:at + (size if n is None else a + n)]

        def R(name, a=0, n=1):
            return par[:, PARAM[name][0] + a:PARAM[name][0] + a + n]

        def W(block, n=1):
            return work[:, block * BLK:(block + n) * BLK]

        def Wc(col, n):
            return work[:, col:col + n]

        def xb(b, n=1):
            return x[:, b * BLK:(b + n) * BLK]

        def banks(b, n=2):
            return ps[:, b:b + n, :].rearrange("p b c -> p (b c)")

        def r3(ap, b):
            return ap.rearrange("p (b c) -> p b c", b=b)

        raw_loaded = [sem(f"raw_loaded{i}") for i in range(DEPTH)]
        hi_ready = sem("hi_ready")
        lo_ready = sem("lo_ready")
        slot_used = sem("slot_used")
        banks_drained = sem("banks_drained")
        gate_act = sem("gate_act")
        act_ready = sem("act_ready")
        acc_ready = sem("acc_ready")
        acc_drained = sem("acc_drained")
        dve_step = sem("dve_step")
        act_step = sem("act_step")
        last_step = sem("last_step")
        params_loaded = sem("params_loaded")
        x_loaded = sem("x_loaded")
        positions_loaded = sem("positions_loaded")
        stage_loaded = sem("stage_loaded")
        mem_loaded = sem("mem_loaded")
        w1_loaded = sem("w1_loaded")
        angles_ready = sem("angles_ready")
        sines_ready = sem("sines_ready")
        zero_ready = sem("zero_ready")
        out_stored = sem("out_stored")
        squares_ready = sem("squares_ready")
        sums_ready = sem("sums_ready")
        rstd_ready = sem("rstd_ready")
        mean_ready = sem("mean_ready")
        x_ready = sem("x_ready")
        h_ready = sem("h_ready")
        head_sq = sem("head_sq")
        head_sums = sem("head_sums")
        head_rstd = sem("head_rstd")
        rope_in = sem("rope_in")
        rope_rot = sem("rope_rot")
        heads_ready = sem("heads_ready")
        dup_ready = sem("dup_ready")
        dup_copied = sem("dup_copied")
        v_turned = sem("v_turned")
        v_copied = sem("v_copied")
        scores_ready = sem("scores_ready")
        scores_masked = sem("scores_masked")
        negmax_ready = sem("negmax_ready")
        exp_done = sem("exp_done")
        probs_ready = sem("probs_ready")
        pt_ready = sem("pt_ready")
        pt_copied = sem("pt_copied")
        pv_done = sem("pv_done")
        o_drained = sem("o_drained")
        z_ready = sem("z_ready")
        z_masked = sem("z_masked")
        soft_ready = sem("soft_ready")
        sp_ready = sem("sp_ready")
        cs_ready = sem("cs_ready")
        d_ready = sem("d_ready")
        a_ready = sem("a_ready")
        sb_pv_done = sem("sb_pv_done")
        hg_lb = sem("hg_lb")
        hg_lb_exp = sem("hg_lb_exp")
        hg_sig = sem("hg_sig")
        hg_kf = sem("hg_kf")
        hg_log = sem("hg_log")
        hg_d = sem("hg_d")
        hg_e = sem("hg_e")
        hg_x = sem("hg_x")
        hg_s = sem("hg_s")
        hg_a = sem("hg_a")
        hg_o = sem("hg_o")
        hg_osq = sem("hg_osq")
        hg_osum = sem("hg_osum")
        hg_orstd = sem("hg_orstd")
        gates_ps = sem("gates_ps")
        gates_ready = sem("gates_ready")
        cmp_dup = sem("cmp_dup")
        cmp_cols = sem("cmp_cols")
        cmp_hidden = sem("cmp_hidden")
        cmp_bias = sem("cmp_bias")
        cmp_silu = sem("cmp_silu")
        cmp_kv = sem("cmp_kv")
        cmp_kv_copied = sem("cmp_kv_copied")
        cmp_rot = sem("cmp_rot")
        cmp_roped = sem("cmp_roped")
        cmp_scores = sem("cmp_scores")
        cmp_shifted = sem("cmp_shifted")
        cmp_exp = sem("cmp_exp")
        cmp_probs = sem("cmp_probs")
        cmp_turned = sem("cmp_turned")
        cmp_ready = sem("cmp_ready")
        logits_ps = sem("logits_ps")
        top2_diff = sem("top2_diff")
        top2_exp = sem("top2_exp")
        cw_diag = sem("cw_diag")
        cw_ps = sem("cw_ps")
        cw_ready = sem("cw_ready")

        picked = sem("picked")
        counts_ps = sem("counts_ps")
        few_ready = sem("few_ready")
        x_turned = sem("x_turned")
        x_tokens = sem("x_tokens")
        places_built = sem("places_built")
        spread_ps = sem("spread_ps")
        spread_ready = sem("spread_ready")
        gathered_ps = sem("gathered_ps")
        gathered = sem("gathered")
        y_ready = sem("y_ready")
        y_kept = sem("y_kept")
        spread_out = sem("spread_out")
        y_added = sem("y_added")

        block = ctx.enter_context(nc.Block())

        def few_act(n):
            return Wc(n * P, P)

        FEW_X = Wc(2048, 1024)
        FEW_Y = Wc(3072, 1024)
        FEW_TAKE = 24 * BLK
        FEW_WEIGHT = Wc(32 * BLK, 2048)
        FEW_GIVE = 40 * BLK
        FEW_TOK = Wc(48 * BLK, 2048)
        FEW_GATE = 56 * BLK

        SWA_U, XA_U, NSA_U = 0, (4, 6), 8
        SWA_O, SB_O, XA_O, NSA_O = 0, 4, (8, 10), 12
        PROBS = [Wc(10752, 1024), Wc(11776, 1024), hf[:, 0:1024]]
        MEAN_BANK = (4, 0, 3, 0)
        STATS = (0, 32, 576)
        PT = [Wc(12800 + 1024 * i, 1024) for i in range(2)]
        ROPED = (0, 2, 4, 6, 12, 16)
        PCT = (2048, 8192)
        HG_D = [W(16, 8), hf[:, :]]
        SB_T = [Wc(4608 + 1024 * i, 1024) for i in range(2)]

        def place(kind, h):
            return h if kind == "xa" else (h % 2) * 2 + h // 2

        def key_tiles(kind, qt):
            return 1 if kind != "xa" and qt == 0 else 2

        def units(kind):
            if kind == "swa":
                return [(g, qt, 0) for g in range(2) for qt in range(2)]
            if kind == "nsa":
                return [(g, qt, br) for g in range(4) for qt in range(2) for br in range(2)]
            return [(0, qt, 0) for qt in range(2)]

        def slot_loop(eng, ph, body, n=None, peel=0):
            n = ph.n if n is None else n
            rounds = n // DEPTH
            for i in range(min(peel, rounds)):
                for k in range(DEPTH):
                    body(i, k, DEPTH * i + k)
            if rounds - peel > 1:
                with eng.Fori(peel, rounds) as i:
                    for k in range(DEPTH):
                        body(i, k, i * DEPTH + k)
            elif rounds - peel == 1:
                for k in range(DEPTH):
                    body(peel, k, DEPTH * peel + k)
            for s in range(DEPTH * rounds, n):
                body(rounds, s - DEPTH * rounds, s)

        def at_least(eng, s, value):
            if not (isinstance(value, int) and value <= 0):
                eng.wait_ge(s, value)

        def few_flag(eng):
            eng.wait_ge(few_ready, 1)
            return eng.value_load(few[0:1, 0:1]) > 0

        @block.sync
        def _(sp):
            sp.dma_start(x[:, :], x_in).then_inc(x_loaded, 16)
            sp.dma_start(const[:, :], consts).then_inc(params_loaded, 16)
            sp.dma_start(par[:, :], params).then_inc(params_loaded, 16)
            sp.dma_start(Wc(10752, 256).bitcast(I32), pos_in).then_inc(positions_loaded, 16)
            for k in range(DEPTH):
                sp.dma_start(raw[k][:, :], stream[k]).then_inc(raw_loaded[k], 16)

            def load(i, k, s):
                sp.wait_ge(lo_ready, s + 1)
                sp.dma_start(raw[k][:, :], stream[s + DEPTH]).then_inc(raw_loaded[k], 16)

            first = PHASES["moe_gu"].g
            slot_loop(sp, None, load, n=first)
            with sp.If(few_flag(sp)):
                sp.wait_ge(lo_ready, first + DEPTH)

                def load_few(i, k, s):
                    p = (first + k) % DEPTH
                    sp.wait_ge(slot_used, s + (first + 1))
                    sp.dma_start(raw[p][:, :], stream[s + (first + DEPTH)]).then_inc(raw_loaded[p], 16)

                slot_loop(sp, None, load_few, n=SLOTS - DEPTH - first)
            with sp.Else():
                def load_all(i, k, s):
                    p = (first + k) % DEPTH
                    sp.wait_ge(lo_ready, s + (first + 1))
                    sp.dma_start(raw[p][:, :], stream[s + (first + DEPTH)]).then_inc(raw_loaded[p], 16)

                slot_loop(sp, None, load_all, n=SLOTS - first)
            sp.wait_ge(x_ready, 4)
            sp.dma_start(out, x[:, :]).then_inc(out_stored, 16)
            sp.wait_ge(out_stored, 16)

        @block.gpsimd
        def _(pool):
            def split_lo(k, s, first):
                p = (first + k) % DEPTH
                pool.wait_ge(hi_ready, s + (first + 1))
                nc.gpsimd.tensor_tensor(wlo[p][:, :], raw[p][:, :], whi[p][:, :].bitcast(F32),
                                        ALU.subtract).then_inc(lo_ready, 1)

            first = PHASES["moe_gu"].g + DEPTH
            slot_loop(pool, None, lambda i, k, s: split_lo(k, s, 0), n=first)
            with pool.If(few_flag(pool)):
                pass
            with pool.Else():
                slot_loop(pool, None, lambda i, k, s: split_lo(k, s, first), n=STREAM - first)

        @block.scalar
        def _(act):
            chain = [0]

            def link(ins):
                chain[0] += 1
                ins.then_inc(act_step, 1)
                act.wait_ge(act_step, chain[0])

            def split_hi(ph, i, k, s, off=0):
                p = (ph.g + k) % DEPTH
                act.wait_ge(raw_loaded[p], i * 16 + (16 * ((ph.g + k) // DEPTH + 2) + off * 16))
                act.wait_ge(slot_used, s + (ph.g + 1) + off * DEPTH)
                nc.scalar.activation(whi[p][:, :], raw[p][:, :], ACT.Copy).then_inc(hi_ready, 1)

            def split_phase(name, then=None):
                ph = PHASES[name]

                def body(i, k, s):
                    split_hi(ph, i, k, s)
                    if then is not None and s == 1:
                        then()

                slot_loop(act, ph, body, peel=0 if then is None else 1)

            def norm_act(n, count, eps):
                act.wait_ge(sums_ready, n + 1)
                link(nc.scalar.activation(rstd[:, :], ps[:, 7, 0:BLK], ACT.Ln, scale=1.0 / count, bias=eps_ap(eps)))
                nc.scalar.activation(rstd[:, :], rstd[:, :], ACT.Exp, scale=-0.5).then_inc(rstd_ready, 1)

            def eps_ap(eps):
                return C("eps6") if eps == 1e-6 else C("eps5")

            def softmax_act(kind, u0):
                us = units(kind)
                for step in range(len(us) + 2):
                    if step < len(us):
                        u = u0 + step
                        act.wait_ge(negmax_ready, u + 1)
                        probs, s0, nk = PROBS[u % 3], STATS[u % 3], P * key_tiles(kind, us[step][1])
                        if kind == "swa":
                            nc.scalar.activation(small[:, s0 + 12:s0 + 16], small[:, s0 + 8:s0 + 12], ACT.Exp)
                        for h in range(4):
                            ins = nc.scalar.activation(probs[:, h * 256:h * 256 + nk], probs[:, h * 256:h * 256 + nk],
                                                       ACT.Exp, bias=small[:, s0 + h:s0 + h + 1],
                                                       accum_out=small[:, s0 + 4 + h:s0 + 5 + h])
                        ins.then_inc(exp_done, 1)
                    if step >= 2:
                        u = u0 + step - 2
                        nk = P * key_tiles(kind, us[step - 2][1])
                        act.wait_ge(pt_ready, u + 1)
                        at_least(act, pv_done, u - 1)
                        nc.scalar.activation(r3(PT[u % 2], 4)[:, :, 0:nk], r3(banks(2), 4)[:, :, 0:nk], ACT.Copy).then_inc(pt_copied, 1)

            def ffn_act(layer, conv):
                for i in range(4):
                    ph = PHASES[f"ffn{layer}_{i}"]
                    if ph.kind == "down":
                        split_phase(ph.name)
                        continue

                    def body(i, k, s, ph=ph):
                        if conv:
                            gate = Wc(512 * ((ph.g + k) % DEPTH), BLK)
                            act.wait_ge(banks_drained, s + (ph.e + 1))
                            nc.scalar.activation(gate, gate, ACT.Silu).then_inc(gate_act, 1)
                        else:
                            silu_gate(ph, k, s)
                        split_hi(ph, i, k, s)

                    slot_loop(act, ph, body)

            def silu_gate(ph, k, s, off_g=0, off_a=0):
                bank = (ph.g + k) % DEPTH
                act.wait_ge(slot_used, s + (ph.g + 1) + off_g)
                act.wait_ge(act_ready, s + (ph.a - 2) + off_a)
                nc.scalar.activation(Wc(512 * bank, BLK), ps[:, bank, 0:BLK], ACT.Silu).then_inc(gate_act, 1)

            def xa_act(layer, before):
                act.wait_ge(h_ready, QUARTERS * (2 + 6 * layer))
                act.dma_start(W(24, 8), mem_in).then_inc(mem_loaded, 16)
                split_phase(before, lambda: norm_act(layer * 4 + 1, D, 1e-6))
                split_phase(f"kv{layer}", lambda: norm_act(layer * 4 + 2, D, 1e-6))
                split_phase(f"q{layer}")
                act.wait_ge(head_sums, 2 + layer)
                link(nc.scalar.activation(W(42, 8), banks(0, 4), ACT.Ln, scale=1.0 / 256, bias=C("eps6")))
                nc.scalar.activation(W(42, 8), W(42, 8), ACT.Exp, scale=-0.5).then_inc(head_rstd, 1)
                softmax_act("xa", XA_U[layer])
                split_phase(f"o{layer}")

            for k in range(DEPTH):
                act.wait_ge(raw_loaded[k], 16)
                nc.scalar.activation(whi[k][:, :], raw[k][:, :], ACT.Copy).then_inc(hi_ready, 1)
            act.dma_start(stage[:, :], stage_consts[STAGE["attn"]]).then_inc(stage_loaded, 16)
            act.wait_ge(angles_ready, 1)
            nc.scalar.activation(W(33, 2), W(33, 2), ACT.Sin).then_inc(sines_ready, 1)
            norm_act(0, D, 1e-6)
            split_phase("ab_in")
            act.wait_ge(head_sums, 1)
            link(nc.scalar.activation(W(23, 5), banks(0, 3)[:, 0:5 * BLK], ACT.Ln, scale=1.0 / 64, bias=C("eps6")))
            nc.scalar.activation(W(23, 5), W(23, 5), ACT.Exp, scale=-0.5).then_inc(head_rstd, 1)
            softmax_act("swa", SWA_U)
            for st in range(5):
                if st < 4:
                    u = st
                    act.wait_ge(z_masked, u + 1)
                    link(nc.scalar.activation(SB_T[u % 2], PROBS[u % 3], ACT.Abs))
                    link(nc.scalar.activation(SB_T[u % 2], SB_T[u % 2], ACT.Exp, scale=-1.0))
                    nc.scalar.activation(SB_T[u % 2], SB_T[u % 2], ACT.Ln, bias=1.0).then_inc(soft_ready, 1)
                if st >= 1:
                    u = st - 1
                    act.wait_ge(d_ready, u + 1)
                    at_least(act, sb_pv_done, u - 1)
                    nc.scalar.activation(PT[u % 2], PROBS[u % 3], ACT.Exp).then_inc(a_ready, 1)
            xa_act(0, "ab_out")
            norm_act(3, D, 1e-6)
            ffn_act(0, True)
            act.dma_start(stage[:, :], stage_consts[STAGE["hgrn"]]).then_inc(stage_loaded, 16)
            norm_act(4, D, 1e-6)
            act.wait_ge(hg_lb, 1)
            nc.scalar.activation(small[:, 416:432], small[:, 400:416], ACT.Exp).then_inc(hg_lb_exp, 1)
            split_phase("hg_in")
            act.wait_ge(banks_drained, PHASES["hg_in"].e + PHASES["hg_in"].n)
            nc.scalar.activation(W(32, 8), W(8, 8), ACT.Sigmoid, scale=-1.0)
            nc.scalar.activation(W(8, 8), W(8, 8), ACT.Sigmoid).then_inc(hg_sig, 1)
            nc.scalar.activation(W(24, 8), W(24, 8), ACT.Silu)
            act.wait_ge(hg_kf, 1)
            nc.scalar.activation(W(8, 8), W(8, 8), ACT.Ln).then_inc(hg_log, 1)
            for lv in range(HG_LEVELS + 1):
                act.wait_ge(hg_d, lv + 1)
                if lv:
                    link(nc.scalar.activation(HG_D[lv % 2], HG_D[lv % 2], ACT.Abs))
                nc.scalar.activation(HG_D[lv % 2], HG_D[lv % 2], ACT.Exp, scale=-1.0 if lv else 1.0).then_inc(hg_e, 1)
            act.wait_ge(hg_osum, 1)
            link(nc.scalar.activation(W(8, 8), banks(4, 4), ACT.Ln, scale=1.0 / 128, bias=C("eps6")))
            nc.scalar.activation(W(8, 8), W(8, 8), ACT.Exp, scale=-0.5).then_inc(hg_orstd, 1)
            act.dma_start(stage[:, :], stage_consts[STAGE["pool"]]).then_inc(stage_loaded, 16)
            xa_act(1, "hg_out")
            norm_act(7, D, 1e-6)
            ffn_act(1, True)
            split_phase("pool")
            norm_act(8, D, 1e-5)
            act.dma_start(stage[:, :], stage_consts[STAGE["nsa"]]).then_inc(stage_loaded, 16)
            act.dma_start(Wc(8192, 4480), w1_in).then_inc(w1_loaded, 16)
            ffn_act(2, False)
            norm_act(9, D, 1e-5)
            split_phase("nsa_in")
            act.wait_ge(gates_ps, 1)
            nc.scalar.activation(small[:, 64:160], ps[:, 7, 0:96], ACT.Sigmoid).then_inc(gates_ready, 1)
            act.wait_ge(cmp_bias, 1)
            for br in range(2):
                ins = nc.scalar.activation(small[:, 160 + 60 * br:220 + 60 * br], ps[:, 6, 64 * br:64 * br + 60],
                                           ACT.Silu, bias=small[:, 280 + br:281 + br])
            ins.then_inc(cmp_silu, 1)
            act.wait_ge(cmp_shifted, 1)
            nc.scalar.activation(Wc(10240, 480), Wc(10240, 480), ACT.Exp).then_inc(cmp_exp, 1)
            softmax_act("nsa", NSA_U)
            split_phase("nsa_out")
            norm_act(10, D, 1e-5)
            act.wait_ge(top2_diff, 1)
            nc.scalar.activation(small[:, 504:506], small[:, 504:506], ACT.Exp).then_inc(top2_exp, 1)
            gu, down = PHASES["moe_gu"], PHASES["moe_down"]
            act.wait_ge(x_turned, 1)
            nc.scalar.activation(FEW_TOK, banks(3, 4), ACT.Copy).then_inc(x_tokens, 1)

            def few_half(half):
                def body(i, k, s):
                    bank = (gu.g + k) % DEPTH
                    act.wait_ge(slot_used, s + (gu.g + 1) + half * PER_HALF)
                    act.wait_ge(act_ready, s + (gu.a - 2) + half * HALF)
                    nc.scalar.activation(Wc(FEW_GATE + P * bank, P), ps[:, bank, 0:P], ACT.Silu).then_inc(gate_act, 1)

                slot_loop(act, gu, body)

            with act.If(few_flag(act)):
                act.wait_ge(spread_ps, 1)
                nc.scalar.activation(work[:, FEW_GIVE:FEW_GIVE + 2048], banks(4, 4), ACT.Copy).then_inc(spread_ready, 1)
                with act.Fori(0, 2 * EXPERTS) as half:
                    few_half(half)
            with act.Else():
                with act.Fori(0, EXPERTS) as e:
                    with act.Fori(0, 2) as part:
                        half = e * 2 + part
                        rounds = half * (PER_HALF // DEPTH)

                        def body(i, k, s):
                            silu_gate(gu, k, s, half * PER_HALF, half * HALF)
                            split_hi(gu, i, k, s, rounds)

                        slot_loop(act, gu, body)
                        slot_loop(act, down, lambda i, k, s: split_hi(down, i, k, s, rounds))
            norm_act(11, D, 1e-5)

        @block.tensor
        def _(pe):
            mm = nc.tensor.matmul

            def split_mm(out_ap, hi_w, lo_w, hi_x, lo_x, start, stop, **kw):
                mm(out_ap, hi_w, hi_x, start=start, stop=False, **kw)
                mm(out_ap, hi_w, lo_x, start=False, stop=False, **kw)
                return mm(out_ap, lo_w, hi_x, start=False, stop=stop, **kw)

            def proj_slot(ph, k, s, off_g=0, off_e=0, h=None):
                p = (ph.g + k) % DEPTH
                pe.wait_ge(lo_ready, s + (ph.g + 1) + off_g)
                at_least(pe, banks_drained, s + (ph.e - 2) + off_e)
                for b in range(2):
                    for c in range(NB):
                        if h is not None and isinstance(s, int) and s == 0 and b == 0 and c % 2 == 0:
                            pe.wait_ge(h_ready, QUARTERS * (h - 1) + c // 2 + 1)
                        w = slice((b * NB + c) * P, (b * NB + c + 1) * P)
                        m = slice(c * BLK, (c + 1) * BLK)
                        last = split_mm(ps[:, p, b * BLK:(b + 1) * BLK], whi[p][:, w], wlo[p][:, w],
                                        hh[:, m], hl[:, m], c == 0, c == NB - 1)
                last.then_inc(slot_used, 1)

            def proj_pe(name, h, then=None):
                ph = PHASES[name]

                def body(i, k, s):
                    proj_slot(ph, k, s, h=h)
                    if then is not None and isinstance(s, int) and s == 1:
                        then()

                slot_loop(pe, ph, body, peel=1)

            def down_slot(ph, k, s, act_at, off_g=0):
                p = (ph.g + k) % DEPTH
                pe.wait_ge(lo_ready, s + (ph.g + 1) + off_g)
                for c in range(2):
                    m = bass.ds(s * (2 * BLK) + c * BLK, BLK)
                    if isinstance(s, int):
                        m = slice((2 * s + c) * BLK, (2 * s + c + 1) * BLK)
                    pe.wait_ge(act_ready, act_at(s, c))
                    for b in range(NB):
                        w = slice((c * NB + b) * P, (c * NB + b + 1) * P)
                        last = split_mm(ps[:, 3 + b // 2, (b % 2) * BLK:(b % 2 + 1) * BLK], whi[p][:, w],
                                        wlo[p][:, w], ahi[:, m], alo[:, m], False, False, skip_group_check=True)
                last.then_inc(slot_used, 1)

            def acc_zero(start, stop):
                for b in range(4):
                    last = mm(ps[:, 3 + b, :], zero[:, :], zero[:, :].unsqueeze(1).to_broadcast([P, 4, P]), start=start, stop=stop,
                              skip_group_check=True)
                return last

            def sums_pe(src, bank, wait):
                for b in range(NB):
                    if b % 2 == 0:
                        wait(b // 2)
                    last = mm(ps[:, bank, 0:BLK], C("ones"), src[:, b * BLK:(b + 1) * BLK], start=(b == 0), stop=(b == NB - 1))
                return last

            def norm_pe(n):
                sums_pe(hf, 7, lambda c: pe.wait_ge(squares_ready, QUARTERS * n + c + 1)).then_inc(sums_ready, 1)

            def layer_norm_pe(i, added, count):
                sums_pe(x, MEAN_BANK[i], lambda c: pe.wait_ge(added, count(c))).then_inc(mean_ready, 1)
                norm_pe(8 + i)

            def ffn_pe(layer, h):
                at_least(pe, acc_drained, QUARTERS * layer)
                for i in range(4):
                    ph = PHASES[f"ffn{layer}_{i}"]
                    if ph.kind == "gu":
                        slot_loop(pe, ph, lambda i, k, s: proj_slot(ph, k, s, h=h), peel=1 if i == 0 else 0)
                        a0 = ph.a
                    else:
                        if i == 1:
                            acc_zero(True, False)
                        slot_loop(pe, ph, lambda i, k, s: down_slot(ph, k, s, lambda s, c: s * 2 + (a0 + c + 1)))
                acc_zero(False, True).then_inc(acc_ready, 1)

            def turn(dst, src):
                return nc.tensor.transpose(dst, src, C("ident"))

            def softmax_pe(kind, u0, o0, q_at, k_at, v_at, cmp=None):
                us = units(kind)
                branches = 2 if kind == "nsa" else 1
                for step in range(len(us) + 3):
                    if step < len(us):
                        u = u0 + step
                        g, qt, br = us[step]
                        nk = P * key_tiles(kind, qt)
                        at_least(pe, scores_masked, u)
                        for h in range(4):
                            for last_c, (q, kk) in zip((False, True) if kind == "xa" else (True,), zip(q_at(g, h, qt), k_at(g, h, br))):
                                at = place(kind, h)
                                last = mm(ps[:, at // 2, (at % 2) * 256:(at % 2) * 256 + nk], q, kk[:, 0:nk],
                                          start=(not last_c or kind != "xa"), stop=last_c)
                        last.then_inc(scores_ready, 1)
                    if 2 <= step <= len(us) + 1:
                        u = u0 + step - 2
                        pe.wait_ge(probs_ready, u + 1)
                        at_least(pe, pt_copied, u)
                        for h in range(4):
                            for kt in range(key_tiles(kind, us[step - 2][1])):
                                n = h * 2 + kt
                                last = turn(ps[:, 2 + n // 4, (n % 4) * P:(n % 4 + 1) * P],
                                            PROBS[u % 3][:, h * 256 + kt * P:h * 256 + (kt + 1) * P])
                        last.then_inc(pt_ready, 1)
                    if step >= 3:
                        u = u0 + step - 3
                        g, qt, br = us[step - 3]
                        o = o0 + (step - 3) // branches
                        kts = key_tiles(kind, qt)
                        pe.wait_ge(pt_copied, u + 1)
                        if br == 0:
                            at_least(pe, o_drained, o - 1)
                        bank = 4 + 2 * (o % 2)
                        pt = PT[u % 2]
                        for h in range(4):
                            at = 2 * place(kind, h)
                            if kind == "xa":
                                for eb in range(2):
                                    n = 2 * h + eb
                                    for kt in range(2):
                                        last = mm(ps[:, bank + n // 4, (n % 4) * P:(n % 4 + 1) * P], v_at(g, h, kt, eb),
                                                  pt[:, (at + kt) * P:(at + kt + 1) * P], start=(kt == 0), stop=(kt == 1))
                                continue
                            half = 64 * (h % 2)
                            dst = ps[half:half + 64, bank, (h // 2) * P:(h // 2 + 1) * P]
                            fresh = h < 2
                            if cmp is not None and br == 0:
                                vc, pc = cmp(g, h, qt)
                                mm(dst, vc, pc, start=fresh, stop=False, skip_group_check=True)
                                fresh = False
                            for kt in range(kts):
                                last = mm(dst, v_at(g, h, kt, br), pt[:, (at + kt) * P:(at + kt + 1) * P],
                                          start=(fresh and kt == 0 and br == 0), stop=(kt == kts - 1 and br == branches - 1),
                                          skip_group_check=True)
                        last.then_inc(pv_done, 1)

            def xa_pe(layer, h):
                proj_pe(f"kv{layer}", h, lambda: norm_pe(layer * 4 + 2))
                proj_pe(f"q{layer}", h + 1)
                pe.wait_ge(head_sq, 2 + layer)
                for n in range(8):
                    for b in range(2):
                        last = mm(ps[:, n // 2, (n % 2) * 256:(n % 2 + 1) * 256], C("ones"), W(24 + 2 * n + b),
                                  start=(b == 0), stop=(b == 1))
                last.then_inc(head_sums, 1)
                for tt in range(2):
                    for b in range(8):
                        n = tt * 8 + b
                        last = turn(ps[:, 4 + n // 4, (n % 4) * P:(n % 4 + 1) * P], W(8 + b)[:, tt * P:(tt + 1) * P])
                last.then_inc(v_turned, 1)
                pe.wait_ge(v_copied, 2 + 2 * layer)
                pe.wait_ge(heads_ready, 2 + layer)
                softmax_pe("xa", XA_U[layer], XA_O[layer],
                           lambda g, h, qt: [W(16 + 2 * h + c)[:, qt * P:(qt + 1) * P] for c in range(2)],
                           lambda g, h, br: [W(2 * h + c) for c in range(2)],
                           lambda g, h, kt, eb: Wc(6144 + kt * 1024 + (2 * h + eb) * P, P))
                proj_pe(f"o{layer}", h + 2)

            pe.wait_ge(params_loaded, 32)
            pe.wait_ge(zero_ready, 1)
            norm_pe(0)
            proj_pe("ab_in", 1)
            pe.wait_ge(head_sq, 1)
            for b in range(5):
                last = mm(ps[:, b // 2, (b % 2) * 256:(b % 2 + 1) * 256], C("ones64"), W(18 + b), start=True, stop=True)
            last.then_inc(head_sums, 1)
            for tt in range(2):
                turn(ps[:, 4, tt * P:(tt + 1) * P], W(5)[:, tt * P:(tt + 1) * P])
                for b in range(4):
                    last = turn(ps[:, 5 + tt, b * P:(b + 1) * P], W(14 + b)[:, tt * P:(tt + 1) * P])
            last.then_inc(v_turned, 1)
            pe.wait_ge(rope_in, 1)
            for b in range(5):
                last = mm(ps[:, b // 2, (b % 2) * 256:(b % 2 + 1) * 256], C("rot"), W(b), start=True, stop=True)
            last.then_inc(rope_rot, 1)
            pe.wait_ge(heads_ready, 1)
            for g in range(2):
                last = mm(ps[:, 3, g * 256:(g + 1) * 256], C(f"dup{g}"), W(4), start=True, stop=True)
            last.then_inc(dup_ready, 1)
            pe.wait_ge(dup_copied, 1)
            softmax_pe("swa", SWA_U, SWA_O,
                       lambda g, h, qt: [W(2 * g + h // 2)[64 * (h % 2):64 * (h % 2) + 64, qt * P:(qt + 1) * P]],
                       lambda g, h, br: [W(35 + g)[64 * (h % 2):64 * (h % 2) + 64, :]],
                       lambda g, h, kt, br: Wc(9472 + kt * P + g * 64, 64))
            pe.wait_ge(o_drained, 4)
            for st in range(6):
                if st < 4:
                    u = st
                    at_least(pe, z_masked, u)
                    for h in range(2):
                        rows = slice(64 * h, 64 * h + 64)
                        for kt in range(2):
                            last = mm(ps[:, h, kt * 256:(kt + 1) * 256], W(10 + u)[rows, kt * P:(kt + 1) * P], W(6 + u)[rows, :],
                                      start=True, stop=True)
                    last.then_inc(z_ready, 1)
                if 1 <= st < 5:
                    u = st - 1
                    pe.wait_ge(sp_ready, u + 1)
                    at_least(pe, d_ready, u)
                    sp_t = SB_T[u % 2]
                    for h in range(2):
                        lo_t, hi_t = sp_t[:, h * 512:h * 512 + 256], sp_t[:, h * 512 + 256:h * 512 + 512]
                        mm(ps[:, 2 + h, 0:256], C("ge"), lo_t, start=True, stop=False)
                        mm(ps[:, 2 + h, 0:256], C("ones"), hi_t, start=False, stop=True)
                        last = mm(ps[:, 2 + h, 256:512], C("ge"), hi_t, start=True, stop=True)
                    last.then_inc(cs_ready, 1)
                if st >= 2:
                    u = st - 2
                    pe.wait_ge(a_ready, u + 1)
                    o = SB_O + u
                    at_least(pe, o_drained, o - 1)
                    for h in range(2):
                        for kt in range(2):
                            last = mm(ps[64 * h:64 * h + 64, 4 + 2 * (o % 2), 0:256], Wc(9728 + kt * 512 + (2 * u + h) * 64, 64),
                                      PT[u % 2][:, h * 512 + kt * 256:h * 512 + (kt + 1) * 256], start=(kt == 0), stop=(kt == 1))
                    last.then_inc(sb_pv_done, 1)
            proj_pe("ab_out", 2, lambda: norm_pe(1))
            xa_pe(0, 3)
            norm_pe(3)
            ffn_pe(0, 6)
            norm_pe(4)
            proj_pe("hg_in", 7)
            pe.wait_ge(banks_drained, PHASES["hg_in"].e + PHASES["hg_in"].n)
            for tt in range(2):
                for b in range(8):
                    n = tt * 8 + b
                    last = turn(ps[:, 4 + n // 4, (n % 4) * P:(n % 4 + 1) * P], W(16 + b)[:, tt * P:(tt + 1) * P])
            last.then_inc(v_turned, 1)

            def hg_scores(bank, lhs, rhs, tiles):
                for h in range(8):
                    for n, tt in enumerate(tiles):
                        col = h * len(tiles) + n
                        last = mm(ps[:, bank + col // 4, (col % 4) * P:(col % 4 + 1) * P], lhs(h, tt[0]), rhs(h, tt[1]), start=True, stop=True)
                last.then_inc(hg_s, 1)

            pe.wait_ge(hg_kf, 1)
            hg_scores(0, lambda h, t: W(32 + h)[:, t * P:(t + 1) * P], lambda h, t: W(h)[:, t * P:(t + 1) * P], [(0, 0), (1, 1)])
            for lv in range(HG_LEVELS + 1):
                pe.wait_ge(hg_x, lv + 1)
                if lv == 0:
                    pe.wait_ge(v_copied, 3)
                else:
                    pe.wait_ge(hg_a, lv)
                both = lambda h, t: HG_D[lv % 2][:, h * BLK + t * P:h * BLK + (t + 1) * P]
                hg_scores(4 - 4 * (lv % 2), both, both, [(0, 1)] if lv == 0 else [(0, 0), (1, 1)])
            pe.wait_ge(hg_a, HG_LEVELS + 2)
            pe.wait_ge(v_copied, 3)
            A = lambda h, n: Wc(10240 + h * 384 + n * P, P)
            V = lambda h, t: Wc(13312 + t * 1024 + h * P, P)
            for h in range(8):
                o = lambda t: ps[:, h // 2, (h % 2) * 256 + t * P:(h % 2) * 256 + (t + 1) * P]
                mm(o(0), V(h, 0), A(h, 0), start=True, stop=True)
                mm(o(1), V(h, 0), A(h, 1), start=True, stop=False)
                last = mm(o(1), V(h, 1), A(h, 2), start=False, stop=True)
            last.then_inc(hg_o, 1)
            pe.wait_ge(hg_osq, 1)
            for h in range(8):
                last = mm(ps[:, 4 + h // 2, (h % 2) * 256:(h % 2 + 1) * 256], C("ones"), hf[:, h * BLK:(h + 1) * BLK],
                          start=True, stop=True)
            last.then_inc(hg_osum, 1)
            proj_pe("hg_out", 8, lambda: norm_pe(5))
            xa_pe(1, 9)
            norm_pe(7)
            ffn_pe(1, 12)
            ph = PHASES["pool"]
            pe.wait_ge(lo_ready, ph.g + 1)
            p = ph.g % DEPTH
            pe.wait_ge(banks_drained, ph.e)
            for g in range(4):
                pe.wait_ge(h_ready, QUARTERS * 12 + g + 1)
                for b in range(2):
                    for c in range(2):
                        w = slice(((g * 2 + b) * 2 + c) * P, ((g * 2 + b) * 2 + c + 1) * P)
                        m = slice((2 * g + c) * BLK, (2 * g + c + 1) * BLK)
                        last = split_mm(ps[:, g, b * BLK:(b + 1) * BLK], whi[p][:, w], wlo[p][:, w], hh[:, m], hl[:, m],
                                        c == 0, c == 1)
            last.then_inc(slot_used, 1)

            layer_norm_pe(0, banks_drained, lambda c: ph.e + 1)
            ffn_pe(2, 14)
            layer_norm_pe(1, acc_drained, lambda c: QUARTERS * 2 + c + 1)
            proj_pe("nsa_in", 15)
            pe.wait_ge(w1_loaded, 16)
            for tt in range(2):
                for c in range(NB):
                    last = mm(ps[:, 7, tt * 48:(tt + 1) * 48], x[:, c * BLK + tt * P:c * BLK + (tt + 1) * P],
                              Wc(12288 + c * 48, 48), start=(c == 0), stop=(c == NB - 1))
            last.then_inc(gates_ps, 1)
            pe.wait_ge(banks_drained, PHASES["nsa_in"].e + PHASES["nsa_in"].n)
            for n, b0 in enumerate(ROPED):
                for b in range(2):
                    last = mm(ps[:, n, b * 256:(b + 1) * 256], C("rot"), W(b0 + b), start=True, stop=True)
            last.then_inc(rope_rot, 1)
            pe.wait_ge(heads_ready, 4)
            for br in range(2):
                for g in range(4):
                    last = mm(ps[:, g // 2 + 2 * br, (g % 2) * 256:(g % 2 + 1) * 256], C(f"dup{g % 2}"),
                              W(8 + 2 * br + g // 2), start=True, stop=True)
            last.then_inc(cmp_dup, 1)
            pe.wait_ge(cmp_cols, 1)
            for br, pe_name in enumerate(("pe_k", "pe_v")):
                for j in range(16):
                    cols = W(20 + 4 * br, 2).rearrange("p (g m) -> p g m", g=4)[:, :, j:j + 8 * (NCMP - 1) + 1:8]
                    mm(ps[:, 6, 64 * br:64 * br + 60], Wc(8192 + 2048 * br + j * P, P), cols, start=(j == 0), stop=(j == 15))
                for j in range(16):
                    last = mm(ps[:, 5, br:br + 1], Wc(8192 + 2048 * br + j * P, P), R(pe_name, j), start=(j == 0), stop=(j == 15))
            last.then_inc(cmp_hidden, 1)
            pe.wait_ge(cmp_silu, 1)
            mm(ps[:, 1, 0:60], R("w2_k", 0, 128), small[:, 160:220], start=True, stop=True)
            for g in range(4):
                last = mm(ps[0:NCMP, 2, g * 64:(g + 1) * 64], small[:, 220 + g * NCMP:220 + (g + 1) * NCMP], R("w2_v", 0, 64),
                          start=True, stop=True)
            last.then_inc(cmp_kv, 1)
            pe.wait_ge(cmp_kv_copied, 1)
            mm(ps[:, 3, 0:60], C("rot"), small[:, 288:348], start=True, stop=True).then_inc(cmp_rot, 1)
            pe.wait_ge(cmp_roped, 1)
            for qt in range(2):
                for h in range(16):
                    g, rows = h // 4, slice(64 * (h % 2), 64 * (h % 2) + 64)
                    at = (qt * 8 + h // 2) * NCMP
                    last = mm(ps[:, 4 + h % 2, at:at + NCMP], W(h // 2)[rows, qt * P:(qt + 1) * P],
                              small[rows, 288 + g * 15:288 + g * 15 + 15], start=True, stop=True)
            last.then_inc(cmp_scores, 1)
            pe.wait_ge(gates_ready, 1)
            for n, b0 in enumerate((12, 16)):
                for g in range(4):
                    last = mm(ps[:, 2 * n + g // 2, (g % 2) * 256:(g % 2 + 1) * 256], C(f"dup{g % 2}"), W(b0 + g // 2),
                              start=True, stop=True)
            last.then_inc(dup_ready, 1)
            for n, b0 in enumerate((14, 18)):
                for tt in range(2):
                    for b in range(2):
                        last = turn(ps[:, 6 + n, (tt * 2 + b) * P:(tt * 2 + b + 1) * P], W(b0 + b)[:, tt * P:(tt + 1) * P])
            last.then_inc(v_turned, 1)
            pe.wait_ge(cmp_probs, 1)
            pe.wait_ge(dup_copied, 2)
            pe.wait_ge(v_copied, 5)
            for n in range(4):
                for h in range(8):
                    head = (n // 2) * 8 + h
                    last = turn(ps[0:NCMP, 2 * n + h // 4, (h % 4) * P:(h % 4 + 1) * P],
                                Wc(10240 + ((head % 2) * 16 + (n % 2) * 8 + head // 2) * NCMP, NCMP))
            last.then_inc(cmp_turned, 1)
            pe.wait_ge(cmp_ready, 1)
            softmax_pe("nsa", NSA_U, NSA_O,
                       lambda g, h, qt: [W(2 * g + h // 2)[64 * (h % 2):64 * (h % 2) + 64, qt * P:(qt + 1) * P]],
                       lambda g, h, br: [W(20 + 4 * br + g)[64 * (h % 2):64 * (h % 2) + 64, :]],
                       lambda g, h, kt, br: Wc(7168 + 512 * br + kt * 256 + g * 64, 64),
                       cmp=lambda g, h, qt: (rstd[0:NCMP, g * 64:(g + 1) * 64],
                                             Wc(PCT[g // 2] + ((g % 2) * 4 + h) * 256 + qt * P, P)[0:NCMP, :]))
            proj_pe("nsa_out", 16)
            layer_norm_pe(2, banks_drained, lambda c: PHASES["nsa_out"].e + c + 1)
            pe.wait_ge(x_ready, 3)
            for tt in range(2):
                for c in range(NB):
                    last = mm(ps[:, 0, tt * 8:(tt + 1) * 8], x[:, c * BLK + tt * P:c * BLK + (tt + 1) * P],
                              R("router", c * 8, 8), start=(c == 0), stop=(c == NB - 1))
            last.then_inc(logits_ps, 1)
            for tt in range(2):
                for c in range(NB):
                    last = turn(ps[:, 3 + 2 * tt + c // 4, (c % 4) * P:(c % 4 + 1) * P], x[:, c * BLK + tt * P:c * BLK + (tt + 1) * P])
            last.then_inc(x_turned, 1)
            pe.wait_ge(picked, 1)
            ind = small[:, 608:624]
            mm(ps[:, 1, 0:16], C("ge"), ind, start=True, stop=True)
            mm(ps[:, 1, 0:8], C("ones"), ind[:, 8:16], start=False, stop=True, skip_group_check=True)
            mm(ps[:, 1, 16:24], C("ones"), ind[:, 0:8], start=True, stop=False)
            last = mm(ps[:, 1, 16:24], C("ones"), ind[:, 8:16], start=False, stop=True)
            last.then_inc(counts_ps, 1)
            gu, down = PHASES["moe_gu"], PHASES["moe_down"]

            def few_gather(e):
                for c in range(NB):
                    for tt in range(2):
                        take = bass.ds(e * 256 + (FEW_TAKE + tt * P), P)
                        last = mm(ps[:, 5 + c // 4, (c % 4) * P:(c % 4 + 1) * P], FEW_TOK[:, tt * 1024 + c * P:tt * 1024 + (c + 1) * P],
                                  work[:, take], start=(tt == 0), stop=(tt == 1))
                last.then_inc(gathered_ps, 1)

            def few_gu(half, i, k, s):
                p = (gu.g + k) % DEPTH
                pe.wait_ge(raw_loaded[p], i * 16 + 16 * ((gu.g + k) // DEPTH + 1) + half * (16 * PER_HALF // DEPTH))
                pe.wait_ge(act_ready, s + (gu.a - 2) + half * HALF)
                for b in range(2):
                    for c in range(NB):
                        last = mm(ps[:, p, b * P:(b + 1) * P], raw[p][:, (b * NB + c) * P:(b * NB + c + 1) * P],
                                  FEW_X[:, c * P:(c + 1) * P], start=(c == 0), stop=(c == NB - 1))
                last.then_inc(slot_used, 1)

            def few_down(half, s):
                k = s % DEPTH
                p = (down.g + k) % DEPTH
                pe.wait_ge(raw_loaded[p], 16 * ((down.g + k) // DEPTH + 1 + s // DEPTH) + half * (16 * PER_HALF // DEPTH))
                for c in range(2):
                    pe.wait_ge(act_ready, 2 * s + c + 1 + gu.a + half * HALF)
                    for b in range(2):
                        last = mm(ps[:, 3 + b, :], few_act(2 * s + c), raw[p][:, c * 1024 + b * 512:c * 1024 + (b + 1) * 512],
                                  start=False, stop=False, skip_group_check=True)
                last.then_inc(slot_used, 1)

            def few_zero(start, stop):
                for b in range(2):
                    last = mm(ps[:, 3 + b, :], zero[:, :], zero[:, :].unsqueeze(1).to_broadcast([P, 4, P]), start=start, stop=stop,
                              skip_group_check=True)
                return last

            def few_expert(e, more):
                pe.wait_ge(gathered, e + 1)
                pe.wait_ge(y_added, e + 1)
                few_zero(True, False)
                with pe.Fori(0, 2) as part:
                    half = e * 2 + part
                    slot_loop(pe, gu, lambda i, k, s: few_gu(half, i, k, s))
                    for s in range(down.n):
                        few_down(half, s)
                few_zero(False, True).then_inc(y_ready, 1)
                if more:
                    few_gather(e + 1)
                pe.wait_ge(y_kept, e + 1)
                for c in range(NB):
                    if more and c == 4:
                        pe.wait_ge(gathered, e + 2)
                    give = bass.ds(e * 256 + FEW_GIVE, 256)
                    last = mm(ps[:, 3 + c // 2, (c % 2) * 256:(c % 2 + 1) * 256], FEW_Y[:, c * P:(c + 1) * P], work[:, give],
                              start=True, stop=True)
                last.then_inc(spread_out, 1)

            with pe.If(few_flag(pe)):
                pe.wait_ge(places_built, 1)
                pe.wait_ge(x_tokens, 1)
                few_gather(0)
                pe.wait_ge(gathered, 1)
                for n in range(16):
                    last = turn(ps[:, 4 + n // 4, (n % 4) * P:(n % 4 + 1) * P], FEW_WEIGHT[:, n * P:(n + 1) * P])
                last.then_inc(spread_ps, 1)
                pe.wait_ge(spread_ready, 1)
                with pe.Fori(0, EXPERTS - 1) as e:
                    few_expert(e, True)
                few_expert(EXPERTS - 1, False)
            with pe.Else():
                pe.wait_ge(x_tokens, 1)
                pe.wait_ge(cw_diag, 1)
                for n in range(4):
                    last = mm(ps[:, n, :], C("ones"), Wc(n * 512, 512), start=True, stop=True)
                last.then_inc(cw_ps, 1)
                pe.wait_ge(h_ready, QUARTERS * 17)
                pe.wait_ge(cw_ready, 1)
                acc_zero(True, False)
                with pe.Fori(0, EXPERTS) as e:
                    with pe.Fori(0, 2) as part:
                        half = e * 2 + part
                        slot_loop(pe, gu, lambda i, k, s: proj_slot(gu, k, s, half * PER_HALF, half * HALF))
                        slot_loop(pe, down, lambda i, k, s: down_slot(
                            down, k, s, lambda s, c: s * 2 + (gu.a + c + 1) + half * HALF, half * PER_HALF))
                acc_zero(False, True).then_inc(acc_ready, 1)
            layer_norm_pe(3, acc_drained, lambda c: QUARTERS * 3 + c + 1)

        @block.vector
        def _(dve):
            chain, order = [0], [dve_step]
            V = nc.vector

            def step(ins):
                chain[0] = chain[0] + 1
                ins.then_inc(order[0], 1)

            def sync():
                dve.wait_ge(order[0], chain[0])

            def link(ins):
                step(ins)
                sync()

            def drain(ph, k, s, write, off_g=0):
                dve.wait_ge(slot_used, s + (ph.g + 1) + off_g)
                write((ph.g + k) % DEPTH, s).then_inc(banks_drained, 1)

            def proj_copy(name, b0, then=None):
                ph = PHASES[name]

                def write(bank, s):
                    at = bass.ds(s * 512 + b0 * BLK, 512) if not isinstance(s, int) else slice(s * 512 + b0 * BLK, s * 512 + b0 * BLK + 512)
                    return V.tensor_copy(work[:, at], ps[:, bank, :])

                def body(i, k, s):
                    drain(ph, k, s, write)
                    if then is not None and s == 2:
                        then()

                slot_loop(dve, ph, body, peel=0 if then is None else 1)
                dve.wait_ge(banks_drained, ph.e + ph.n)

            def proj_add(name, alpha=1.0, square=False, then=None):
                ph = PHASES[name]

                def body(i, k, s):
                    drain(ph, k, s, lambda bank, s: V.scalar_tensor_tensor(
                        out=xs(s), in0=xs(s), scalar=alpha, in1=ps[:, bank, :], op0=ALU.mult, op1=ALU.add))
                    if square:
                        dve.wait_ge(banks_drained, ph.e + s + 1)
                        squares(x[:, :], s)
                    if then is not None and s in then:
                        then[s]()

                slot_loop(dve, ph, body)
                dve.wait_ge(banks_drained, ph.e + ph.n)

            def xs(s):
                return x[:, bass.ds(s * 512, 512)] if not isinstance(s, int) else x[:, s * 512:s * 512 + 512]

            def q4(t, c):
                return t[:, c * 512:(c + 1) * 512]

            def squares(src, c):
                V.tensor_tensor(q4(hf, c), q4(src, c), q4(src, c), ALU.mult).then_inc(squares_ready, 1)

            def all_squares(src):
                for c in range(QUARTERS):
                    squares(src, c)

            def staged(*stages):
                done = {}
                for t in range(QUARTERS + len(stages) - 1):
                    for j, stage_of in enumerate(stages):
                        c = t - j
                        if 0 <= c < QUARTERS:
                            if j:
                                dve.wait_ge(order[0], done[j - 1, c])
                            stage_of(c)
                            done[j, c] = chain[0]

            def to_hi(src):
                return lambda c: step(V.tensor_copy(q4(hh, c), q4(src, c)))

            def to_lo(src):
                return lambda c: V.tensor_tensor(q4(hl, c), q4(src, c), q4(hh, c).bitcast(F32), ALU.subtract).then_inc(h_ready, 1)

            def split_h(src):
                staged(to_hi(src), to_lo(src))

            def scaled(src, gain, at):
                def stage_of(c):
                    for b in (2 * c, 2 * c + 1):
                        step(V.scalar_tensor_tensor(out=hf[:, b * BLK:(b + 1) * BLK], in0=src[:, b * BLK:(b + 1) * BLK],
                                                    scalar=R(gain, at + b), in1=rstd[:, :], op0=ALU.mult, op1=ALU.mult))
                return stage_of

            def rms_norm(n, src, gain, at):
                dve.wait_ge(rstd_ready, n + 1)
                staged(scaled(src, gain, at), to_hi(hf), to_lo(hf))

            def norm_ahead(n, src, gain, at):
                dve.wait_ge(rstd_ready, n + 1)
                for c in range(QUARTERS):
                    scaled(src, gain, at)(c)

            def layer_norm(i, g_at, last=False):
                dve.wait_ge(mean_ready, i + 1)

                def centre(c):
                    for b in (2 * c, 2 * c + 1):
                        step(V.scalar_tensor_tensor(out=xb(b), in0=ps[:, MEAN_BANK[i], 0:BLK], scalar=-1.0 / D, in1=xb(b),
                                                    op0=ALU.mult, op1=ALU.add))

                staged(centre, lambda c: squares(x, c))
                dve.wait_ge(rstd_ready, 9 + i)

                def scale(c):
                    for b in (2 * c, 2 * c + 1):
                        step(V.scalar_tensor_tensor(out=xb(b), in0=xb(b), scalar=R("ln_g", g_at + b), in1=rstd[:, :],
                                                    op0=ALU.mult, op1=ALU.mult))

                def shift(c):
                    for b in (2 * c, 2 * c + 1):
                        ins = V.tensor_scalar(xb(b), xb(b), R("ln_b", g_at + b), None, ALU.add)
                        if b < NB - 1:
                            step(ins)
                        else:
                            ins.then_inc(x_ready, 1)

                def hi_of(c):
                    if c == QUARTERS - 1:
                        dve.wait_ge(x_ready, i + 1)
                    to_hi(x)(c)

                if last:
                    staged(scale, shift)
                    dve.wait_ge(x_ready, i + 1)
                else:
                    staged(scale, shift, hi_of, to_lo(x))

            def softmax_dve(kind, u0, o0, scale, mask, o_blocks):
                us = units(kind)
                branches = 2 if kind == "nsa" else 1
                for st in range(len(us) + 3):
                    if st < len(us):
                        u = u0 + st
                        g, qt, br = us[st]
                        pr, s0, nk = PROBS[u % 3], STATS[u % 3], P * key_tiles(kind, qt)
                        dve.wait_ge(scores_ready, u + 1)
                        at_least(dve, pt_ready, u - 2)
                        if mask is None:
                            V.tensor_scalar(pr, banks(0), scale, None, ALU.mult).then_inc(scores_masked, 1)
                        else:
                            V.scalar_tensor_tensor(out=r3(pr, 4)[:, :, 0:nk], in0=r3(banks(0), 4)[:, :, 0:nk], scalar=scale,
                                                   in1=mask(qt)[:, 0:nk].unsqueeze(1).to_broadcast([P, 4, nk]),
                                                   op0=ALU.mult, op1=ALU.add).then_inc(scores_masked, 1)
                        dve.wait_ge(scores_masked, u + 1)
                        link(V.tensor_reduce(small[:, s0:s0 + 4], r3(pr, 4)[:, :, 0:nk], AX, ALU.max))
                        if kind == "swa":
                            link(V.tensor_tensor(small[:, s0:s0 + 4], small[:, s0:s0 + 4], R("sinks", 4 * g, 4), ALU.max))
                            link(V.tensor_tensor(small[:, s0 + 8:s0 + 12], R("sinks", 4 * g, 4), small[:, s0:s0 + 4], ALU.subtract))
                        V.tensor_scalar(small[:, s0:s0 + 4], small[:, s0:s0 + 4], -1.0, None, ALU.mult).then_inc(negmax_ready, 1)
                    if 1 <= st <= len(us):
                        u = u0 + st - 1
                        g, qt, br = us[st - 1]
                        pr, s0, nk = PROBS[u % 3], STATS[u % 3], P * key_tiles(kind, qt)
                        dve.wait_ge(exp_done, u + 1)
                        if kind == "swa":
                            link(V.tensor_tensor(small[:, s0 + 4:s0 + 8], small[:, s0 + 4:s0 + 8], small[:, s0 + 12:s0 + 16], ALU.add))
                        link(V.reciprocal(small[:, s0 + 16:s0 + 20], small[:, s0 + 4:s0 + 8]))
                        if kind == "nsa":
                            at = 64 + qt * 48 + g * 12
                            coef = small[:, s0 + 16:s0 + 20].rearrange("p (par j) -> p par j", par=2)
                            link(V.tensor_tensor(coef, coef, small[:, at:at + 12].rearrange(
                                "p (j par b) -> p par j b", j=2, par=2)[:, :, :, br + 1], ALU.mult))
                        for h in range(4):
                            ins = V.tensor_scalar(pr[:, h * 256:h * 256 + nk], pr[:, h * 256:h * 256 + nk],
                                                  small[:, s0 + 16 + h:s0 + 17 + h], None, ALU.mult)
                        ins.then_inc(probs_ready, 1)
                    if st >= 3:
                        u = u0 + st - 3
                        g, qt, br = us[st - 3]
                        if br == branches - 1:
                            o = o0 + (st - 3) // branches
                            dve.wait_ge(pv_done, u + 1)
                            evacuate(o, o_blocks(g), qt * P, 4 + 2 * (o % 2))

            def evacuate(o, blocks, col, bank, width=P):
                b0, n = blocks
                view = lambda t: t[:, :].rearrange("p (b c) -> p b c", b=NB)[:, b0:b0 + n, col:col + width]
                src = banks(bank)[:, 0:n * width].rearrange("p (b c) -> p b c", b=n)
                link(V.tensor_copy(view(hh), src))
                V.tensor_tensor(view(hl), src, view(hh).bitcast(F32), ALU.subtract).then_inc(o_drained, 1)

            def conv_ffn(layer, l, alpha):
                conv = l is not None
                for i in range(4):
                    ph = PHASES[f"ffn{layer}_{i}"]
                    if ph.kind == "down":
                        continue
                    c0 = chain[0]
                    first = 0 if i == 0 else HALF

                    def body(i, k, s, ph=ph, c0=c0, first=first):
                        bank = (ph.g + k) % DEPTH
                        buf = Wc(512 * bank, 512)
                        f = Wc(1536 + 256 * bank, 256)
                        chain[0] = s * steps + c0
                        dve.wait_ge(slot_used, s + (ph.g + 1))
                        if conv:
                            for b in range(2):
                                p0 = b * FF + first
                                step(V.tensor_scalar(buf[:, b * BLK:(b + 1) * BLK], ps[:, bank, b * BLK:(b + 1) * BLK],
                                                     Rd("conv_w", l * 132 + 88 + p0, s), Rd("conv_b", l * 44 + p0, s), ALU.mult, ALU.add))
                            sync()
                            for tap in (1, 2):
                                for b in range(2):
                                    p0 = b * FF + first
                                    o = buf[:, b * BLK + tap:(b + 1) * BLK]
                                    ins = V.scalar_tensor_tensor(out=o, in0=ps[:, bank, b * BLK:(b + 1) * BLK - tap],
                                                                 scalar=Rd("conv_w", l * 132 + (2 - tap) * 44 + p0, s), in1=o,
                                                                 op0=ALU.mult, op1=ALU.add)
                                    if (tap, b) != (2, 1):
                                        step(ins)
                                if tap == 1:
                                    sync()
                            ins.then_inc(banks_drained, 1)
                            dve.wait_ge(banks_drained, s + (ph.e + 1))
                            dve.wait_ge(gate_act, s + (ph.a + 1))
                            link(V.tensor_tensor(f, buf[:, 0:BLK], buf[:, BLK:2 * BLK], ALU.mult))
                        else:
                            dve.wait_ge(gate_act, s + (ph.a + 1))
                            V.tensor_tensor(f, buf[:, 0:BLK], ps[:, bank, BLK:2 * BLK], ALU.mult).then_inc(banks_drained, 1)
                            dve.wait_ge(banks_drained, s + (ph.e + 1))
                        split_act(s, f)

                    steps = 7 if conv else 1
                    slot_loop(dve, ph, body)
                    chain[0] = c0 + steps * ph.n
                dve.wait_ge(acc_ready, layer + 1)
                for c in range(QUARTERS + 1):
                    if c < QUARTERS:
                        V.scalar_tensor_tensor(out=xs(c), in0=xs(c), scalar=alpha, in1=ps[:, 3 + c, :], op0=ALU.mult,
                                               op1=ALU.add).then_inc(acc_drained, 1)
                    if layer == 0 and c:
                        dve.wait_ge(acc_drained, c)
                        squares(x, c - 1)
                dve.wait_ge(acc_drained, QUARTERS * (layer + 1))

            def Rd(name, a, s):
                at = PARAM[name][0] + a
                return par[:, at + s:at + s + 1] if isinstance(s, int) else par[:, bass.ds(s + at, 1)]

            def split_act(s, f):
                at = slice(s * BLK, (s + 1) * BLK) if isinstance(s, int) else bass.ds(s * BLK, BLK)
                link(V.tensor_copy(ahi[:, at], f))
                V.tensor_tensor(alo[:, at], f, ahi[:, at].bitcast(F32), ALU.subtract).then_inc(act_ready, 1)

            def xa(layer, before):
                mem = W(24, 8)

                def mem_squares():
                    dve.wait_ge(mem_loaded, 16 * (layer + 1))
                    all_squares(mem)

                proj_add(before, then={0: mem_squares, 2: lambda: norm_ahead(layer * 4 + 1, mem, "norm_mem", layer * 8)})
                sync()
                split_h(hf)
                dve.wait_ge(h_ready, QUARTERS * (3 + 6 * layer))
                all_squares(x)
                proj_copy(f"kv{layer}", 0, lambda: norm_ahead(layer * 4 + 2, x, "norm_cross", layer * 8))
                sync()
                split_h(hf)
                proj_copy(f"q{layer}", 16)
                step(V.tensor_tensor(W(24, 8), W(16, 8), W(16, 8), ALU.mult))
                V.tensor_tensor(W(32, 8), W(0, 8), W(0, 8), ALU.mult).then_inc(head_sq, 1)
                dve.wait_ge(head_rstd, 2 + layer)
                for h in range(8):
                    for c in range(2):
                        blk = W(16 + 2 * h + c) if h < 4 else W(2 * (h - 4) + c)
                        ins = V.scalar_tensor_tensor(out=blk, in0=blk, scalar=R("xa_q" if h < 4 else "xa_k", 2 * layer + c),
                                                     in1=W(42 + h), op0=ALU.mult, op1=ALU.mult)
                        if (h, c) == (7, 1):
                            ins.then_inc(heads_ready, 1)
                dve.wait_ge(heads_ready, 2 + layer)
                dve.wait_ge(v_turned, 2 + 2 * layer)
                V.tensor_copy(W(24, 8), banks(4, 4)).then_inc(v_copied, 1)
                softmax_dve("xa", XA_U[layer], XA_O[layer], 256 ** -0.5, None, lambda g: (0, 8))
                attention_whole(XA_O[layer] + 2)
                proj_add(f"o{layer}", square=True)

            def attention_whole(outputs):
                dve.wait_ge(o_drained, outputs)
                V.memset(small[:, 639:640], 0.0).then_inc(h_ready, QUARTERS)

            def rope(dst, rot_ps, n, cos, sin, tmp):
                wide = lambda t: t.unsqueeze(1).to_broadcast([P, n, t.shape[-1]])
                link(V.tensor_tensor(r3(tmp, n), r3(rot_ps, n), wide(sin), ALU.mult))
                link(V.tensor_tensor(r3(dst, n), r3(dst, n), wide(cos), ALU.mult))
                return V.tensor_tensor(dst, dst, tmp, ALU.add)

            V.memset(zero[:, :].bitcast(F32), 0.0).then_inc(zero_ready, 1)
            dve.wait_ge(params_loaded, 32)
            dve.wait_ge(positions_loaded, 16)
            ang, turns, pos = W(43), W(44), W(42)
            link(V.tensor_copy(ang, pos.bitcast(I32)))
            link(V.tensor_scalar(ang, ang, C("invf"), None, ALU.mult))
            link(V.tensor_scalar(turns, ang, float(1.0 / (2.0 * np.pi)), ROUND, ALU.mult, ALU.add))
            link(V.tensor_scalar(turns, turns, ROUND, None, ALU.subtract))
            for part in TWO_PI:
                link(V.scalar_tensor_tensor(out=ang, in0=turns, scalar=-part, in1=ang, op0=ALU.mult, op1=ALU.add))
            link(V.tensor_scalar(W(33), ang, PI, -PI, ALU.min, ALU.max))
            link(V.tensor_scalar(ang, ang, float(np.pi / 2), None, ALU.add))
            link(V.tensor_scalar(turns, ang, PI, float(-2 * np.pi), ALU.is_gt, ALU.mult))
            link(V.tensor_tensor(ang, ang, turns, ALU.add))
            V.tensor_scalar(W(34), ang, PI, -PI, ALU.min, ALU.max).then_inc(angles_ready, 1)
            dve.wait_ge(x_loaded, 16)
            all_squares(x)
            rms_norm(0, x, "norm_mix", 0)
            proj_copy("ab_in", 0)
            V.tensor_tensor(W(18, 5), W(0, 5), W(0, 5), ALU.mult).then_inc(head_sq, 1)
            step(V.tensor_scalar(W(6, 4), W(6, 4), 64 ** -0.5, None, ALU.mult))
            dve.wait_ge(head_rstd, 1)
            step(V.scalar_tensor_tensor(out=W(0, 4), in0=W(0, 4), scalar=R("swa_q"), in1=W(23, 4), op0=ALU.mult, op1=ALU.mult))
            V.scalar_tensor_tensor(out=W(4), in0=W(4), scalar=R("swa_k"), in1=W(27), op0=ALU.mult, op1=ALU.mult).then_inc(rope_in, 1)
            dve.wait_ge(rope_in, 1)
            dve.wait_ge(v_turned, 1)
            step(V.tensor_copy(W(37), ps[:, 4, 0:256]))
            V.tensor_copy(W(38, 4), banks(5)).then_inc(v_copied, 1)
            dve.wait_ge(rope_rot, 1)
            dve.wait_ge(sines_ready, 1)
            rope(W(0, 5), banks(0, 3)[:, 0:5 * BLK], 5, W(34), W(33), W(28, 5)).then_inc(heads_ready, 1)
            dve.wait_ge(dup_ready, 1)
            V.tensor_copy(W(35, 2), ps[:, 3, :]).then_inc(dup_copied, 1)
            dve.wait_ge(stage_loaded, 16)
            softmax_dve("swa", SWA_U, SWA_O, 64 ** -0.5, lambda qt: stage[:, qt * 256:(qt + 1) * 256], lambda g: (2 * g, 2))
            for st in range(6):
                if st < 4:
                    u = st
                    dve.wait_ge(z_ready, u + 1)
                    at_least(dve, a_ready, u - 2)
                    V.tensor_tensor(r3(PROBS[u % 3], 2), r3(banks(0), 2), stage[:, 512:1024].unsqueeze(1).to_broadcast([P, 2, 512]),
                                    ALU.add).then_inc(z_masked, 1)
                if 1 <= st < 5:
                    u = st - 1
                    z, t = PROBS[u % 3], SB_T[u % 2]
                    dve.wait_ge(soft_ready, u + 1)
                    V.scalar_tensor_tensor(out=t, in0=z, scalar=0.0, in1=t, op0=ALU.max, op1=ALU.add).then_inc(sp_ready, 1)
                    dve.wait_ge(cs_ready, u + 1)
                    V.tensor_tensor(z, z, banks(2), ALU.subtract).then_inc(d_ready, 1)
                if st >= 2:
                    u = st - 2
                    dve.wait_ge(sb_pv_done, u + 1)
                    o = SB_O + u
                    evacuate(o, (4 + u, 1), 0, 4 + 2 * (o % 2), BLK)
            attention_whole(SB_O + 4)
            xa(0, "ab_out")
            rms_norm(3, x, "norm_ffn", 0)
            conv_ffn(0, 0, 1.0)
            rms_norm(4, x, "norm_mix", 8)
            link(V.tensor_tensor(small[:, 408:416], R("lb", 0, 8), R("lb", 8, 8), ALU.max))
            step(V.tensor_tensor(small[:, 400:408], R("lb", 0, 8), small[:, 408:416], ALU.subtract))
            V.tensor_tensor(small[:, 408:416], R("lb", 8, 8), small[:, 408:416], ALU.subtract).then_inc(hg_lb, 1)
            dve.wait_ge(hg_lb_exp, 1)
            link(V.tensor_tensor(small[:, 440:448], small[:, 416:424], small[:, 424:432], ALU.add))
            link(V.reciprocal(small[:, 440:448], small[:, 440:448]))
            link(V.tensor_tensor(small[:, 432:440], small[:, 424:432], small[:, 440:448], ALU.mult))
            link(V.tensor_scalar(small[:, 440:448], small[:, 432:440], -1.0, 1.0, ALU.mult, ALU.add))
            proj_copy("hg_in", 0)
            dve.wait_ge(hg_sig, 1)
            for h in range(8):
                step(V.tensor_scalar(W(32 + h), W(32 + h), small[:, 440 + h:441 + h], None, ALU.mult))
                ins = V.tensor_scalar(W(8 + h), W(8 + h), small[:, 440 + h:441 + h], small[:, 432 + h:433 + h], ALU.mult, ALU.add)
                if h < 7:
                    step(ins)
            ins.then_inc(hg_kf, 1)
            dve.wait_ge(v_turned, 3)
            V.tensor_copy(W(52, 8), banks(4, 4)).then_inc(v_copied, 1)
            link(V.memset(hf[:, :], 1.0))
            link(V.memset(hf[:, 0:NB * BLK:P], 0.0))
            step(V.memset(W(40, 12), 0.0))
            dve.wait_ge(hg_log, 1)
            link(V.tensor_tensor_scan(W(8, 8), hf[:, :], W(8, 8), 0.0, ALU.mult, ALU.add))
            dve.wait_ge(stage_loaded, 32)
            A = W(40, 12).rearrange("p (h n t) -> p h n t", h=8, n=3)
            tiles = lambda t: t.rearrange("p (h n t) -> p h n t", h=8, n=2)
            b, q, key = W(8, 8), W(0, 8), W(32, 8)
            halves = lambda t, half: t.rearrange("p (n t) -> p n t", t=2 * half)

            def keep(lv, n, bank):
                dve.wait_ge(hg_s, n)
                mask = stage[:, lv * P:(lv + 1) * P].bitcast(I32)
                for tt in range(2):
                    ins = V.copy_predicated(A[:, :, 2 * tt, :], mask.unsqueeze(1).to_broadcast([P, 8, P]),
                                            tiles(banks(bank, 4))[:, :, tt, :])
                    if tt == 0:
                        step(ins)
                ins.then_inc(hg_a, 1)

            def decays(lv):
                d = HG_D[lv % 2]
                if lv == 0:
                    step(V.tensor_tensor(tiles(d)[:, :, 0, :], tiles(b)[:, :, 0, P - 1:P].to_broadcast([P, 8, P]),
                                         tiles(b)[:, :, 0, :], ALU.subtract))
                    V.tensor_copy(tiles(d)[:, :, 1, :], tiles(b)[:, :, 1, :]).then_inc(hg_d, 1)
                else:
                    half = P >> lv
                    V.tensor_tensor(halves(d, half), halves(b, half),
                                    halves(b, half)[:, :, half - 1:half].to_broadcast([P, NB * BLK // (2 * half), 2 * half]),
                                    ALU.subtract).then_inc(hg_d, 1)

            decays(0)
            decays(1)
            keep(0, 1, 0)
            for lv in range(HG_LEVELS + 2):
                if lv <= HG_LEVELS:
                    half = P >> lv if lv else P
                    e_ = xk = HG_D[lv % 2]
                    dve.wait_ge(hg_e, lv + 1)
                    step(V.tensor_tensor(halves(xk, half)[:, :, 0:half], halves(e_, half)[:, :, 0:half],
                                         halves(key, half)[:, :, 0:half], ALU.mult))
                    V.tensor_tensor(halves(xk, half)[:, :, half:2 * half], halves(e_, half)[:, :, half:2 * half],
                                    halves(q, half)[:, :, half:2 * half], ALU.mult).then_inc(hg_x, 1)
                if lv == 1:
                    dve.wait_ge(hg_s, 2)
                    V.tensor_copy(A[:, :, 1, :], r3(banks(4), 8)).then_inc(hg_a, 1)
                elif lv > 1:
                    dve.wait_ge(hg_a, lv)
                    keep(lv - 1, lv + 1, 4 - 4 * ((lv - 1) % 2))
                if lv + 2 <= HG_LEVELS:
                    dve.wait_ge(hg_s, lv + 2)
                    decays(lv + 2)
            dve.wait_ge(hg_o, 1)
            link(V.tensor_copy(W(16, 8), banks(0, 4)))
            V.tensor_tensor(hf[:, :], W(16, 8), W(16, 8), ALU.mult).then_inc(hg_osq, 1)
            dve.wait_ge(hg_orstd, 1)
            link(V.tensor_tensor(W(16, 8), W(16, 8), W(8, 8), ALU.mult))
            link(V.scalar_tensor_tensor(out=W(16, 8), in0=W(16, 8), scalar=R("o_norm"), in1=W(24, 8), op0=ALU.mult, op1=ALU.mult))
            split_h(W(16, 8))
            xa(1, "hg_out")
            rms_norm(7, x, "norm_ffn", 8)
            conv_ffn(1, 1, 1.0)
            pad = 16
            sums = [Wc(4352 * i, NB * (pad + BLK)).rearrange("p (b t) -> p b t", b=NB) for i in range(2)]
            for i in range(2):
                step(V.memset(sums[i][:, :, 0:pad], 0.0))
            link(V.tensor_copy(sums[0][:, :, pad:], x[:, :].rearrange("p (b t) -> p b t", b=NB)))
            dve.wait_ge(stage_loaded, 48)
            for g in range(4):
                old, new, back = sums[g % 2], sums[(g + 1) % 2], 1 << g
                link(V.tensor_tensor(new[:, 2 * g:, pad:], old[:, 2 * g:, pad:], old[:, 2 * g:, pad - back:pad + BLK - back], ALU.add))
                count = stage[:, g * BLK:(g + 1) * BLK].unsqueeze(1).to_broadcast([P, 2, BLK])
                step(V.tensor_tensor(r3(hf[:, 2 * g * BLK:(2 * g + 2) * BLK], 2), new[:, 2 * g:2 * g + 2, pad:], count, ALU.mult))
            sync()
            link(V.tensor_tensor(hf[:, :], hf[:, :], x[:, :], ALU.subtract))
            split_h(hf)
            dve.wait_ge(h_ready, QUARTERS * 13)
            step(V.tensor_scalar(hf[:, :], x[:, :], ALPHA, None, ALU.mult))
            dve.wait_ge(slot_used, PHASES["pool"].g + 1)
            sync()
            for c in range(NB):
                ins = V.scalar_tensor_tensor(out=xb(c), in0=ps[:, c // 2, (c % 2) * BLK:(c % 2 + 1) * BLK], scalar=R("pool_scale", c),
                                             in1=hf[:, c * BLK:(c + 1) * BLK], op0=ALU.mult, op1=ALU.add)
            ins.then_inc(banks_drained, 1)
            layer_norm(0, 0)
            conv_ffn(2, None, ALPHA)
            layer_norm(1, 8)
            proj_copy("nsa_in", 0)
            dve.wait_ge(rope_rot, 2)
            dve.wait_ge(stage_loaded, 64)
            for n, b0 in enumerate(ROPED):
                ins = rope(W(b0, 2), ps[:, n, :], 2, stage[:, 512:768], stage[:, 768:1024], W(50 + 2 * (n % 2), 2))
                if n < 5:
                    step(ins)
            ins.then_inc(heads_ready, 1)
            dve.wait_ge(cmp_dup, 1)
            for br in range(2):
                for odd in range(2):
                    rows = slice(64 * odd, 64 * odd + 64)
                    ins = V.tensor_copy(W(20 + 4 * br, 2)[rows, :].rearrange("p (g m) -> p g m", g=4),
                                        banks(2 * br)[rows, :].rearrange("p (g m two) -> p g m two", g=4, two=2)[:, :, :, odd])
                    if (br, odd) != (1, 1):
                        step(ins)
            ins.then_inc(cmp_cols, 1)
            dve.wait_ge(cmp_hidden, 1)
            V.tensor_copy(small[:, 280:282], ps[:, 5, 0:2]).then_inc(cmp_bias, 1)
            dve.wait_ge(cmp_kv, 1)
            step(V.tensor_copy(rstd[0:NCMP, :], ps[0:NCMP, 2, 0:256]))
            V.tensor_copy(small[:, 288:348], ps[:, 1, 0:60]).then_inc(cmp_kv_copied, 1)
            dve.wait_ge(cmp_rot, 1)
            dve.wait_ge(cmp_kv_copied, 1)
            rope(small[:, 288:348], ps[:, 3, 0:60], 4, C("cend_cos"), C("cend_sin"), small[:, 348:408]).then_inc(cmp_roped, 1)
            dve.wait_ge(cmp_scores, 1)
            rows_of = lambda t: t.rearrange("p (h n) -> p h n", n=NCMP)
            wide = lambda t: t.unsqueeze(2).to_broadcast([P, 32, NCMP])
            pc = Wc(10240, 480)
            for n in range(4):
                odd, qt = n // 2, n % 2
                step(V.scalar_tensor_tensor(out=rows_of(pc[:, n * 120:(n + 1) * 120]),
                                            in0=rows_of(ps[:, 4 + odd, qt * 120:(qt + 1) * 120]), scalar=64 ** -0.5,
                                            in1=C("cmp_mask", qt * 15, 15).unsqueeze(1).to_broadcast([P, 8, NCMP]),
                                            op0=ALU.mult, op1=ALU.add))
            sync()
            link(V.tensor_reduce(small[:, 512:544], rows_of(pc), AX, ALU.max))
            V.tensor_tensor(rows_of(pc), rows_of(pc), wide(small[:, 512:544]), ALU.subtract).then_inc(cmp_shifted, 1)
            dve.wait_ge(cmp_exp, 1)
            link(V.tensor_reduce(small[:, 544:576], rows_of(pc), AX, ALU.add))
            link(V.reciprocal(small[:, 544:576], small[:, 544:576]))
            dve.wait_ge(gates_ready, 1)
            for n in range(4):
                odd, qt = n // 2, n % 2
                rows = small[:, 544 + 8 * n:552 + 8 * n]
                step(V.scalar_tensor_tensor(out=rows, in0=rows, scalar=C("cmp_any", qt, 1),
                                            in1=small[:, 64 + qt * 48 + odd * 3:64 + qt * 48 + odd * 3 + 43:6],
                                            op0=ALU.mult, op1=ALU.mult))
            sync()
            V.tensor_tensor(rows_of(pc), rows_of(pc), wide(small[:, 544:576]), ALU.mult).then_inc(cmp_probs, 1)
            dve.wait_ge(dup_ready, 2)
            V.tensor_copy(W(20, 8), banks(0, 4)).then_inc(dup_copied, 1)
            dve.wait_ge(v_turned, 5)
            V.tensor_copy(W(28, 4), banks(6, 2)).then_inc(v_copied, 1)
            dve.wait_ge(cmp_turned, 1)
            for n in range(4):
                ins = V.tensor_copy(r3(Wc(PCT[n // 2], 2048)[0:NCMP, :], 8)[:, :, (n % 2) * P:(n % 2 + 1) * P],
                                    banks(2 * n)[0:NCMP, :].rearrange("p (h t) -> p h t", h=8))
                if n < 3:
                    step(ins)
            ins.then_inc(cmp_ready, 1)
            softmax_dve("nsa", NSA_U, NSA_O, 64 ** -0.5, lambda qt: stage[:, qt * 256:(qt + 1) * 256], lambda g: (2 * g, 2))
            attention_whole(NSA_O + 8)
            proj_add("nsa_out", ALPHA)
            layer_norm(2, 16, last=True)
            dve.wait_ge(logits_ps, 1)
            link(V.tensor_copy(small[:, 448:464], ps[:, 0, 0:16]))
            for tt in range(2):
                step(V.max(small[:, 464 + 8 * tt:472 + 8 * tt], small[:, 448 + 8 * tt:456 + 8 * tt]))
            sync()
            for tt in range(2):
                step(V.max_index(idx[:, 8 * tt:8 * tt + 8], small[:, 464 + 8 * tt:472 + 8 * tt], small[:, 448 + 8 * tt:456 + 8 * tt]))
            sync()
            step(V.tensor_copy(small[:, 480:496], idx[:, :]))
            V.tensor_tensor(small[:, 504:506], small[:, 465:474:8], small[:, 464:473:8], ALU.subtract).then_inc(top2_diff, 1)
            sync()
            dve.wait_ge(top2_exp, 1)
            link(V.tensor_scalar(small[:, 506:508], small[:, 504:506], 1.0, None, ALU.add))
            link(V.reciprocal(small[:, 506:508], small[:, 506:508]))
            link(V.tensor_tensor(small[:, 508:510], small[:, 504:506], small[:, 506:508], ALU.mult))
            for tt in range(2):
                link(V.tensor_scalar(small[:, 576 + 8 * tt:584 + 8 * tt], C("iota8"), small[:, 480 + 8 * tt:481 + 8 * tt],
                                     small[:, 506 + tt:507 + tt], ALU.is_equal, ALU.mult))
                link(V.tensor_scalar(small[:, 592 + 8 * tt:600 + 8 * tt], C("iota8"), small[:, 481 + 8 * tt:482 + 8 * tt],
                                     small[:, 508 + tt:509 + tt], ALU.is_equal, ALU.mult))
            link(V.tensor_tensor(small[:, 576:592], small[:, 576:592], small[:, 592:608], ALU.add))
            V.tensor_scalar(small[:, 608:624], small[:, 576:592], 0.0, None, ALU.is_gt).then_inc(picked, 1)
            dve.wait_ge(counts_ps, 1)
            step(V.tensor_reduce(small[:, 472:473], ps[:, 1, 16:24], AX, ALU.max))
            dve.wait_ge(picked, 1)
            step(V.tensor_tensor(small[:, 448:464], ps[:, 1, 0:16], small[:, 608:624], ALU.mult))
            sync()
            V.tensor_scalar(few[:, :], small[:, 472:473], float(P), None, ALU.is_le).then_inc(few_ready, 1)
            gu = PHASES["moe_gu"]
            with dve.If(few_flag(dve)):
                for n in range(16):
                    e, tt = n // 2, n % 2
                    at = FEW_TAKE + n * P
                    V.tensor_scalar(work[:, at:at + P], C("places"), small[:, 448 + tt * 8 + e:449 + tt * 8 + e], None, ALU.is_equal)
                    ins = V.tensor_scalar(FEW_WEIGHT[:, n * P:(n + 1) * P], C("places"), small[:, 448 + tt * 8 + e:449 + tt * 8 + e],
                                          small[:, 576 + tt * 8 + e:577 + tt * 8 + e], ALU.is_equal, ALU.mult)
                ins.then_inc(places_built, 1)
                dve.wait_ge(gathered_ps, 1)
                V.tensor_copy(FEW_X, banks(5)).then_inc(gathered, 1)
                dve.wait_ge(x_turned, 1)
                V.tensor_scalar(x[:, :], x[:, :], ALPHA, None, ALU.mult).then_inc(y_added, 1)

                def few_expert(e, more):
                    with dve.Fori(0, 2) as part:
                        half = e * 2 + part

                        def body(i, k, s):
                            bank = (gu.g + k) % DEPTH
                            at = slice(s * P, (s + 1) * P) if isinstance(s, int) else bass.ds(s * P, P)
                            dve.wait_ge(gate_act, s + (gu.a + 1) + half * HALF)
                            V.tensor_tensor(work[:, at], Wc(FEW_GATE + P * bank, P), ps[:, bank, P:2 * P],
                                            ALU.mult).then_inc(act_ready, 1)

                        slot_loop(dve, gu, body)
                    dve.wait_ge(y_ready, e + 1)
                    V.tensor_copy(FEW_Y, banks(3)).then_inc(y_kept, 1)
                    if more:
                        dve.wait_ge(gathered_ps, e + 2)
                        V.tensor_copy(FEW_X, banks(5)).then_inc(gathered, 1)
                    dve.wait_ge(spread_out, e + 1)
                    dve.wait_ge(y_added, e + 1)
                    V.tensor_tensor(x[:, :], x[:, :], banks(3, 4), ALU.add).then_inc(y_added, 1)

                with dve.Fori(0, EXPERTS - 1) as e:
                    few_expert(e, True)
                few_expert(EXPERTS - 1, False)
                dve.wait_ge(y_added, EXPERTS + 1)
                V.memset(small[:, 638:639], 0.0).then_inc(acc_drained, QUARTERS)
            with dve.Else():
                split_h(x)
                for tt in range(2):
                    ins = V.tensor_tensor(r3(Wc(tt * 1024, 1024), 8), C("ident").unsqueeze(1).to_broadcast([P, 8, P]),
                                          small[:, 576 + 8 * tt:584 + 8 * tt].unsqueeze(2).to_broadcast([P, 8, P]), ALU.mult)
                    if tt == 0:
                        step(ins)
                ins.then_inc(cw_diag, 1)
                dve.wait_ge(cw_ps, 1)
                cw = W(16, 8)
                for tt in range(2):
                    ins = V.tensor_copy(r3(cw, 8)[:, :, tt * P:(tt + 1) * P], r3(banks(2 * tt), 8))
                    if tt == 0:
                        step(ins)
                ins.then_inc(cw_ready, 1)
                dve.wait_ge(cw_ready, 1)
                c0 = chain[0]
                with dve.Fori(0, EXPERTS) as e:
                    with dve.Fori(0, 2) as part:
                        half = e * 2 + part

                        def body(i, k, s):
                            bank = (gu.g + k) % DEPTH
                            f = Wc(1536 + 256 * bank, 256)
                            chain[0] = s * 2 + c0 + half * (2 * HALF)
                            dve.wait_ge(gate_act, s + (gu.a + 1) + half * HALF)
                            V.tensor_tensor(f, Wc(512 * bank, BLK), ps[:, bank, BLK:2 * BLK], ALU.mult).then_inc(banks_drained, 1)
                            dve.wait_ge(banks_drained, s + (gu.e + 1) + half * HALF)
                            link(V.tensor_tensor(f, f, work[:, bass.ds(e * BLK + 16 * BLK, BLK)], ALU.mult))
                            split_act(s, f)

                        slot_loop(dve, gu, body)
                dve.wait_ge(acc_ready, 4)
                for c in range(QUARTERS):
                    V.scalar_tensor_tensor(out=xs(c), in0=xs(c), scalar=ALPHA, in1=ps[:, 3 + c, :], op0=ALU.mult,
                                           op1=ALU.add).then_inc(acc_drained, 1)
            dve.wait_ge(acc_drained, QUARTERS * 4)
            chain[0], order[0] = 0, last_step
            layer_norm(3, 24, last=True)


SINK_ORDER = [0, 2, 1, 3, 4, 6, 5, 7]


def _block_slots(m):
    k, n = m.shape
    b = m.reshape(k // P, P, n // P, P).transpose(1, 2, 0, 3)
    return b.reshape(P, n // P // 2, SLOT).transpose(1, 0, 2)


def _gu_slots(m):
    k, n = m.shape
    b = m.reshape(k // P, P, 2, n // P // 2, P).transpose(3, 1, 2, 0, 4)
    return b.reshape(n // P // 2, P, SLOT)


def _down_slots(m):
    k, n = m.shape
    b = m.reshape(k // P // 2, 2, P, n // P, P).transpose(0, 2, 1, 3, 4)
    return b.reshape(k // P // 2, P, SLOT)


def _ffn_slots(gu, down):
    g, d = _gu_slots(gu), _down_slots(down)
    parts = []
    for a in range(0, g.shape[0], HALF):
        b = min(a + HALF, g.shape[0])
        parts += [g[a:b], d[a // 2:b // 2]]
    return parts


def _columns(v):
    return v.reshape(-1, P).T


def _channel_major(a):
    return a.reshape(T, NB, P).transpose(2, 1, 0).reshape(P, NB * T)


def _constants():
    i = np.arange(P)
    freq = (np.float32(10000.0) ** (-np.arange(0, 64, 2, dtype=np.float32) / np.float32(64))).astype(np.float32)
    lane = freq[i % 32][:, None]
    rot = np.zeros((P, P), np.float32)
    first = (i % 64) < 32
    rot[i[first] + 32, i[first]] = -1.0
    rot[i[~first] - 32, i[~first]] = 1.0
    cend = 16 * np.arange(NCMP, dtype=np.float32) + 31
    t = np.arange(T)
    cmp_valid = (16 * np.arange(NCMP)[None] + 31) <= t[:, None]
    c = {
        "ident": np.eye(P), "ones": np.ones((P, P)), "ones64": (i[:, None] // 64 == i[None] // 64), "rot": rot,
        "dup0": i[:, None] == (i[None] % 64), "dup1": i[:, None] == 64 + (i[None] % 64),
        "ge": i[:, None] >= i[None], "invf": lane, "eps6": np.full((P, 1), 1e-6), "eps5": np.full((P, 1), 1e-5),
        "cend_cos": np.cos(lane * cend[None]), "cend_sin": np.sin(lane * cend[None]),
        "cmp_mask": np.where(cmp_valid, 0.0, MASKED).reshape(2, P, NCMP).transpose(1, 0, 2).reshape(P, 30),
        "cmp_any": cmp_valid.any(1).reshape(2, P).T, "iota8": np.broadcast_to(np.arange(8), (P, 8)),
        "places": np.broadcast_to(np.arange(1, P + 1), (P, P)),
    }
    consts = np.concatenate([np.asarray(c[n], np.float32) for n in CONST], 1)
    q, k = t[:, None], t[None]
    swa = (k <= q) & (k + P > q)
    by_query = lambda m: np.where(m, 0.0, MASKED).reshape(2, P, T).transpose(1, 0, 2).reshape(P, 512)
    attn = np.concatenate([by_query(swa), by_query(k > q)], 1)
    levels = [np.eye(P)]
    for lv in range(1, HG_LEVELS + 1):
        half = P >> lv
        s_, t_ = i[:, None], i[None]
        levels.append((s_ // (2 * half) == t_ // (2 * half)) & (s_ % (2 * half) < half) & (t_ % (2 * half) >= half))
    pool = np.concatenate([np.broadcast_to(1.0 / np.minimum(t + 1, w), (P, T)) for w in (2, 4, 8, 16)], 1)
    ang = lane * t[None].astype(np.float32)
    nsa = np.concatenate([by_query(k <= q), np.cos(ang), np.sin(ang)], 1)
    stages = [attn, np.concatenate(levels, 1), pool, nsa]
    return consts, np.stack([np.asarray(s, np.float32) for s in stages])


def _stream(v):
    parts = [_block_slots(v["ab_w_in"][0]), _block_slots(v["ab_w_out"][0])]
    for layer in range(2):
        if layer == 1:
            parts += [_block_slots(v["hgrn_w_in"][0]), _block_slots(v["hgrn_w_out"][0])]
        parts += [_block_slots(v["xa_w_kv"][layer]), _block_slots(v["xa_w_q"][layer]), _block_slots(v["xa_w_o"][layer])]
        parts += _ffn_slots(v["ffn_w_up"][layer], v["ffn_w_down"][layer])
    parts += [v["pool_w_2"][0].reshape(4, 2, P, 2, P).transpose(2, 0, 3, 1, 4).reshape(1, P, SLOT)]
    parts += _ffn_slots(v["ffn_w_gu_2"][0], v["ffn_w_down_2"][0])
    parts += [_block_slots(v["nsa_w_in_2"][0][:, :20 * P]), _block_slots(v["nsa_w_out_2"][0])]
    for e in range(EXPERTS):
        parts += _ffn_slots(v["moe_w_gu_2"][0, e], v["moe_w_down_2"][0, e])
    parts += [np.zeros((DEPTH, P, SLOT), np.float32)]
    return np.concatenate(parts)


def kernel(**inputs):
    import concourse.bacc as bacc
    from concourse.bass_utils import run_bass_kernel_spmd

    v = {k: np.asarray(a) for k, a in inputs.items()}
    stream = _stream(v)
    twice = lambda a: np.concatenate([a, a], -1)
    p = {
        "norm_mix": _columns(v["norm_mix"]), "norm_cross": _columns(v["norm_cross"]), "norm_mem": _columns(v["norm_mem"]),
        "norm_ffn": _columns(v["norm_ffn"]), "swa_q": _columns(twice(v["swa_q_norm"][0])), "swa_k": _columns(twice(v["swa_k_norm"][0])),
        "sinks": np.broadcast_to(v["swa_sinks"][0][SINK_ORDER], (P, 8)), "o_norm": _columns(v["hgrn_o_norm"][0]), "lb": _columns(v["hgrn_lb"]),
        "xa_q": _columns(v["xa_q_norm"]), "xa_k": _columns(v["xa_k_norm"]), "conv_w": _columns(v["ffn_conv_w"]),
        "conv_b": _columns(v["ffn_conv_b"]), "ln_g": _columns(v["ln_g_2"]), "ln_b": _columns(v["ln_b_2"]),
        "pool_scale": _columns(v["pool_scale_2"][0]),
        "router": v["moe_router_2"][0].reshape(NB, P, 8).transpose(1, 0, 2).reshape(P, 64),
        "pe_k": _columns(v["nsa_pe_k_2"][0]), "pe_v": _columns(v["nsa_pe_v_2"][0]),
        "w2_k": twice(v["nsa_w2_k_2"][0]), "w2_v": v["nsa_w2_v_2"][0],
    }
    params = np.concatenate([p[n] for n in PARAM], 1)
    w1 = [v[n][0].reshape(16, P, P).transpose(1, 0, 2).reshape(P, 2048) for n in ("nsa_w1_k_2", "nsa_w1_v_2")]
    gates = v["nsa_w_in_2"][0][:, 20 * P:].reshape(NB, P, 48).transpose(1, 0, 2).reshape(P, 384)
    consts, stages = _constants()
    arrays = {
        "stream": stream, "x_in": _channel_major(v["x"][0]), "mem_in": _channel_major(v["mem"][0]),
        "pos_in": np.broadcast_to(v["positions"][0], (P, T)), "params": params, "consts": consts, "stage_consts": stages,
        "w1_in": np.concatenate(w1 + [gates], 1),
    }
    arrays = {k: np.ascontiguousarray(a) for k, a in arrays.items()}
    nc = bacc.Bacc("TRN2", target_bir_lowering=False, num_devices=1)
    args = [nc.dram_tensor(k, a.shape, mybir.dt.from_np(a.dtype), kind="ExternalInput").ap() for k, a in arrays.items()]
    out = nc.dram_tensor("out", (P, NB * T), F32, kind="ExternalOutput").ap()
    build(nc, *args, out)
    r = run_bass_kernel_spmd(nc, [arrays], core_ids=[0])
    got = r.results[0]["out"]
    return got.reshape(P, NB, T).transpose(2, 1, 0).reshape(1, T, D)
```

```python
from contextlib import ExitStack

import concourse.bass as bass
import numpy as np
from concourse import mybir

F32 = mybir.dt.float32
F32R = mybir.dt.float32r
I32 = mybir.dt.int32
U32 = mybir.dt.uint32
ALU = mybir.AluOpType
ACT = mybir.ActivationFunctionType
AX = mybir.AxisListType.X

P = 128
T = 256
D = 1024
NB = D // P
BLK = T
SLOT = 16 * P
QUARTERS = 4
DEPTH = 3
FF = 22
MOE_FF = 28
EXPERTS = 8
HALF = MOE_FF // 2
ALPHA = 4.0 ** 0.25
NCMP = 15
MASKED = -1.0e30
HG_LEVELS = 7
ROUND = 1.5 * 2.0 ** 23
_C1 = 6.28125
_C2 = round((2.0 * np.pi - _C1) * 2.0 ** 20) / 2.0 ** 20
TWO_PI = (_C1, _C2, 2.0 * np.pi - _C1 - _C2)
PI = 3.1415925


class Phase:

    def __init__(self, name, kind, n, g, e, a):
        self.name, self.kind, self.n, self.g, self.e, self.a = name, kind, n, g, e, a


def plan():
    phases, g, e, a = {}, 0, 0, 0
    ffn = [("gu", HALF), ("down", HALF // 2), ("gu", FF - HALF), ("down", (FF - HALF) // 2)]
    order = [("ab_in", "proj", 9), ("ab_out", "proj", 4)]
    for layer in range(2):
        if layer == 1:
            order += [("hg_in", "proj", 16), ("hg_out", "proj", 4)]
        order += [(f"kv{layer}", "proj", 8), (f"q{layer}", "proj", 4), (f"o{layer}", "proj", 4)]
        order += [(f"ffn{layer}_{i}", k, n) for i, (k, n) in enumerate(ffn)]
    order += [("pool", "pool", 1)]
    order += [(f"ffn2_{i}", k, n) for i, (k, n) in enumerate(ffn)]
    order += [("nsa_in", "proj", 10), ("nsa_out", "proj", 4)]
    order += [("moe_gu", "gu", HALF), ("moe_down", "down", HALF // 2)]
    for name, kind, n in order:
        phases[name] = Phase(name, kind, n, g, e, a)
        g += n
        if kind != "down":
            e += n
        if kind == "gu":
            a += n
    per_half = HALF + HALF // 2
    total = phases["moe_gu"].g + 2 * EXPERTS * per_half
    return phases, per_half, total


PHASES, PER_HALF, SLOTS = plan()
LO_CUT = 12 * P
STREAM = SLOTS + DEPTH

CONST = {}
_at = 0
for _name, _n in [("ident", 128), ("ones", 128), ("ones64", 128), ("rot", 128), ("dup0", 128), ("dup1", 128),
                  ("ge", 128), ("invf", 1), ("eps6", 1), ("eps5", 1), ("cend_cos", 15), ("cend_sin", 15), ("cmp_mask", 30),
                  ("cmp_any", 2), ("iota8", 8), ("places", 128)]:
    CONST[_name] = (_at, _n)
    _at += _n
N_CONST = _at
STAGE = {"attn": 0, "hgrn": 1, "pool": 2, "nsa": 3}
PARAM = {}
_at = 0
for _name, _n in [("norm_mix", 16), ("norm_cross", 16), ("norm_mem", 16), ("norm_ffn", 16), ("swa_q", 1),
                  ("swa_k", 1), ("sinks", 8), ("o_norm", 1), ("lb", 16), ("xa_q", 4), ("xa_k", 4),
                  ("conv_w", 264), ("conv_b", 88), ("ln_g", 32), ("ln_b", 32), ("pool_scale", 8),
                  ("router", 64), ("pe_k", 16), ("pe_v", 16), ("w2_k", 128), ("w2_v", 64)]:
    PARAM[_name] = (_at, _n)
    _at += _n
N_PARAM = _at


def build(nc, stream, x_in, mem_in, pos_in, params, consts, stage_consts, w1_in, out):
    ctx = ExitStack()
    with ctx:
        def sb(name, cols, dt=F32):
            return ctx.enter_context(nc.sbuf_tensor(name, [P, cols], dt))

        def sem(name):
            return ctx.enter_context(nc.semaphore(name))

        raw = [sb(f"raw{i}", SLOT) for i in range(DEPTH)]
        whi = [sb(f"whi{i}", SLOT, F32R) for i in range(DEPTH)]
        wlo = [sb(f"wlo{i}", SLOT, F32R) for i in range(DEPTH)]
        x = sb("x", NB * BLK)
        hh = sb("hh", NB * BLK, F32R)
        hl = sb("hl", NB * BLK, F32R)
        ahi = sb("ahi", HALF * BLK, F32R)
        alo = sb("alo", HALF * BLK, F32R)
        hf = sb("hf", NB * BLK)
        rstd = sb("rstd", BLK)
        const = sb("const", N_CONST)
        par = sb("par", N_PARAM)
        stage = sb("stage", 1024)
        zero = sb("zero", P, F32R)
        small = sb("small", 640)
        idx = sb("idx", 16, U32)
        pool_mark = sb("pool_mark", DEPTH)
        few = sb("few", 1, I32)
        work = sb("work", 60 * BLK)
        ps = ctx.enter_context(nc.psum_tensor("ps", [P, 8, 512], F32))

        def C(name, a=0, n=None):
            at, size = CONST[name]
            return const[:, at + a:at + (size if n is None else a + n)]

        def R(name, a=0, n=1):
            return par[:, PARAM[name][0] + a:PARAM[name][0] + a + n]

        def W(block, n=1):
            return work[:, block * BLK:(block + n) * BLK]

        def Wc(col, n):
            return work[:, col:col + n]

        def xb(b, n=1):
            return x[:, b * BLK:(b + n) * BLK]

        def banks(b, n=2):
            return ps[:, b:b + n, :].rearrange("p b c -> p (b c)")

        def r3(ap, b):
            return ap.rearrange("p (b c) -> p b c", b=b)

        raw_loaded = [sem(f"raw_loaded{i}") for i in range(DEPTH)]
        hi_ready = sem("hi_ready")
        lo_ready = sem("lo_ready")
        slot_used = sem("slot_used")
        banks_drained = sem("banks_drained")
        gate_act = sem("gate_act")
        act_ready = sem("act_ready")
        acc_ready = sem("acc_ready")
        acc_drained = sem("acc_drained")
        dve_step = sem("dve_step")
        act_step = sem("act_step")
        last_step = sem("last_step")
        params_loaded = sem("params_loaded")
        x_loaded = sem("x_loaded")
        positions_loaded = sem("positions_loaded")
        stage_loaded = sem("stage_loaded")
        mem_loaded = sem("mem_loaded")
        w1_loaded = sem("w1_loaded")
        angles_ready = sem("angles_ready")
        sines_ready = sem("sines_ready")
        zero_ready = sem("zero_ready")
        out_stored = sem("out_stored")
        squares_ready = sem("squares_ready")
        sums_ready = sem("sums_ready")
        rstd_ready = sem("rstd_ready")
        mean_ready = sem("mean_ready")
        x_ready = sem("x_ready")
        h_ready = sem("h_ready")
        pool_ps = sem("pool_ps")
        pool_added = sem("pool_added")
        head_sq = sem("head_sq")
        head_sums = sem("head_sums")
        head_rstd = sem("head_rstd")
        rope_in = sem("rope_in")
        xa_squares = sem("xa_squares")
        xa_sums = sem("xa_sums")
        xa_rstd = sem("xa_rstd")
        rope_rot = sem("rope_rot")
        heads_ready = sem("heads_ready")
        dup_ready = sem("dup_ready")
        dup_copied = sem("dup_copied")
        v_turned = sem("v_turned")
        v_copied = sem("v_copied")
        scores_ready = sem("scores_ready")
        scores_masked = sem("scores_masked")
        negmax_ready = sem("negmax_ready")
        exp_done = sem("exp_done")
        probs_ready = sem("probs_ready")
        pt_ready = sem("pt_ready")
        pt_copied = sem("pt_copied")
        pv_done = sem("pv_done")
        o_drained = sem("o_drained")
        z_ready = sem("z_ready")
        z_masked = sem("z_masked")
        soft_ready = sem("soft_ready")
        sp_ready = sem("sp_ready")
        cs_ready = sem("cs_ready")
        d_ready = sem("d_ready")
        a_ready = sem("a_ready")
        sb_pv_done = sem("sb_pv_done")
        hg_lb = sem("hg_lb")
        hg_lb_exp = sem("hg_lb_exp")
        hg_sig = sem("hg_sig")
        hg_kf = sem("hg_kf")
        hg_log = sem("hg_log")
        hg_d = sem("hg_d")
        hg_e = sem("hg_e")
        hg_x = sem("hg_x")
        hg_s = sem("hg_s")
        hg_a = sem("hg_a")
        hg_o = sem("hg_o")
        hg_osq = sem("hg_osq")
        hg_gate = sem("hg_gate")
        hg_osum = sem("hg_osum")
        hg_orstd = sem("hg_orstd")
        gates_ps = sem("gates_ps")
        gates_ready = sem("gates_ready")
        cmp_dup = sem("cmp_dup")
        cmp_cols = sem("cmp_cols")
        cmp_hidden = sem("cmp_hidden")
        cmp_bias = sem("cmp_bias")
        cmp_silu = sem("cmp_silu")
        cmp_kv = sem("cmp_kv")
        cmp_kv_copied = sem("cmp_kv_copied")
        cmp_rot = sem("cmp_rot")
        cmp_roped = sem("cmp_roped")
        cmp_scores = sem("cmp_scores")
        cmp_shifted = sem("cmp_shifted")
        cmp_exp = sem("cmp_exp")
        cmp_probs = sem("cmp_probs")
        cmp_turned = sem("cmp_turned")
        cmp_ready = sem("cmp_ready")
        logits_t = sem("logits_t")
        logits_kept = sem("logits_kept")
        logits_ps = sem("logits_ps")
        top2_diff = sem("top2_diff")
        top2_exp = sem("top2_exp")
        cw_diag = sem("cw_diag")
        cw_ps = sem("cw_ps")
        cw_ready = sem("cw_ready")

        few_lo = [sem(f"few_lo{i}") for i in range(DEPTH)]
        few_tok = sem("few_tok")
        few_turned = sem("few_turned")
        few_act_hi = sem("few_act_hi")
        few_x_hi = sem("few_x_hi")
        picked = sem("picked")
        counts_ps = sem("counts_ps")
        few_ready = sem("few_ready")
        x_turned = sem("x_turned")
        x_tokens = sem("x_tokens")
        places_built = sem("places_built")
        spread_ps = sem("spread_ps")
        spread_ready = sem("spread_ready")
        gathered_ps = sem("gathered_ps")
        gathered = sem("gathered")
        y_ready = sem("y_ready")
        y_kept = sem("y_kept")
        spread_out = sem("spread_out")
        y_added = sem("y_added")

        block = ctx.enter_context(nc.Block())

        def few_act(t, n):
            return t[:, n * P:(n + 1) * P]

        FEW_TOK_ACT = 8 * BLK
        FEW_Y = Wc(3072, 1024)
        FEW_TAKE = 24 * BLK
        FEW_WEIGHT = Wc(32 * BLK, 2048)
        FEW_GIVE = 40 * BLK
        FEW_TOK = Wc(48 * BLK, 2048)
        SPREAD_AT = [(3 + n // 4 if n < 8 else (2 if n < 12 else 7), (n % 4) * P) for n in range(16)]
        FEW_GATE = 56 * BLK

        SWA_U, XA_U, NSA_U = 0, (4, 6), 8
        SWA_O, SB_O, XA_O, NSA_O = 0, 4, (8, 10), 12
        PROBS = [Wc(10752, 1024), Wc(11776, 1024), hf[:, 0:1024]]
        MEAN_BANK = (4, 0, 3, 0)
        STATS = (0, 32, 576)
        PT = [Wc(12800 + 1024 * i, 1024) for i in range(2)]
        ROPED = (0, 2, 4, 6, 12, 16)
        ROPE_BANK = (3, 4, 5, 6, 0, 1)
        CMP_GROUPS = 7
        CMP_COLS = (20 * BLK, 24 * BLK)
        PCT = (2048, 8192)
        HG_D = [W(16, 8), hf[:, :]]
        SB_T = [Wc(4608 + 1024 * i, 1024) for i in range(2)]

        def place(kind, h):
            return h if kind == "xa" else (h % 2) * 2 + h // 2

        def key_tiles(kind, qt):
            return 1 if kind != "xa" and qt == 0 else 2

        def units(kind):
            if kind == "swa":
                return [(g, qt, 0) for g in range(2) for qt in range(2)]
            if kind == "nsa":
                return [(g, qt, br) for g in range(4) for qt in range(2) for br in range(2)]
            return [(0, qt, 0) for qt in range(2)]

        def slot_loop(eng, ph, body, n=None, peel=0):
            n = ph.n if n is None else n
            rounds = n // DEPTH
            for i in range(min(peel, rounds)):
                for k in range(DEPTH):
                    body(i, k, DEPTH * i + k)
            if rounds - peel > 1:
                with eng.Fori(peel, rounds) as i:
                    for k in range(DEPTH):
                        body(i, k, i * DEPTH + k)
            elif rounds - peel == 1:
                for k in range(DEPTH):
                    body(peel, k, DEPTH * peel + k)
            for s in range(DEPTH * rounds, n):
                body(rounds, s - DEPTH * rounds, s)

        def straight(then):
            return 0 if then is None else max(then) // DEPTH + 1

        def at_least(eng, s, value):
            if not (isinstance(value, int) and value <= 0):
                eng.wait_ge(s, value)

        def few_flag(eng):
            eng.wait_ge(few_ready, 1)
            return eng.value_load(few[0:1, 0:1]) > 0

        @block.sync
        def _(sp):
            sp.dma_start(x[:, :], x_in).then_inc(x_loaded, 16)
            sp.dma_start(const[:, :], consts).then_inc(params_loaded, 16)
            sp.dma_start(par[:, :], params).then_inc(params_loaded, 16)
            sp.dma_start(Wc(10752, 256).bitcast(I32), pos_in).then_inc(positions_loaded, 16)
            for k in range(DEPTH):
                sp.dma_start(raw[k][:, :], stream[k]).then_inc(raw_loaded[k], 16)

            def load(i, k, s):
                sp.wait_ge(lo_ready, s + 1)
                sp.dma_start(raw[k][:, :], stream[s + DEPTH]).then_inc(raw_loaded[k], 16)

            first = PHASES["moe_gu"].g
            slot_loop(sp, None, load, n=first)
            with sp.If(few_flag(sp)):
                def load_few(i, k, s):
                    p = (first + k) % DEPTH
                    sp.wait_ge(few_lo[p], i * 2 + 2)
                    sp.dma_start(raw[p][:, :], stream[s + (first + DEPTH)]).then_inc(raw_loaded[p], 16)

                slot_loop(sp, None, load_few, n=SLOTS - first)
            with sp.Else():
                def load_all(i, k, s):
                    p = (first + k) % DEPTH
                    sp.wait_ge(lo_ready, s + (first + 1))
                    sp.dma_start(raw[p][:, :], stream[s + (first + DEPTH)]).then_inc(raw_loaded[p], 16)

                slot_loop(sp, None, load_all, n=SLOTS - first)
            for c in range(QUARTERS):
                sp.wait_ge(x_ready, QUARTERS * 3 + c + 1)
                sp.dma_start(out[:, c * 512:(c + 1) * 512], x[:, c * 512:(c + 1) * 512]).then_inc(out_stored, 16)
            sp.wait_ge(out_stored, 16 * QUARTERS)

        @block.gpsimd
        def _(pool):
            def split_lo(k, s, first):
                p = (first + k) % DEPTH
                pool.wait_ge(hi_ready, s + (first + 1))
                nc.gpsimd.tensor_tensor(wlo[p][:, :], raw[p][:, :], whi[p][:, :].bitcast(F32),
                                        ALU.subtract).then_inc(lo_ready, 1)

            moe = PHASES["moe_gu"].g
            first = moe + DEPTH
            slot_loop(pool, None, lambda i, k, s: split_lo(k, s, 0), n=first)
            with pool.If(few_flag(pool)):
                for p in range(DEPTH):
                    pool.wait_ge(lo_ready, first)
                    nc.gpsimd.memset(pool_mark[:, p:p + 1], 0.0).then_inc(few_lo[p], 2)
                def split_few(i, k, s):
                    p = (moe + k) % DEPTH
                    pool.wait_ge(hi_ready, s + (first + 1))
                    own = slice(LO_CUT, SLOT)
                    nc.gpsimd.tensor_tensor(wlo[p][:, own], raw[p][:, own], whi[p][:, own].bitcast(F32),
                                            ALU.subtract).then_inc(few_lo[p], 1)

                slot_loop(pool, None, split_few, n=STREAM - first)
            with pool.Else():
                slot_loop(pool, None, lambda i, k, s: split_lo(k, s, first), n=STREAM - first)

        @block.scalar
        def _(act):
            chain = [0]

            def link(ins):
                chain[0] += 1
                ins.then_inc(act_step, 1)
                act.wait_ge(act_step, chain[0])

            def split_hi(ph, i, k, s, off=0):
                p = (ph.g + k) % DEPTH
                act.wait_ge(raw_loaded[p], i * 16 + (16 * ((ph.g + k) // DEPTH + 2) + off * 16))
                act.wait_ge(slot_used, s + (ph.g + 1) + off * DEPTH)
                nc.scalar.activation(whi[p][:, :], raw[p][:, :], ACT.Copy).then_inc(hi_ready, 1)

            def split_phase(name, then=None):
                ph = PHASES[name]

                def body(i, k, s):
                    split_hi(ph, i, k, s)
                    if then is not None and s in then:
                        then[s]()

                slot_loop(act, ph, body, peel=straight(then))

            def norm_act(n, count, eps):
                act.wait_ge(sums_ready, n + 1)
                link(nc.scalar.activation(rstd[:, :], ps[:, 7, 0:BLK], ACT.Ln, scale=1.0 / count, bias=eps_ap(eps)))
                nc.scalar.activation(rstd[:, :], rstd[:, :], ACT.Exp, scale=-0.5).then_inc(rstd_ready, 1)

            def eps_ap(eps):
                return C("eps6") if eps == 1e-6 else C("eps5")

            def softmax_act(kind, u0):
                us = units(kind)
                for step in range(len(us) + 2):
                    if step < len(us):
                        u = u0 + step
                        act.wait_ge(negmax_ready, u + 1)
                        probs, s0, nk = PROBS[u % 3], STATS[u % 3], P * key_tiles(kind, us[step][1])
                        if kind == "swa":
                            nc.scalar.activation(small[:, s0 + 12:s0 + 16], small[:, s0 + 8:s0 + 12], ACT.Exp)
                        for h in range(4):
                            ins = nc.scalar.activation(probs[:, h * 256:h * 256 + nk], probs[:, h * 256:h * 256 + nk],
                                                       ACT.Exp, bias=small[:, s0 + h:s0 + h + 1],
                                                       accum_out=small[:, s0 + 4 + h:s0 + 5 + h])
                        ins.then_inc(exp_done, 1)
                    if step >= 2:
                        u = u0 + step - 2
                        nk = P * key_tiles(kind, us[step - 2][1])
                        act.wait_ge(pt_ready, u + 1)
                        at_least(act, pv_done, u - 1)
                        nc.scalar.activation(r3(PT[u % 2], 4)[:, :, 0:nk], r3(banks(2), 4)[:, :, 0:nk], ACT.Copy).then_inc(pt_copied, 1)

            def ffn_act(layer, conv):
                for i in range(4):
                    ph = PHASES[f"ffn{layer}_{i}"]
                    if ph.kind == "down":
                        split_phase(ph.name)
                        continue

                    def body(i, k, s, ph=ph):
                        if conv:
                            gate = Wc(512 * ((ph.g + k) % DEPTH), BLK)
                            act.wait_ge(banks_drained, s + (ph.e + 1))
                            nc.scalar.activation(gate, gate, ACT.Silu).then_inc(gate_act, 1)
                        else:
                            silu_gate(ph, k, s)
                        split_hi(ph, i, k, s)

                    slot_loop(act, ph, body)

            def silu_gate(ph, k, s, off_g=0, off_a=0):
                bank = (ph.g + k) % DEPTH
                act.wait_ge(slot_used, s + (ph.g + 1) + off_g)
                act.wait_ge(act_ready, s + (ph.a - 2) + off_a)
                nc.scalar.activation(Wc(512 * bank, BLK), ps[:, bank, 0:BLK], ACT.Silu).then_inc(gate_act, 1)

            def xa_act(layer, before):
                act.wait_ge(h_ready, QUARTERS * (2 + 6 * layer))
                act.dma_start(W(24, 8), mem_in).then_inc(mem_loaded, 16)
                split_phase(before, {1: lambda: norm_act(layer * 4 + 1, D, 1e-6)})
                split_phase(f"kv{layer}", {1: lambda: norm_act(layer * 4 + 2, D, 1e-6)})

                def head_rstd_of(n, block, bank, banks_read):
                    act.wait_ge(xa_sums, 3 * layer + n)
                    r = W(block, 2 * banks_read)
                    link(nc.scalar.activation(r, banks(bank, banks_read), ACT.Ln, scale=1.0 / 256, bias=C("eps6")))
                    nc.scalar.activation(r, r, ACT.Exp, scale=-0.5).then_inc(xa_rstd, 1)

                split_phase(f"q{layer}", {1: lambda: head_rstd_of(1, 46, 4, 2), 2: lambda: head_rstd_of(2, 42, 6, 1),
                                          3: lambda: head_rstd_of(3, 44, 7, 1)})
                softmax_act("xa", XA_U[layer])
                split_phase(f"o{layer}")

            for k in range(DEPTH):
                act.wait_ge(raw_loaded[k], 16)
                nc.scalar.activation(whi[k][:, :], raw[k][:, :], ACT.Copy).then_inc(hi_ready, 1)
            act.dma_start(stage[:, :], stage_consts[STAGE["attn"]]).then_inc(stage_loaded, 16)
            act.wait_ge(angles_ready, 1)
            nc.scalar.activation(W(33, 2), W(33, 2), ACT.Sin).then_inc(sines_ready, 1)
            norm_act(0, D, 1e-6)

            def swa_rstd():
                act.wait_ge(head_sums, 1)
                link(nc.scalar.activation(W(23, 5), banks(3, 3)[:, 0:5 * BLK], ACT.Ln, scale=1.0 / 64, bias=C("eps6")))
                nc.scalar.activation(W(23, 5), W(23, 5), ACT.Exp, scale=-0.5).then_inc(head_rstd, 1)

            split_phase("ab_in", {3: swa_rstd})
            softmax_act("swa", SWA_U)
            for st in range(5):
                if st < 4:
                    u = st
                    act.wait_ge(z_masked, u + 1)
                    link(nc.scalar.activation(SB_T[u % 2], PROBS[u % 3], ACT.Abs))
                    link(nc.scalar.activation(SB_T[u % 2], SB_T[u % 2], ACT.Exp, scale=-1.0))
                    nc.scalar.activation(SB_T[u % 2], SB_T[u % 2], ACT.Ln, bias=1.0).then_inc(soft_ready, 1)
                if st >= 1:
                    u = st - 1
                    act.wait_ge(d_ready, u + 1)
                    at_least(act, sb_pv_done, u - 1)
                    nc.scalar.activation(PT[u % 2], PROBS[u % 3], ACT.Exp).then_inc(a_ready, 1)
            xa_act(0, "ab_out")
            norm_act(3, D, 1e-6)
            ffn_act(0, True)
            act.dma_start(stage[:, :], stage_consts[STAGE["hgrn"]]).then_inc(stage_loaded, 16)
            norm_act(4, D, 1e-6)
            act.wait_ge(hg_lb, 1)
            nc.scalar.activation(small[:, 416:432], small[:, 400:416], ACT.Exp).then_inc(hg_lb_exp, 1)
            e_hg = PHASES["hg_in"].e

            def gates_of_f():
                act.wait_ge(banks_drained, e_hg + 8)
                nc.scalar.activation(W(32, 8), W(8, 8), ACT.Sigmoid, scale=-1.0)
                nc.scalar.activation(W(8, 8), W(8, 8), ACT.Sigmoid).then_inc(hg_sig, 1)

            def log_decay():
                act.wait_ge(hg_kf, 1)
                nc.scalar.activation(W(8, 8), W(8, 8), ACT.Ln).then_inc(hg_log, 1)

            split_phase("hg_in", {8: gates_of_f, 10: log_decay})
            for lv in range(HG_LEVELS + 1):
                act.wait_ge(hg_d, lv + 1)
                if lv:
                    link(nc.scalar.activation(HG_D[lv % 2], HG_D[lv % 2], ACT.Abs))
                nc.scalar.activation(HG_D[lv % 2], HG_D[lv % 2], ACT.Exp, scale=-1.0 if lv else 1.0).then_inc(hg_e, 1)
            act.wait_ge(banks_drained, e_hg + 16)
            nc.scalar.activation(W(24, 8), W(24, 8), ACT.Silu).then_inc(hg_gate, 1)
            act.wait_ge(hg_osum, 1)
            link(nc.scalar.activation(W(8, 8), banks(4, 4), ACT.Ln, scale=1.0 / 128, bias=C("eps6")))
            nc.scalar.activation(W(8, 8), W(8, 8), ACT.Exp, scale=-0.5).then_inc(hg_orstd, 1)
            act.dma_start(stage[:, :], stage_consts[STAGE["pool"]]).then_inc(stage_loaded, 16)
            xa_act(1, "hg_out")
            norm_act(7, D, 1e-6)
            ffn_act(1, True)
            split_phase("pool")
            norm_act(8, D, 1e-5)
            act.dma_start(stage[:, :], stage_consts[STAGE["nsa"]]).then_inc(stage_loaded, 16)
            act.dma_start(Wc(8192, 4480), w1_in).then_inc(w1_loaded, 16)
            ffn_act(2, False)
            norm_act(9, D, 1e-5)

            def branch_gates():
                act.wait_ge(gates_ps, 1)
                nc.scalar.activation(small[:, 64:160], ps[:, 7, 0:96], ACT.Sigmoid).then_inc(gates_ready, 1)

            split_phase("nsa_in", {7: branch_gates})
            act.wait_ge(cmp_bias, 1)
            for br in range(2):
                ins = nc.scalar.activation(small[:, 160 + 60 * br:220 + 60 * br], ps[:, 7, 128 * br + 128:128 * br + 188],
                                           ACT.Silu, bias=small[:, 280 + br:281 + br])
            ins.then_inc(cmp_silu, 1)
            act.wait_ge(cmp_shifted, 1)
            nc.scalar.activation(Wc(10240, 480), Wc(10240, 480), ACT.Exp).then_inc(cmp_exp, 1)
            softmax_act("nsa", NSA_U)
            split_phase("nsa_out")
            norm_act(10, D, 1e-5)
            act.wait_ge(top2_diff, 1)
            nc.scalar.activation(small[:, 504:506], small[:, 504:506], ACT.Exp).then_inc(top2_exp, 1)
            gu, down = PHASES["moe_gu"], PHASES["moe_down"]
            act.wait_ge(x_turned, 1)
            nc.scalar.activation(FEW_TOK, banks(3, 4), ACT.Copy).then_inc(x_tokens, 1)

            def few_half(half):
                rounds = half * (PER_HALF // DEPTH)

                def body(i, k, s):
                    bank = (gu.g + k) % DEPTH
                    act.wait_ge(slot_used, s + (gu.g + 1) + half * PER_HALF)
                    act.wait_ge(few_tok, s + 1 + half * HALF)
                    nc.scalar.activation(Wc(FEW_GATE + P * bank, P), ps[:, bank, 0:P], ACT.Silu).then_inc(gate_act, 1)
                    split_hi(gu, i, k, s, rounds)

                slot_loop(act, gu, body, peel=HALF // DEPTH)
                slot_loop(act, down, lambda i, k, s: split_hi(down, i, k, s, rounds), peel=down.n // DEPTH)

            with act.If(few_flag(act)):
                for n, (col, bank, width) in enumerate(((0, 3, 2), (1024, 2, 1), (1536, 7, 1))):
                    act.wait_ge(spread_ps, n + 1)
                    nc.scalar.activation(Wc(FEW_GIVE + col, 512 * width), banks(bank, width), ACT.Copy).then_inc(spread_ready, 1)
                with act.Fori(0, 2 * EXPERTS) as half:
                    few_half(half)
            with act.Else():
                with act.Fori(0, EXPERTS) as e:
                    with act.Fori(0, 2) as part:
                        half = e * 2 + part
                        rounds = half * (PER_HALF // DEPTH)

                        def body(i, k, s):
                            silu_gate(gu, k, s, half * PER_HALF, half * HALF)
                            split_hi(gu, i, k, s, rounds)

                        slot_loop(act, gu, body)
                        slot_loop(act, down, lambda i, k, s: split_hi(down, i, k, s, rounds))
            norm_act(11, D, 1e-5)

        @block.tensor
        def _(pe):
            mm = nc.tensor.matmul

            def split_mm(out_ap, hi_w, lo_w, hi_x, lo_x, start, stop, **kw):
                mm(out_ap, hi_w, hi_x, start=start, stop=False, **kw)
                mm(out_ap, hi_w, lo_x, start=False, stop=False, **kw)
                return mm(out_ap, lo_w, hi_x, start=False, stop=stop, **kw)

            def proj_slot(ph, k, s, off_g=0, off_e=0, h=None):
                p = (ph.g + k) % DEPTH
                pe.wait_ge(lo_ready, s + (ph.g + 1) + off_g)
                at_least(pe, banks_drained, s + (ph.e - 2) + off_e)
                for b in range(2):
                    for c in range(NB):
                        if h is not None and isinstance(s, int) and s == 0 and b == 0 and c % 2 == 0:
                            pe.wait_ge(h_ready, QUARTERS * (h - 1) + c // 2 + 1)
                        w = slice((b * NB + c) * P, (b * NB + c + 1) * P)
                        m = slice(c * BLK, (c + 1) * BLK)
                        last = split_mm(ps[:, p, b * BLK:(b + 1) * BLK], whi[p][:, w], wlo[p][:, w],
                                        hh[:, m], hl[:, m], c == 0, c == NB - 1)
                last.then_inc(slot_used, 1)

            def proj_pe(name, h, then=None):
                ph = PHASES[name]

                def body(i, k, s):
                    proj_slot(ph, k, s, h=h)
                    if then is not None and s in then:
                        then[s]()

                slot_loop(pe, ph, body, peel=max(1, straight(then)))

            def down_slot(ph, k, s, act_at, off_g=0):
                p = (ph.g + k) % DEPTH
                pe.wait_ge(lo_ready, s + (ph.g + 1) + off_g)
                for c in range(2):
                    m = bass.ds(s * (2 * BLK) + c * BLK, BLK)
                    if isinstance(s, int):
                        m = slice((2 * s + c) * BLK, (2 * s + c + 1) * BLK)
                    pe.wait_ge(act_ready, act_at(s, c))
                    for b in range(NB):
                        w = slice((c * NB + b) * P, (c * NB + b + 1) * P)
                        last = split_mm(ps[:, 3 + b // 2, (b % 2) * BLK:(b % 2 + 1) * BLK], whi[p][:, w],
                                        wlo[p][:, w], ahi[:, m], alo[:, m], False, False, skip_group_check=True)
                last.then_inc(slot_used, 1)

            def acc_zero(start, stop):
                for b in range(4):
                    last = mm(ps[:, 3 + b, :], zero[:, :], zero[:, :].unsqueeze(1).to_broadcast([P, 4, P]), start=start, stop=stop,
                              skip_group_check=True)
                return last

            def sums_pe(src, bank, wait):
                for b in range(NB):
                    if b % 2 == 0:
                        wait(b // 2)
                    last = mm(ps[:, bank, 0:BLK], C("ones"), src[:, b * BLK:(b + 1) * BLK], start=(b == 0), stop=(b == NB - 1))
                return last

            def norm_pe(n):
                sums_pe(hf, 7, lambda c: pe.wait_ge(squares_ready, QUARTERS * n + c + 1)).then_inc(sums_ready, 1)

            def layer_norm_pe(i, wait):
                sums_pe(x, MEAN_BANK[i], wait).then_inc(mean_ready, 1)
                norm_pe(8 + i)

            def ffn_pe(layer, h):
                at_least(pe, acc_drained, QUARTERS * layer)
                for i in range(4):
                    ph = PHASES[f"ffn{layer}_{i}"]
                    if ph.kind == "gu":
                        slot_loop(pe, ph, lambda i, k, s: proj_slot(ph, k, s, h=h), peel=1 if i == 0 else 0)
                        a0 = ph.a
                    else:
                        if i == 1:
                            acc_zero(True, False)
                        slot_loop(pe, ph, lambda i, k, s: down_slot(ph, k, s, lambda s, c: s * 2 + (a0 + c + 1)))
                acc_zero(False, True).then_inc(acc_ready, 1)

            def turn(dst, src):
                return nc.tensor.transpose(dst, src, C("ident"))

            def softmax_pe(kind, u0, o0, q_at, k_at, v_at, cmp=None):
                us = units(kind)
                branches = 2 if kind == "nsa" else 1
                for step in range(len(us) + 3):
                    if step < len(us):
                        u = u0 + step
                        g, qt, br = us[step]
                        nk = P * key_tiles(kind, qt)
                        at_least(pe, scores_masked, u)
                        for h in range(4):
                            for last_c, (q, kk) in zip((False, True) if kind == "xa" else (True,), zip(q_at(g, h, qt), k_at(g, h, br))):
                                at = place(kind, h)
                                last = mm(ps[:, at // 2, (at % 2) * 256:(at % 2) * 256 + nk], q, kk[:, 0:nk],
                                          start=(not last_c or kind != "xa"), stop=last_c)
                        last.then_inc(scores_ready, 1)
                    if 2 <= step <= len(us) + 1:
                        u = u0 + step - 2
                        pe.wait_ge(probs_ready, u + 1)
                        at_least(pe, pt_copied, u)
                        for h in range(4):
                            for kt in range(key_tiles(kind, us[step - 2][1])):
                                n = h * 2 + kt
                                last = turn(ps[:, 2 + n // 4, (n % 4) * P:(n % 4 + 1) * P],
                                            PROBS[u % 3][:, h * 256 + kt * P:h * 256 + (kt + 1) * P])
                        last.then_inc(pt_ready, 1)
                    if step >= 3:
                        u = u0 + step - 3
                        g, qt, br = us[step - 3]
                        o = o0 + (step - 3) // branches
                        kts = key_tiles(kind, qt)
                        pe.wait_ge(pt_copied, u + 1)
                        if br == 0:
                            at_least(pe, o_drained, o - 1)
                        bank = 4 + 2 * (o % 2)
                        pt = PT[u % 2]
                        for h in range(4):
                            at = 2 * place(kind, h)
                            if kind == "xa":
                                for eb in range(2):
                                    n = 2 * h + eb
                                    for kt in range(2):
                                        last = mm(ps[:, bank + n // 4, (n % 4) * P:(n % 4 + 1) * P], v_at(g, h, kt, eb),
                                                  pt[:, (at + kt) * P:(at + kt + 1) * P], start=(kt == 0), stop=(kt == 1))
                                continue
                            half = 64 * (h % 2)
                            dst = ps[half:half + 64, bank, (h // 2) * P:(h // 2 + 1) * P]
                            fresh = h < 2
                            if cmp is not None and br == 0:
                                vc, pc = cmp(g, h, qt)
                                mm(dst, vc, pc, start=fresh, stop=False, skip_group_check=True)
                                fresh = False
                            for kt in range(kts):
                                last = mm(dst, v_at(g, h, kt, br), pt[:, (at + kt) * P:(at + kt + 1) * P],
                                          start=(fresh and kt == 0 and br == 0), stop=(kt == kts - 1 and br == branches - 1),
                                          skip_group_check=True)
                        last.then_inc(pv_done, 1)

            def xa_pe(layer, h):
                proj_pe(f"kv{layer}", h, {1: lambda: norm_pe(layer * 4 + 2)})

                def turn_values():
                    pe.wait_ge(banks_drained, PHASES[f"kv{layer}"].e + PHASES[f"kv{layer}"].n)
                    for tt in range(2):
                        for b in range(8):
                            n = tt * 8 + b
                            last = turn(ps[:, 4 + n // 4, (n % 4) * P:(n % 4 + 1) * P], W(8 + b)[:, tt * P:(tt + 1) * P])
                    last.then_inc(v_turned, 1)

                def head_sums_of(squares_at, src, heads, bank):
                    pe.wait_ge(xa_squares, 5 * layer + squares_at)
                    for n in heads:
                        for b in range(2):
                            last = mm(ps[:, bank + n // 2, (n % 2) * 256:(n % 2 + 1) * 256], C("ones"),
                                      src[:, (2 * n + b) * BLK:(2 * n + b + 1) * BLK], start=(b == 0), stop=(b == 1))
                    last.then_inc(xa_sums, 1)

                def key_sums():
                    pe.wait_ge(v_copied, 2 + 2 * layer)
                    head_sums_of(1, W(32, 8), range(4), 4)

                proj_pe(f"q{layer}", h + 1, {0: turn_values, 1: key_sums,
                                             2: lambda: head_sums_of(3, hf, (0, 1), 6),
                                             3: lambda: head_sums_of(5, hf, (2, 3), 6)})
                pe.wait_ge(heads_ready, 2 + layer)
                softmax_pe("xa", XA_U[layer], XA_O[layer],
                           lambda g, h, qt: [W(16 + 2 * h + c)[:, qt * P:(qt + 1) * P] for c in range(2)],
                           lambda g, h, br: [W(2 * h + c) for c in range(2)],
                           lambda g, h, kt, eb: Wc(6144 + kt * 1024 + (2 * h + eb) * P, P))
                proj_pe(f"o{layer}", h + 2)

            pe.wait_ge(params_loaded, 32)
            pe.wait_ge(zero_ready, 1)
            norm_pe(0)

            def swa_sums():
                pe.wait_ge(head_sq, 1)
                for b in range(5):
                    last = mm(ps[:, 3 + b // 2, (b % 2) * 256:(b % 2 + 1) * 256], C("ones64"), W(18 + b), start=True, stop=True)
                last.then_inc(head_sums, 1)

            def swa_half_turns():
                pe.wait_ge(rope_in, 1)
                for b in range(5):
                    last = mm(ps[:, 3 + b // 2, (b % 2) * 256:(b % 2 + 1) * 256], C("rot"), W(b), start=True, stop=True)
                last.then_inc(rope_rot, 1)

            def swa_key_copies():
                pe.wait_ge(heads_ready, 1)
                for g in range(2):
                    last = mm(ps[:, 3, g * 256:(g + 1) * 256], C(f"dup{g}"), W(4), start=True, stop=True)
                last.then_inc(dup_ready, 1)

            proj_pe("ab_in", 1, {3: swa_sums, 5: swa_half_turns, 7: swa_key_copies})
            pe.wait_ge(banks_drained, PHASES["ab_in"].e + PHASES["ab_in"].n)
            for tt in range(2):
                turn(ps[:, 4, tt * P:(tt + 1) * P], W(5)[:, tt * P:(tt + 1) * P])
                for b in range(4):
                    last = turn(ps[:, 5 + tt, b * P:(b + 1) * P], W(14 + b)[:, tt * P:(tt + 1) * P])
            last.then_inc(v_turned, 1)
            pe.wait_ge(dup_copied, 1)
            pe.wait_ge(v_copied, 1)
            softmax_pe("swa", SWA_U, SWA_O,
                       lambda g, h, qt: [W(2 * g + h // 2)[64 * (h % 2):64 * (h % 2) + 64, qt * P:(qt + 1) * P]],
                       lambda g, h, br: [W(35 + g)[64 * (h % 2):64 * (h % 2) + 64, :]],
                       lambda g, h, kt, br: Wc(9472 + kt * P + g * 64, 64))
            pe.wait_ge(o_drained, 4)
            for st in range(6):
                if st < 4:
                    u = st
                    at_least(pe, z_masked, u)
                    for h in range(2):
                        rows = slice(64 * h, 64 * h + 64)
                        for kt in range(2):
                            last = mm(ps[:, h, kt * 256:(kt + 1) * 256], W(10 + u)[rows, kt * P:(kt + 1) * P], W(6 + u)[rows, :],
                                      start=True, stop=True)
                    last.then_inc(z_ready, 1)
                if 1 <= st < 5:
                    u = st - 1
                    pe.wait_ge(sp_ready, u + 1)
                    at_least(pe, d_ready, u)
                    sp_t = SB_T[u % 2]
                    for h in range(2):
                        lo_t, hi_t = sp_t[:, h * 512:h * 512 + 256], sp_t[:, h * 512 + 256:h * 512 + 512]
                        mm(ps[:, 2 + h, 0:256], C("ge"), lo_t, start=True, stop=False)
                        mm(ps[:, 2 + h, 0:256], C("ones"), hi_t, start=False, stop=True)
                        last = mm(ps[:, 2 + h, 256:512], C("ge"), hi_t, start=True, stop=True)
                    last.then_inc(cs_ready, 1)
                if st >= 2:
                    u = st - 2
                    pe.wait_ge(a_ready, u + 1)
                    o = SB_O + u
                    at_least(pe, o_drained, o - 1)
                    for h in range(2):
                        for kt in range(2):
                            last = mm(ps[64 * h:64 * h + 64, 4 + 2 * (o % 2), 0:256], Wc(9728 + kt * 512 + (2 * u + h) * 64, 64),
                                      PT[u % 2][:, h * 512 + kt * 256:h * 512 + (kt + 1) * 256], start=(kt == 0), stop=(kt == 1))
                    last.then_inc(sb_pv_done, 1)
            proj_pe("ab_out", 2, {1: lambda: norm_pe(1)})
            xa_pe(0, 3)
            norm_pe(3)
            ffn_pe(0, 6)
            norm_pe(4)
            def hg_turn_values():
                pe.wait_ge(banks_drained, PHASES["hg_in"].e + 12)
                for tt in range(2):
                    for b in range(8):
                        n = tt * 8 + b
                        last = turn(ps[:, 4 + n // 4, (n % 4) * P:(n % 4 + 1) * P], W(16 + b)[:, tt * P:(tt + 1) * P])
                last.then_inc(v_turned, 1)

            proj_pe("hg_in", 7, {12: hg_turn_values})
            pe.wait_ge(banks_drained, PHASES["hg_in"].e + PHASES["hg_in"].n)

            def hg_scores(bank, lhs, rhs, tiles):
                for h in range(8):
                    for n, tt in enumerate(tiles):
                        col = h * len(tiles) + n
                        last = mm(ps[:, bank + col // 4, (col % 4) * P:(col % 4 + 1) * P], lhs(h, tt[0]), rhs(h, tt[1]), start=True, stop=True)
                last.then_inc(hg_s, 1)

            pe.wait_ge(hg_kf, 1)
            hg_scores(0, lambda h, t: W(32 + h)[:, t * P:(t + 1) * P], lambda h, t: W(h)[:, t * P:(t + 1) * P], [(0, 0), (1, 1)])
            for lv in range(HG_LEVELS + 1):
                pe.wait_ge(hg_x, lv + 1)
                if lv == 0:
                    pe.wait_ge(v_copied, 3)
                else:
                    pe.wait_ge(hg_a, lv)
                both = lambda h, t: HG_D[lv % 2][:, h * BLK + t * P:h * BLK + (t + 1) * P]
                hg_scores(4 - 4 * (lv % 2), both, both, [(0, 1)] if lv == 0 else [(0, 0), (1, 1)])
            pe.wait_ge(hg_a, HG_LEVELS + 2)
            pe.wait_ge(v_copied, 3)
            A = lambda h, n: Wc(10240 + h * 384 + n * P, P)
            V = lambda h, t: Wc(13312 + t * 1024 + h * P, P)
            for h in range(8):
                o = lambda t: ps[:, h // 2, (h % 2) * 256 + t * P:(h % 2) * 256 + (t + 1) * P]
                mm(o(0), V(h, 0), A(h, 0), start=True, stop=True)
                mm(o(1), V(h, 0), A(h, 1), start=True, stop=False)
                last = mm(o(1), V(h, 1), A(h, 2), start=False, stop=True)
            last.then_inc(hg_o, 1)
            pe.wait_ge(hg_osq, 1)
            for h in range(8):
                last = mm(ps[:, 4 + h // 2, (h % 2) * 256:(h % 2 + 1) * 256], C("ones"), hf[:, h * BLK:(h + 1) * BLK],
                          start=True, stop=True)
            last.then_inc(hg_osum, 1)
            proj_pe("hg_out", 8, {1: lambda: norm_pe(5)})
            xa_pe(1, 9)
            norm_pe(7)
            ffn_pe(1, 12)
            ph = PHASES["pool"]
            pe.wait_ge(lo_ready, ph.g + 1)
            p = ph.g % DEPTH
            pe.wait_ge(banks_drained, ph.e)
            for g in range(4):
                pe.wait_ge(h_ready, QUARTERS * 12 + g + 1)
                for b in range(2):
                    for c in range(2):
                        w = slice(((g * 2 + b) * 2 + c) * P, ((g * 2 + b) * 2 + c + 1) * P)
                        m = slice((2 * g + c) * BLK, (2 * g + c + 1) * BLK)
                        last = split_mm(ps[:, g, b * BLK:(b + 1) * BLK], whi[p][:, w], wlo[p][:, w], hh[:, m], hl[:, m],
                                        c == 0, c == 1)
                last.then_inc(pool_ps if g < 3 else slot_used, 1)

            layer_norm_pe(0, lambda c: pe.wait_ge(pool_added, c + 1) if c < 3 else pe.wait_ge(banks_drained, ph.e + 1))
            ffn_pe(2, 14)
            layer_norm_pe(1, lambda c: pe.wait_ge(acc_drained, QUARTERS * 2 + c + 1))
            e_nsa = PHASES["nsa_in"].e

            def group_copies():
                pe.wait_ge(banks_drained, e_nsa + 6)
                for br in range(2):
                    for g in range(4):
                        last = mm(ps[:, 3 + g // 2 + 2 * br, (g % 2) * 256:(g % 2 + 1) * 256], C(f"dup{g % 2}"),
                                  W(8 + 2 * br + g // 2), start=True, stop=True)
                last.then_inc(cmp_dup, 1)

            def half_turns(which):
                for n in which:
                    for b in range(2):
                        last = mm(ps[:, ROPE_BANK[n], b * 256:(b + 1) * 256], C("rot"), W(ROPED[n] + b), start=True, stop=True)
                last.then_inc(rope_rot, 1)

            def gates_and_query_turns():
                pe.wait_ge(w1_loaded, 16)
                for tt in range(2):
                    for c in range(NB):
                        last = mm(ps[:, 7, tt * 48:(tt + 1) * 48], x[:, c * BLK + tt * P:c * BLK + (tt + 1) * P],
                                  Wc(12288 + c * 48, 48), start=(c == 0), stop=(c == NB - 1))
                last.then_inc(gates_ps, 1)
                pe.wait_ge(cmp_cols, 1)
                half_turns(range(4))

            def hidden_layers():
                pe.wait_ge(gates_ready, 1)
                for br in range(2):
                    for j in range(16):
                        cols = Wc(CMP_COLS[br], CMP_GROUPS * P).rearrange("p (g m) -> p g m", g=CMP_GROUPS)[:, :, j:j + 8 * (NCMP - 1) + 1:8]
                        last = mm(ps[:, 7, 128 * br + 128:128 * br + 128 + CMP_GROUPS * NCMP], Wc(8192 + 2048 * br + j * P, P), cols,
                                  start=(j == 0), stop=(j == 15))
                last.then_inc(cmp_hidden, 1)

            proj_pe("nsa_in", 15, {6: group_copies, 7: gates_and_query_turns, 8: hidden_layers})
            pe.wait_ge(banks_drained, e_nsa + PHASES["nsa_in"].n)
            half_turns((4, 5))
            pe.wait_ge(cmp_silu, 1)
            mm(ps[:, 2, 0:60], R("w2_k", 0, 128), small[:, 160:220], start=True, stop=True)
            for g in range(4):
                last = mm(ps[0:NCMP, 2, 64 + g * 64:64 + (g + 1) * 64], small[:, 220 + g * NCMP:220 + (g + 1) * NCMP], R("w2_v", 0, 64),
                          start=True, stop=True)
            last.then_inc(cmp_kv, 1)
            pe.wait_ge(cmp_kv_copied, 1)
            mm(ps[:, 3, 0:60], C("rot"), small[:, 288:348], start=True, stop=True).then_inc(cmp_rot, 1)
            pe.wait_ge(cmp_roped, 1)
            for qt in range(2):
                for h in range(16):
                    g, rows = h // 4, slice(64 * (h % 2), 64 * (h % 2) + 64)
                    at = (qt * 8 + h // 2) * NCMP
                    last = mm(ps[:, 4 + h % 2, at:at + NCMP], W(h // 2)[rows, qt * P:(qt + 1) * P],
                              small[rows, 288 + g * 15:288 + g * 15 + 15], start=True, stop=True)
            last.then_inc(cmp_scores, 1)
            pe.wait_ge(heads_ready, 4)
            for n, b0 in enumerate((12, 16)):
                for g in range(4):
                    last = mm(ps[:, 2 * n + g // 2, (g % 2) * 256:(g % 2 + 1) * 256], C(f"dup{g % 2}"), W(b0 + g // 2),
                              start=True, stop=True)
            last.then_inc(dup_ready, 1)
            for n, b0 in enumerate((14, 18)):
                for tt in range(2):
                    for b in range(2):
                        last = turn(ps[:, 6 + n, (tt * 2 + b) * P:(tt * 2 + b + 1) * P], W(b0 + b)[:, tt * P:(tt + 1) * P])
            last.then_inc(v_turned, 1)
            pe.wait_ge(cmp_probs, 1)
            pe.wait_ge(dup_copied, 2)
            pe.wait_ge(v_copied, 5)
            for n in range(4):
                for h in range(8):
                    head = (n // 2) * 8 + h
                    last = turn(ps[0:NCMP, 2 * n + h // 4, (h % 4) * P:(h % 4 + 1) * P],
                                Wc(10240 + ((head % 2) * 16 + (n % 2) * 8 + head // 2) * NCMP, NCMP))
            last.then_inc(cmp_turned, 1)
            pe.wait_ge(cmp_ready, 1)
            softmax_pe("nsa", NSA_U, NSA_O,
                       lambda g, h, qt: [W(2 * g + h // 2)[64 * (h % 2):64 * (h % 2) + 64, qt * P:(qt + 1) * P]],
                       lambda g, h, br: [W(20 + 4 * br + g)[64 * (h % 2):64 * (h % 2) + 64, :]],
                       lambda g, h, kt, br: Wc(7168 + 512 * br + kt * 256 + g * 64, 64),
                       cmp=lambda g, h, qt: (rstd[0:NCMP, g * 64:(g + 1) * 64],
                                             Wc(PCT[g // 2] + ((g % 2) * 4 + h) * 256 + qt * P, P)[0:NCMP, :]))
            proj_pe("nsa_out", 16)
            layer_norm_pe(2, lambda c: pe.wait_ge(banks_drained, PHASES["nsa_out"].e + c + 1))
            for b in range(NB):
                if b % 2 == 0:
                    pe.wait_ge(x_ready, QUARTERS * 2 + b // 2 + 1)
                mm(ps[0:8, 0, 0:BLK], R("router", b * 8, 8), xb(b), start=(b == 0), stop=(b == NB - 1)).then_inc(logits_t, 1)
            pe.wait_ge(logits_kept, 1)
            for tt in range(2):
                last = nc.tensor.transpose(ps[:, 1, tt * 8:(tt + 1) * 8], W(56)[0:8, tt * P:(tt + 1) * P], C("ident")[0:8, 0:8])
            last.then_inc(logits_ps, 1)
            for tt in range(2):
                for c in range(NB):
                    last = turn(ps[:, 3 + 2 * tt + c // 4, (c % 4) * P:(c % 4 + 1) * P], x[:, c * BLK + tt * P:c * BLK + (tt + 1) * P])
            last.then_inc(x_turned, 1)
            pe.wait_ge(picked, 1)
            ind = small[:, 608:624]
            mm(ps[:, 1, 0:16], C("ge"), ind, start=True, stop=True)
            mm(ps[:, 1, 0:8], C("ones"), ind[:, 8:16], start=False, stop=True, skip_group_check=True)
            mm(ps[:, 1, 16:24], C("ones"), ind[:, 0:8], start=True, stop=False)
            last = mm(ps[:, 1, 16:24], C("ones"), ind[:, 8:16], start=False, stop=True)
            last.then_inc(counts_ps, 1)
            gu, down = PHASES["moe_gu"], PHASES["moe_down"]

            def few_gather(e):
                for c in range(NB):
                    for tt in range(2):
                        take = bass.ds(e * 256 + (FEW_TAKE + tt * P), P)
                        last = mm(ps[:, 5 + c // 4, (c % 4) * P:(c % 4 + 1) * P], FEW_TOK[:, tt * 1024 + c * P:tt * 1024 + (c + 1) * P],
                                  work[:, take], start=(tt == 0), stop=(tt == 1))
                last.then_inc(gathered_ps, 1)

            def split_x(out_ap, hi_x, lo_x, hi_w, lo_w, start, stop, **kw):
                mm(out_ap, hi_x, hi_w, start=start, stop=False, **kw)
                mm(out_ap, lo_x, hi_w, start=False, stop=False, **kw)
                return mm(out_ap, hi_x, lo_w, start=False, stop=stop, **kw)

            def few_gu(half, i, k, s):
                p = (gu.g + k) % DEPTH
                pe.wait_ge(few_lo[p], i * 2 + 2 + half * (2 * PER_HALF // DEPTH))
                pe.wait_ge(few_tok, s + 1 + half * HALF)
                by_in = lambda t: t[:, :].rearrange("p (b c n) -> p c b n", b=2, c=NB)
                for c in range(NB):
                    at = slice(c * P, (c + 1) * P)
                    last = split_x(ps[:, p, 0:2 * P].rearrange("p (b n) -> p b n", b=2), hh[:, at], hl[:, at], by_in(whi[p])[:, c],
                                   by_in(wlo[p])[:, c], start=(c == 0), stop=(c == NB - 1))
                last.then_inc(slot_used, 1)

            def few_turn(half, s, k):
                pe.wait_ge(few_tok, s + DEPTH + 1 + half * HALF)
                pe.wait_ge(act_ready, s + gu.a + half * HALF)
                turn(ps[:, 7, 0:P], Wc(FEW_TOK_ACT + P * ((gu.g + k) % DEPTH), P)).then_inc(few_turned, 1)

            def few_down(half, s):
                p = (down.g + s) % DEPTH
                pe.wait_ge(few_lo[p], 2 * ((HALF + s) // DEPTH + 1) + half * (2 * PER_HALF // DEPTH))
                for c in range(2):
                    pe.wait_ge(act_ready, 2 * s + c + 1 + gu.a + half * HALF)
                    for b in range(2):
                        w = slice(c * 1024 + b * 512, c * 1024 + (b + 1) * 512)
                        last = split_x(ps[:, 3 + b, :], few_act(ahi, 2 * s + c), few_act(alo, 2 * s + c), whi[p][:, w], wlo[p][:, w],
                                       start=False, stop=False, skip_group_check=True)
                last.then_inc(slot_used, 1)

            def few_zero(start, stop):
                for b in range(2):
                    last = mm(ps[:, 3 + b, :], zero[:, :], zero[:, :].unsqueeze(1).to_broadcast([P, 4, P]), start=start, stop=stop,
                              skip_group_check=True)
                return last

            def few_expert(e, more):
                pe.wait_ge(gathered, e + 1)
                pe.wait_ge(y_added, e + 1)
                few_zero(True, False)
                with pe.Fori(0, 2) as part:
                    half = e * 2 + part

                    def gu_and_turn(i, k, s):
                        few_gu(half, i, k, s)
                        if not isinstance(s, int) or s > 0:
                            few_turn(half, s - 1, (k - 1) % DEPTH)

                    slot_loop(pe, gu, gu_and_turn, peel=1)
                    for s in range(down.n):
                        few_down(half, s)
                        if s == 0:
                            few_turn(half, HALF - 1, (HALF - 1) % DEPTH)
                few_zero(False, True).then_inc(y_ready, 1)
                if more:
                    few_gather(e + 1)
                pe.wait_ge(y_kept, e + 1)
                for c in range(NB):
                    if more and c == 4:
                        pe.wait_ge(gathered, e + 2)
                    give = bass.ds(e * 256 + FEW_GIVE, 256)
                    last = mm(ps[:, 3 + c // 2, (c % 2) * 256:(c % 2 + 1) * 256], FEW_Y[:, c * P:(c + 1) * P], work[:, give],
                              start=True, stop=True)
                last.then_inc(spread_out, 1)

            with pe.If(few_flag(pe)):
                pe.wait_ge(places_built, 1)
                pe.wait_ge(x_tokens, 1)
                few_gather(0)
                pe.wait_ge(places_built, 2)
                for n, (bank, col) in enumerate(SPREAD_AT):
                    last = turn(ps[:, bank, col:col + P], FEW_WEIGHT[:, n * P:(n + 1) * P])
                    if n in (7, 11, 15):
                        last.then_inc(spread_ps, 1)
                pe.wait_ge(places_built, 3)
                pe.wait_ge(spread_ready, 3)
                with pe.Fori(0, EXPERTS - 1) as e:
                    few_expert(e, True)
                few_expert(EXPERTS - 1, False)
            with pe.Else():
                pe.wait_ge(x_tokens, 1)
                pe.wait_ge(cw_diag, 1)
                for n in range(4):
                    last = mm(ps[:, n, :], C("ones"), Wc(n * 512, 512), start=True, stop=True)
                last.then_inc(cw_ps, 1)
                pe.wait_ge(h_ready, QUARTERS * 17)
                pe.wait_ge(cw_ready, 1)
                acc_zero(True, False)
                with pe.Fori(0, EXPERTS) as e:
                    with pe.Fori(0, 2) as part:
                        half = e * 2 + part
                        slot_loop(pe, gu, lambda i, k, s: proj_slot(gu, k, s, half * PER_HALF, half * HALF))
                        slot_loop(pe, down, lambda i, k, s: down_slot(
                            down, k, s, lambda s, c: s * 2 + (gu.a + c + 1) + half * HALF, half * PER_HALF))
                acc_zero(False, True).then_inc(acc_ready, 1)
            layer_norm_pe(3, lambda c: pe.wait_ge(acc_drained, QUARTERS * 3 + c + 1))

        @block.vector
        def _(dve):
            chain, order = [0], [dve_step]
            V = nc.vector

            def step(ins):
                chain[0] = chain[0] + 1
                ins.then_inc(order[0], 1)

            def sync():
                dve.wait_ge(order[0], chain[0])

            def link(ins):
                step(ins)
                sync()

            def drain(ph, k, s, write, off_g=0):
                dve.wait_ge(slot_used, s + (ph.g + 1) + off_g)
                write((ph.g + k) % DEPTH, s).then_inc(banks_drained, 1)

            def proj_copy(name, b0, then=None):
                ph = PHASES[name]

                def write(bank, s):
                    at = bass.ds(s * 512 + b0 * BLK, 512) if not isinstance(s, int) else slice(s * 512 + b0 * BLK, s * 512 + b0 * BLK + 512)
                    return V.tensor_copy(work[:, at], ps[:, bank, :])

                def body(i, k, s):
                    drain(ph, k, s, write)
                    if then is not None and s in then:
                        then[s]()

                slot_loop(dve, ph, body, peel=straight(then))
                dve.wait_ge(banks_drained, ph.e + ph.n)

            def proj_add(name, alpha=1.0, square=False, then=None):
                ph = PHASES[name]

                def body(i, k, s):
                    drain(ph, k, s, lambda bank, s: V.scalar_tensor_tensor(
                        out=xs(s), in0=xs(s), scalar=alpha, in1=ps[:, bank, :], op0=ALU.mult, op1=ALU.add))
                    if square:
                        dve.wait_ge(banks_drained, ph.e + s + 1)
                        squares(x[:, :], s)
                    if then is not None and s in then:
                        then[s]()

                slot_loop(dve, ph, body)
                dve.wait_ge(banks_drained, ph.e + ph.n)

            def xs(s):
                return x[:, bass.ds(s * 512, 512)] if not isinstance(s, int) else x[:, s * 512:s * 512 + 512]

            def q4(t, c):
                return t[:, c * 512:(c + 1) * 512]

            def squares(src, c):
                V.tensor_tensor(q4(hf, c), q4(src, c), q4(src, c), ALU.mult).then_inc(squares_ready, 1)

            def all_squares(src):
                for c in range(QUARTERS):
                    squares(src, c)

            def staged(*stages):
                done = {}
                for t in range(QUARTERS + len(stages) - 1):
                    for j, stage_of in enumerate(stages):
                        c = t - j
                        if 0 <= c < QUARTERS:
                            if j:
                                dve.wait_ge(order[0], done[j - 1, c])
                            stage_of(c)
                            done[j, c] = chain[0]

            def to_hi(src):
                return lambda c: step(V.tensor_copy(q4(hh, c), q4(src, c)))

            def to_lo(src):
                return lambda c: V.tensor_tensor(q4(hl, c), q4(src, c), q4(hh, c).bitcast(F32), ALU.subtract).then_inc(h_ready, 1)

            def split_h(src):
                staged(to_hi(src), to_lo(src))

            def scaled(src, gain, at):
                def stage_of(c):
                    for b in (2 * c, 2 * c + 1):
                        step(V.scalar_tensor_tensor(out=hf[:, b * BLK:(b + 1) * BLK], in0=src[:, b * BLK:(b + 1) * BLK],
                                                    scalar=R(gain, at + b), in1=rstd[:, :], op0=ALU.mult, op1=ALU.mult))
                return stage_of

            def rms_norm(n, src, gain, at):
                dve.wait_ge(rstd_ready, n + 1)
                staged(scaled(src, gain, at), to_hi(hf), to_lo(hf))

            def norm_ahead(n, src, gain, at):
                dve.wait_ge(rstd_ready, n + 1)
                for c in range(QUARTERS):
                    scaled(src, gain, at)(c)

            def layer_norm(i, g_at, last=False):
                dve.wait_ge(mean_ready, i + 1)

                def centre(c):
                    for b in (2 * c, 2 * c + 1):
                        step(V.scalar_tensor_tensor(out=xb(b), in0=ps[:, MEAN_BANK[i], 0:BLK], scalar=-1.0 / D, in1=xb(b),
                                                    op0=ALU.mult, op1=ALU.add))

                staged(centre, lambda c: squares(x, c))
                dve.wait_ge(rstd_ready, 9 + i)

                def scale(c):
                    for b in (2 * c, 2 * c + 1):
                        step(V.scalar_tensor_tensor(out=xb(b), in0=xb(b), scalar=R("ln_g", g_at + b), in1=rstd[:, :],
                                                    op0=ALU.mult, op1=ALU.mult))

                def shift(c):
                    for b in (2 * c, 2 * c + 1):
                        ins = V.tensor_scalar(xb(b), xb(b), R("ln_b", g_at + b), None, ALU.add)
                    ins.then_inc(x_ready, 1)

                def hi_of(c):
                    dve.wait_ge(x_ready, QUARTERS * i + c + 1)
                    to_hi(x)(c)

                if last:
                    staged(scale, shift)
                    dve.wait_ge(x_ready, QUARTERS * (i + 1))
                else:
                    staged(scale, shift, hi_of, to_lo(x))

            def softmax_dve(kind, u0, o0, scale, mask, o_blocks):
                us = units(kind)
                branches = 2 if kind == "nsa" else 1
                for st in range(len(us) + 3):
                    if st < len(us):
                        u = u0 + st
                        g, qt, br = us[st]
                        pr, s0, nk = PROBS[u % 3], STATS[u % 3], P * key_tiles(kind, qt)
                        dve.wait_ge(scores_ready, u + 1)
                        at_least(dve, pt_ready, u - 2)
                        if mask is None:
                            V.tensor_scalar(pr, banks(0), scale, None, ALU.mult).then_inc(scores_masked, 1)
                        else:
                            V.scalar_tensor_tensor(out=r3(pr, 4)[:, :, 0:nk], in0=r3(banks(0), 4)[:, :, 0:nk], scalar=scale,
                                                   in1=mask(qt)[:, 0:nk].unsqueeze(1).to_broadcast([P, 4, nk]),
                                                   op0=ALU.mult, op1=ALU.add).then_inc(scores_masked, 1)
                        dve.wait_ge(scores_masked, u + 1)
                        link(V.tensor_reduce(small[:, s0:s0 + 4], r3(pr, 4)[:, :, 0:nk], AX, ALU.max))
                        if kind == "swa":
                            link(V.tensor_tensor(small[:, s0:s0 + 4], small[:, s0:s0 + 4], R("sinks", 4 * g, 4), ALU.max))
                            link(V.tensor_tensor(small[:, s0 + 8:s0 + 12], R("sinks", 4 * g, 4), small[:, s0:s0 + 4], ALU.subtract))
                        V.tensor_scalar(small[:, s0:s0 + 4], small[:, s0:s0 + 4], -1.0, None, ALU.mult).then_inc(negmax_ready, 1)
                    if 1 <= st <= len(us):
                        u = u0 + st - 1
                        g, qt, br = us[st - 1]
                        pr, s0, nk = PROBS[u % 3], STATS[u % 3], P * key_tiles(kind, qt)
                        dve.wait_ge(exp_done, u + 1)
                        if kind == "swa":
                            link(V.tensor_tensor(small[:, s0 + 4:s0 + 8], small[:, s0 + 4:s0 + 8], small[:, s0 + 12:s0 + 16], ALU.add))
                        link(V.reciprocal(small[:, s0 + 16:s0 + 20], small[:, s0 + 4:s0 + 8]))
                        if kind == "nsa":
                            at = 64 + qt * 48 + g * 12
                            coef = small[:, s0 + 16:s0 + 20].rearrange("p (par j) -> p par j", par=2)
                            link(V.tensor_tensor(coef, coef, small[:, at:at + 12].rearrange(
                                "p (j par b) -> p par j b", j=2, par=2)[:, :, :, br + 1], ALU.mult))
                        for h in range(4):
                            ins = V.tensor_scalar(pr[:, h * 256:h * 256 + nk], pr[:, h * 256:h * 256 + nk],
                                                  small[:, s0 + 16 + h:s0 + 17 + h], None, ALU.mult)
                        ins.then_inc(probs_ready, 1)
                    if st >= 3:
                        u = u0 + st - 3
                        g, qt, br = us[st - 3]
                        if br == branches - 1:
                            o = o0 + (st - 3) // branches
                            dve.wait_ge(pv_done, u + 1)
                            evacuate(o, o_blocks(g), qt * P, 4 + 2 * (o % 2))

            def evacuate(o, blocks, col, bank, width=P):
                b0, n = blocks
                view = lambda t: t[:, :].rearrange("p (b c) -> p b c", b=NB)[:, b0:b0 + n, col:col + width]
                src = banks(bank)[:, 0:n * width].rearrange("p (b c) -> p b c", b=n)
                link(V.tensor_copy(view(hh), src))
                V.tensor_tensor(view(hl), src, view(hh).bitcast(F32), ALU.subtract).then_inc(o_drained, 1)

            def conv_ffn(layer, l, alpha):
                conv = l is not None
                for i in range(4):
                    ph = PHASES[f"ffn{layer}_{i}"]
                    if ph.kind == "down":
                        continue
                    c0 = chain[0]
                    first = 0 if i == 0 else HALF

                    def body(i, k, s, ph=ph, c0=c0, first=first):
                        bank = (ph.g + k) % DEPTH
                        buf = Wc(512 * bank, 512)
                        f = Wc(1536 + 256 * bank, 256)
                        chain[0] = s * steps + c0
                        dve.wait_ge(slot_used, s + (ph.g + 1))
                        if conv:
                            for b in range(2):
                                p0 = b * FF + first
                                step(V.tensor_scalar(buf[:, b * BLK:(b + 1) * BLK], ps[:, bank, b * BLK:(b + 1) * BLK],
                                                     Rd("conv_w", l * 132 + 88 + p0, s), Rd("conv_b", l * 44 + p0, s), ALU.mult, ALU.add))
                            sync()
                            for tap in (1, 2):
                                for b in range(2):
                                    p0 = b * FF + first
                                    o = buf[:, b * BLK + tap:(b + 1) * BLK]
                                    ins = V.scalar_tensor_tensor(out=o, in0=ps[:, bank, b * BLK:(b + 1) * BLK - tap],
                                                                 scalar=Rd("conv_w", l * 132 + (2 - tap) * 44 + p0, s), in1=o,
                                                                 op0=ALU.mult, op1=ALU.add)
                                    if (tap, b) != (2, 1):
                                        step(ins)
                                if tap == 1:
                                    sync()
                            ins.then_inc(banks_drained, 1)
                            dve.wait_ge(banks_drained, s + (ph.e + 1))
                            dve.wait_ge(gate_act, s + (ph.a + 1))
                            link(V.tensor_tensor(f, buf[:, 0:BLK], buf[:, BLK:2 * BLK], ALU.mult))
                        else:
                            dve.wait_ge(gate_act, s + (ph.a + 1))
                            V.tensor_tensor(f, buf[:, 0:BLK], ps[:, bank, BLK:2 * BLK], ALU.mult).then_inc(banks_drained, 1)
                            dve.wait_ge(banks_drained, s + (ph.e + 1))
                        split_act(s, f)

                    steps = 7 if conv else 1
                    slot_loop(dve, ph, body)
                    chain[0] = c0 + steps * ph.n
                dve.wait_ge(acc_ready, layer + 1)
                for c in range(QUARTERS + 1):
                    if c < QUARTERS:
                        V.scalar_tensor_tensor(out=xs(c), in0=xs(c), scalar=alpha, in1=ps[:, 3 + c, :], op0=ALU.mult,
                                               op1=ALU.add).then_inc(acc_drained, 1)
                    if layer == 0 and c:
                        dve.wait_ge(acc_drained, c)
                        squares(x, c - 1)
                dve.wait_ge(acc_drained, QUARTERS * (layer + 1))

            def Rd(name, a, s):
                at = PARAM[name][0] + a
                return par[:, at + s:at + s + 1] if isinstance(s, int) else par[:, bass.ds(s + at, 1)]

            def split_act(s, f):
                at = slice(s * BLK, (s + 1) * BLK) if isinstance(s, int) else bass.ds(s * BLK, BLK)
                link(V.tensor_copy(ahi[:, at], f))
                V.tensor_tensor(alo[:, at], f, ahi[:, at].bitcast(F32), ALU.subtract).then_inc(act_ready, 1)

            def xa(layer, before):
                mem = W(24, 8)

                def mem_squares():
                    dve.wait_ge(mem_loaded, 16 * (layer + 1))
                    all_squares(mem)

                proj_add(before, then={0: mem_squares, 2: lambda: norm_ahead(layer * 4 + 1, mem, "norm_mem", layer * 8)})
                sync()
                split_h(hf)
                dve.wait_ge(h_ready, QUARTERS * (3 + 6 * layer))
                all_squares(x)
                proj_copy(f"kv{layer}", 0, {2: lambda: norm_ahead(layer * 4 + 2, x, "norm_cross", layer * 8)})
                sync()
                split_h(hf)
                V.tensor_tensor(W(32, 8), W(0, 8), W(0, 8), ALU.mult).then_inc(xa_squares, 1)
                e0 = PHASES[f"q{layer}"].e

                def query_squares(s):
                    if s == 0:
                        dve.wait_ge(h_ready, QUARTERS * (4 + 6 * layer))
                    dve.wait_ge(banks_drained, e0 + s + 1)
                    V.tensor_tensor(q4(hf, s), W(16 + 2 * s, 2), W(16 + 2 * s, 2), ALU.mult).then_inc(xa_squares, 1)

                def scale_heads(heads, blk, gain, r, after):
                    dve.wait_ge(xa_rstd, 3 * layer + after)
                    for h in heads:
                        for c in range(2):
                            ins = V.scalar_tensor_tensor(out=W(blk + 2 * h + c), in0=W(blk + 2 * h + c), scalar=R(gain, 2 * layer + c),
                                                         in1=W(r + h), op0=ALU.mult, op1=ALU.mult)
                    return ins

                def keep_values():
                    dve.wait_ge(v_turned, 2 + 2 * layer)
                    V.tensor_copy(W(24, 8), banks(4, 4)).then_inc(v_copied, 1)

                def after_slot(s):
                    query_squares(s)
                    if s == 0:
                        keep_values()
                    if s == 2:
                        scale_heads(range(4), 0, "xa_k", 46, 1)

                proj_copy(f"q{layer}", 16, {s: lambda s=s: after_slot(s) for s in range(4)})
                scale_heads((0, 1), 16, "xa_q", 42, 2)
                scale_heads((2, 3), 16, "xa_q", 42, 3).then_inc(heads_ready, 1)
                dve.wait_ge(heads_ready, 2 + layer)
                softmax_dve("xa", XA_U[layer], XA_O[layer], 256 ** -0.5, None, lambda g: (0, 8))
                attention_whole(XA_O[layer] + 2)
                proj_add(f"o{layer}", square=True)

            def attention_whole(outputs):
                dve.wait_ge(o_drained, outputs)
                V.memset(small[:, 639:640], 0.0).then_inc(h_ready, QUARTERS)

            def rope(dst, rot_ps, n, cos, sin, tmp):
                wide = lambda t: t.unsqueeze(1).to_broadcast([P, n, t.shape[-1]])
                link(V.tensor_tensor(r3(tmp, n), r3(rot_ps, n), wide(sin), ALU.mult))
                link(V.tensor_tensor(r3(dst, n), r3(dst, n), wide(cos), ALU.mult))
                return V.tensor_tensor(dst, dst, tmp, ALU.add)

            V.memset(zero[:, :].bitcast(F32), 0.0).then_inc(zero_ready, 1)
            dve.wait_ge(params_loaded, 32)
            dve.wait_ge(positions_loaded, 16)
            ang, turns, pos = W(43), W(44), W(42)
            link(V.tensor_copy(ang, pos.bitcast(I32)))
            link(V.tensor_scalar(ang, ang, C("invf"), None, ALU.mult))
            link(V.tensor_scalar(turns, ang, float(1.0 / (2.0 * np.pi)), ROUND, ALU.mult, ALU.add))
            link(V.tensor_scalar(turns, turns, ROUND, None, ALU.subtract))
            for part in TWO_PI:
                link(V.scalar_tensor_tensor(out=ang, in0=turns, scalar=-part, in1=ang, op0=ALU.mult, op1=ALU.add))
            link(V.tensor_scalar(W(33), ang, PI, -PI, ALU.min, ALU.max))
            link(V.tensor_scalar(ang, ang, float(np.pi / 2), None, ALU.add))
            link(V.tensor_scalar(turns, ang, PI, float(-2 * np.pi), ALU.is_gt, ALU.mult))
            link(V.tensor_tensor(ang, ang, turns, ALU.add))
            V.tensor_scalar(W(34), ang, PI, -PI, ALU.min, ALU.max).then_inc(angles_ready, 1)
            dve.wait_ge(x_loaded, 16)
            all_squares(x)
            rms_norm(0, x, "norm_mix", 0)

            def swa_squares():
                dve.wait_ge(banks_drained, 3)
                V.tensor_tensor(W(18, 5), W(0, 5), W(0, 5), ALU.mult).then_inc(head_sq, 1)

            def swa_normed():
                dve.wait_ge(head_rstd, 1)
                step(V.scalar_tensor_tensor(out=W(0, 4), in0=W(0, 4), scalar=R("swa_q"), in1=W(23, 4), op0=ALU.mult, op1=ALU.mult))
                V.scalar_tensor_tensor(out=W(4), in0=W(4), scalar=R("swa_k"), in1=W(27), op0=ALU.mult, op1=ALU.mult).then_inc(rope_in, 1)

            def swa_rope():
                dve.wait_ge(rope_in, 1)
                sync()
                dve.wait_ge(rope_rot, 1)
                dve.wait_ge(sines_ready, 1)
                rope(W(0, 5), banks(3, 3)[:, 0:5 * BLK], 5, W(34), W(33), W(28, 5)).then_inc(heads_ready, 1)

            def swa_keys_copied():
                dve.wait_ge(dup_ready, 1)
                V.tensor_copy(W(35, 2), ps[:, 3, :]).then_inc(dup_copied, 1)

            proj_copy("ab_in", 0, {2: swa_squares, 4: swa_normed, 6: swa_rope, 8: swa_keys_copied})
            step(V.tensor_scalar(W(6, 4), W(6, 4), 64 ** -0.5, None, ALU.mult))
            dve.wait_ge(v_turned, 1)
            step(V.tensor_copy(W(37), ps[:, 4, 0:256]))
            V.tensor_copy(W(38, 4), banks(5)).then_inc(v_copied, 1)
            dve.wait_ge(stage_loaded, 16)
            softmax_dve("swa", SWA_U, SWA_O, 64 ** -0.5, lambda qt: stage[:, qt * 256:(qt + 1) * 256], lambda g: (2 * g, 2))
            for st in range(6):
                if st < 4:
                    u = st
                    dve.wait_ge(z_ready, u + 1)
                    at_least(dve, a_ready, u - 2)
                    V.tensor_tensor(r3(PROBS[u % 3], 2), r3(banks(0), 2), stage[:, 512:1024].unsqueeze(1).to_broadcast([P, 2, 512]),
                                    ALU.add).then_inc(z_masked, 1)
                if 1 <= st < 5:
                    u = st - 1
                    z, t = PROBS[u % 3], SB_T[u % 2]
                    dve.wait_ge(soft_ready, u + 1)
                    V.scalar_tensor_tensor(out=t, in0=z, scalar=0.0, in1=t, op0=ALU.max, op1=ALU.add).then_inc(sp_ready, 1)
                    dve.wait_ge(cs_ready, u + 1)
                    V.tensor_tensor(z, z, banks(2), ALU.subtract).then_inc(d_ready, 1)
                if st >= 2:
                    u = st - 2
                    dve.wait_ge(sb_pv_done, u + 1)
                    o = SB_O + u
                    evacuate(o, (4 + u, 1), 0, 4 + 2 * (o % 2), BLK)
            attention_whole(SB_O + 4)
            xa(0, "ab_out")
            rms_norm(3, x, "norm_ffn", 0)
            conv_ffn(0, 0, 1.0)
            rms_norm(4, x, "norm_mix", 8)
            link(V.tensor_tensor(small[:, 408:416], R("lb", 0, 8), R("lb", 8, 8), ALU.max))
            step(V.tensor_tensor(small[:, 400:408], R("lb", 0, 8), small[:, 408:416], ALU.subtract))
            V.tensor_tensor(small[:, 408:416], R("lb", 8, 8), small[:, 408:416], ALU.subtract).then_inc(hg_lb, 1)
            dve.wait_ge(hg_lb_exp, 1)
            link(V.tensor_tensor(small[:, 440:448], small[:, 416:424], small[:, 424:432], ALU.add))
            link(V.reciprocal(small[:, 440:448], small[:, 440:448]))
            link(V.tensor_tensor(small[:, 432:440], small[:, 424:432], small[:, 440:448], ALU.mult))
            link(V.tensor_scalar(small[:, 440:448], small[:, 432:440], -1.0, 1.0, ALU.mult, ALU.add))

            def keys_and_decays():
                dve.wait_ge(hg_sig, 1)
                for h in range(8):
                    step(V.tensor_scalar(W(32 + h), W(32 + h), small[:, 440 + h:441 + h], None, ALU.mult))
                    ins = V.tensor_scalar(W(8 + h), W(8 + h), small[:, 440 + h:441 + h], small[:, 432 + h:433 + h], ALU.mult, ALU.add)
                    if h < 7:
                        step(ins)
                ins.then_inc(hg_kf, 1)
                dve.wait_ge(h_ready, QUARTERS * 7)
                link(V.memset(hf[:, :], 1.0))
                link(V.memset(hf[:, 0:NB * BLK:P], 0.0))
                step(V.memset(W(40, 12), 0.0))

            def scan_decays():
                dve.wait_ge(hg_log, 1)
                link(V.tensor_tensor_scan(W(8, 8), hf[:, :], W(8, 8), 0.0, ALU.mult, ALU.add))

            def values_and_first_decays():
                dve.wait_ge(v_turned, 3)
                V.tensor_copy(W(52, 8), banks(4, 4)).then_inc(v_copied, 1)
                decays(0)
                decays(1)

            A = W(40, 12).rearrange("p (h n t) -> p h n t", h=8, n=3)
            tiles = lambda t: t.rearrange("p (h n t) -> p h n t", h=8, n=2)
            b, q, key = W(8, 8), W(0, 8), W(32, 8)
            halves = lambda t, half: t.rearrange("p (n t) -> p n t", t=2 * half)

            def keep(lv, n, bank):
                dve.wait_ge(hg_s, n)
                mask = stage[:, lv * P:(lv + 1) * P].bitcast(I32)
                for tt in range(2):
                    ins = V.copy_predicated(A[:, :, 2 * tt, :], mask.unsqueeze(1).to_broadcast([P, 8, P]),
                                            tiles(banks(bank, 4))[:, :, tt, :])
                    if tt == 0:
                        step(ins)
                ins.then_inc(hg_a, 1)

            def decays(lv):
                d = HG_D[lv % 2]
                if lv == 0:
                    step(V.tensor_tensor(tiles(d)[:, :, 0, :], tiles(b)[:, :, 0, P - 1:P].to_broadcast([P, 8, P]),
                                         tiles(b)[:, :, 0, :], ALU.subtract))
                    V.tensor_copy(tiles(d)[:, :, 1, :], tiles(b)[:, :, 1, :]).then_inc(hg_d, 1)
                else:
                    half = P >> lv
                    V.tensor_tensor(halves(d, half), halves(b, half),
                                    halves(b, half)[:, :, half - 1:half].to_broadcast([P, NB * BLK // (2 * half), 2 * half]),
                                    ALU.subtract).then_inc(hg_d, 1)

            proj_copy("hg_in", 0, {8: keys_and_decays, 11: scan_decays, 13: values_and_first_decays})
            sync()
            dve.wait_ge(stage_loaded, 32)
            for lv in range(HG_LEVELS + 2):
                if lv <= HG_LEVELS:
                    half = P >> lv if lv else P
                    e_ = xk = HG_D[lv % 2]
                    dve.wait_ge(hg_e, lv + 1)
                    step(V.tensor_tensor(halves(xk, half)[:, :, 0:half], halves(e_, half)[:, :, 0:half],
                                         halves(key, half)[:, :, 0:half], ALU.mult))
                    V.tensor_tensor(halves(xk, half)[:, :, half:2 * half], halves(e_, half)[:, :, half:2 * half],
                                    halves(q, half)[:, :, half:2 * half], ALU.mult).then_inc(hg_x, 1)
                if lv == 0:
                    keep(0, 1, 0)
                if lv == 1:
                    dve.wait_ge(hg_s, 2)
                    V.tensor_copy(A[:, :, 1, :], r3(banks(4), 8)).then_inc(hg_a, 1)
                elif lv > 1:
                    dve.wait_ge(hg_a, lv)
                    keep(lv - 1, lv + 1, 4 - 4 * ((lv - 1) % 2))
                if lv + 2 <= HG_LEVELS:
                    dve.wait_ge(hg_s, lv + 2)
                    decays(lv + 2)
            dve.wait_ge(hg_o, 1)
            link(V.tensor_copy(W(16, 8), banks(0, 4)))
            V.tensor_tensor(hf[:, :], W(16, 8), W(16, 8), ALU.mult).then_inc(hg_osq, 1)
            dve.wait_ge(hg_gate, 1)
            dve.wait_ge(hg_orstd, 1)
            link(V.tensor_tensor(W(16, 8), W(16, 8), W(8, 8), ALU.mult))
            link(V.scalar_tensor_tensor(out=W(16, 8), in0=W(16, 8), scalar=R("o_norm"), in1=W(24, 8), op0=ALU.mult, op1=ALU.mult))
            split_h(W(16, 8))
            xa(1, "hg_out")
            rms_norm(7, x, "norm_ffn", 8)
            conv_ffn(1, 1, 1.0)
            pad = 16
            sums = [Wc(4352 * i, NB * (pad + BLK)).rearrange("p (b t) -> p b t", b=NB) for i in range(2)]
            for i in range(2):
                step(V.memset(sums[i][:, :, 0:pad], 0.0))
            dve.wait_ge(stage_loaded, 48)
            xp = x[:, :].rearrange("p (b t) -> p b t", b=NB)
            own = lambda t, g: t[:, 2 * g:2 * g + 2]

            def double(n):
                def stage_of(g):
                    if n <= g:
                        old, new = own(sums[n % 2], g), own(sums[(n + 1) % 2], g)
                        step(V.tensor_tensor(new[:, :, pad:], old[:, :, pad:], old[:, :, pad - (1 << n):pad + BLK - (1 << n)], ALU.add))
                return stage_of

            staged(lambda g: step(V.tensor_copy(own(sums[0], g)[:, :, pad:], own(xp, g))),
                   double(0), double(1), double(2), double(3),
                   lambda g: step(V.tensor_tensor(r3(q4(hf, g), 2), own(sums[(g + 1) % 2], g)[:, :, pad:],
                                                  stage[:, g * BLK:(g + 1) * BLK].unsqueeze(1).to_broadcast([P, 2, BLK]), ALU.mult)),
                   lambda g: step(V.tensor_tensor(q4(hf, g), q4(hf, g), xs(g), ALU.subtract)),
                   to_hi(hf), to_lo(hf))
            link(V.tensor_scalar(x[:, :], x[:, :], ALPHA, None, ALU.mult))
            for g in range(4):
                if g < 3:
                    dve.wait_ge(pool_ps, g + 1)
                else:
                    dve.wait_ge(slot_used, PHASES["pool"].g + 1)
                for c in (2 * g, 2 * g + 1):
                    ins = V.scalar_tensor_tensor(out=xb(c), in0=ps[:, c // 2, (c % 2) * BLK:(c % 2 + 1) * BLK],
                                                 scalar=R("pool_scale", c), in1=xb(c), op0=ALU.mult, op1=ALU.add)
                ins.then_inc(pool_added if g < 3 else banks_drained, 1)
            dve.wait_ge(pool_added, 3)
            dve.wait_ge(banks_drained, PHASES["pool"].e + 1)
            layer_norm(0, 0)
            conv_ffn(2, None, ALPHA)
            layer_norm(1, 8)

            def cmp_clear():
                for br in range(2):
                    step(V.memset(Wc(CMP_COLS[br] + 4 * P, 3 * P), 0.0))
                sync()
                for br, pe_name in enumerate(("pe_k", "pe_v")):
                    step(V.tensor_copy(Wc(CMP_COLS[br] + 4 * P, 16), R(pe_name, 0, 16)))

            def cmp_columns():
                dve.wait_ge(cmp_dup, 1)
                for br in range(2):
                    for odd in range(2):
                        rows = slice(64 * odd, 64 * odd + 64)
                        ins = V.tensor_copy(Wc(CMP_COLS[br], 512)[rows, :].rearrange("p (g m) -> p g m", g=4),
                                            banks(3 + 2 * br)[rows, :].rearrange("p (g m two) -> p g m two", g=4, two=2)[:, :, :, odd])
                        if (br, odd) != (1, 1):
                            step(ins)
                ins.then_inc(cmp_cols, 1)

            def nsa_rope(which, turned):
                dve.wait_ge(rope_rot, turned)
                dve.wait_ge(stage_loaded, 64)
                for n in which:
                    ins = rope(W(ROPED[n], 2), ps[:, ROPE_BANK[n], :], 2, stage[:, 512:768], stage[:, 768:1024], W(50 + 2 * (n % 2), 2))
                    if n < 5:
                        step(ins)
                return ins

            proj_copy("nsa_in", 0, {1: cmp_clear, 7: cmp_columns, 8: lambda: nsa_rope(range(4), 2)})
            dve.wait_ge(cmp_hidden, 1)
            V.tensor_copy(small[:, 280:282], ps[:, 7, 188:317:128]).then_inc(cmp_bias, 1)
            nsa_rope((4, 5), 3).then_inc(heads_ready, 1)
            dve.wait_ge(cmp_kv, 1)
            step(V.tensor_copy(rstd[0:NCMP, :], ps[0:NCMP, 2, 64:320]))
            V.tensor_copy(small[:, 288:348], ps[:, 2, 0:60]).then_inc(cmp_kv_copied, 1)
            dve.wait_ge(cmp_rot, 1)
            dve.wait_ge(cmp_kv_copied, 1)
            rope(small[:, 288:348], ps[:, 3, 0:60], 4, C("cend_cos"), C("cend_sin"), small[:, 348:408]).then_inc(cmp_roped, 1)
            dve.wait_ge(cmp_scores, 1)
            rows_of = lambda t: t.rearrange("p (h n) -> p h n", n=NCMP)
            wide = lambda t: t.unsqueeze(2).to_broadcast([P, 32, NCMP])
            pc = Wc(10240, 480)
            for n in range(4):
                odd, qt = n // 2, n % 2
                step(V.scalar_tensor_tensor(out=rows_of(pc[:, n * 120:(n + 1) * 120]),
                                            in0=rows_of(ps[:, 4 + odd, qt * 120:(qt + 1) * 120]), scalar=64 ** -0.5,
                                            in1=C("cmp_mask", qt * 15, 15).unsqueeze(1).to_broadcast([P, 8, NCMP]),
                                            op0=ALU.mult, op1=ALU.add))
            sync()
            link(V.tensor_reduce(small[:, 512:544], rows_of(pc), AX, ALU.max))
            V.tensor_tensor(rows_of(pc), rows_of(pc), wide(small[:, 512:544]), ALU.subtract).then_inc(cmp_shifted, 1)
            dve.wait_ge(cmp_exp, 1)
            link(V.tensor_reduce(small[:, 544:576], rows_of(pc), AX, ALU.add))
            link(V.reciprocal(small[:, 544:576], small[:, 544:576]))
            dve.wait_ge(gates_ready, 1)
            for n in range(4):
                odd, qt = n // 2, n % 2
                rows = small[:, 544 + 8 * n:552 + 8 * n]
                step(V.scalar_tensor_tensor(out=rows, in0=rows, scalar=C("cmp_any", qt, 1),
                                            in1=small[:, 64 + qt * 48 + odd * 3:64 + qt * 48 + odd * 3 + 43:6],
                                            op0=ALU.mult, op1=ALU.mult))
            sync()
            V.tensor_tensor(rows_of(pc), rows_of(pc), wide(small[:, 544:576]), ALU.mult).then_inc(cmp_probs, 1)
            dve.wait_ge(dup_ready, 2)
            V.tensor_copy(W(20, 8), banks(0, 4)).then_inc(dup_copied, 1)
            dve.wait_ge(v_turned, 5)
            V.tensor_copy(W(28, 4), banks(6, 2)).then_inc(v_copied, 1)
            dve.wait_ge(cmp_turned, 1)
            for n in range(4):
                ins = V.tensor_copy(r3(Wc(PCT[n // 2], 2048)[0:NCMP, :], 8)[:, :, (n % 2) * P:(n % 2 + 1) * P],
                                    banks(2 * n)[0:NCMP, :].rearrange("p (h t) -> p h t", h=8))
                if n < 3:
                    step(ins)
            ins.then_inc(cmp_ready, 1)
            softmax_dve("nsa", NSA_U, NSA_O, 64 ** -0.5, lambda qt: stage[:, qt * 256:(qt + 1) * 256], lambda g: (2 * g, 2))
            attention_whole(NSA_O + 8)
            proj_add("nsa_out", ALPHA)
            layer_norm(2, 16, last=True)
            dve.wait_ge(logits_t, NB)
            V.tensor_copy(W(56)[0:8, :], ps[0:8, 0, 0:BLK]).then_inc(logits_kept, 1)
            dve.wait_ge(logits_ps, 1)
            link(V.tensor_copy(small[:, 448:464], ps[:, 1, 0:16]))
            for tt in range(2):
                step(V.max(small[:, 464 + 8 * tt:472 + 8 * tt], small[:, 448 + 8 * tt:456 + 8 * tt]))
            sync()
            for tt in range(2):
                step(V.max_index(idx[:, 8 * tt:8 * tt + 8], small[:, 464 + 8 * tt:472 + 8 * tt], small[:, 448 + 8 * tt:456 + 8 * tt]))
            sync()
            step(V.tensor_copy(small[:, 480:496], idx[:, :]))
            V.tensor_tensor(small[:, 504:506], small[:, 465:474:8], small[:, 464:473:8], ALU.subtract).then_inc(top2_diff, 1)
            sync()
            dve.wait_ge(top2_exp, 1)
            link(V.tensor_scalar(small[:, 506:508], small[:, 504:506], 1.0, None, ALU.add))
            link(V.reciprocal(small[:, 506:508], small[:, 506:508]))
            link(V.tensor_tensor(small[:, 508:510], small[:, 504:506], small[:, 506:508], ALU.mult))
            for tt in range(2):
                link(V.tensor_scalar(small[:, 576 + 8 * tt:584 + 8 * tt], C("iota8"), small[:, 480 + 8 * tt:481 + 8 * tt],
                                     small[:, 506 + tt:507 + tt], ALU.is_equal, ALU.mult))
                link(V.tensor_scalar(small[:, 592 + 8 * tt:600 + 8 * tt], C("iota8"), small[:, 481 + 8 * tt:482 + 8 * tt],
                                     small[:, 508 + tt:509 + tt], ALU.is_equal, ALU.mult))
            link(V.tensor_tensor(small[:, 576:592], small[:, 576:592], small[:, 592:608], ALU.add))
            V.tensor_scalar(small[:, 608:624], small[:, 576:592], 0.0, None, ALU.is_gt).then_inc(picked, 1)
            dve.wait_ge(counts_ps, 1)
            step(V.tensor_reduce(small[:, 472:473], ps[:, 1, 16:24], AX, ALU.max))
            dve.wait_ge(picked, 1)
            step(V.tensor_tensor(small[:, 448:464], ps[:, 1, 0:16], small[:, 608:624], ALU.mult))
            sync()
            V.tensor_scalar(few[:, :], small[:, 472:473], float(P), None, ALU.is_le).then_inc(few_ready, 1)
            gu, down = PHASES["moe_gu"], PHASES["moe_down"]
            with dve.If(few_flag(dve)):
                def take_of(n):
                    at, place_at = FEW_TAKE + n * P, 448 + (n % 2) * 8 + n // 2
                    return V.tensor_scalar(work[:, at:at + P], C("places"), small[:, place_at:place_at + 1], None, ALU.is_equal)

                def keep_gathered(e):
                    dve.wait_ge(gathered_ps, e + 1)
                    V.tensor_copy(hh[:, 0:1024], banks(5)).then_inc(few_x_hi, 1)
                    dve.wait_ge(few_x_hi, e + 1)
                    V.tensor_tensor(hl[:, 0:1024], banks(5), hh[:, 0:1024].bitcast(F32), ALU.subtract).then_inc(gathered, 1)

                V.memset(small[:, 638:639], 0.0).then_inc(few_tok, DEPTH)
                take_of(0)
                take_of(1).then_inc(places_built, 1)
                for n in range(16):
                    place_at, weight_at = 448 + (n % 2) * 8 + n // 2, 576 + (n % 2) * 8 + n // 2
                    ins = V.tensor_scalar(FEW_WEIGHT[:, n * P:(n + 1) * P], C("places"), small[:, place_at:place_at + 1],
                                          small[:, weight_at:weight_at + 1], ALU.is_equal, ALU.mult)
                ins.then_inc(places_built, 1)
                keep_gathered(0)
                for n in range(2, 16):
                    ins = take_of(n)
                ins.then_inc(places_built, 1)
                dve.wait_ge(x_turned, 1)
                V.tensor_scalar(x[:, :], x[:, :], ALPHA, None, ALU.mult).then_inc(y_added, 1)

                def few_keep_act(half, s):
                    at = slice(s * P, (s + 1) * P) if isinstance(s, int) else bass.ds(s * P, P)
                    dve.wait_ge(few_turned, s + 1 + half * HALF)
                    V.tensor_copy(ahi[:, at], ps[:, 7, 0:P]).then_inc(few_act_hi, 1)
                    dve.wait_ge(few_act_hi, s + 1 + half * HALF)
                    V.tensor_tensor(alo[:, at], ps[:, 7, 0:P], ahi[:, at].bitcast(F32), ALU.subtract).then_inc(act_ready, 1)

                def few_split_lo(ph, k, s, half):
                    p = (ph.g + k) % DEPTH
                    own = slice(0, LO_CUT)
                    dve.wait_ge(hi_ready, s + (ph.g + DEPTH + 1) + half * PER_HALF)
                    V.tensor_tensor(wlo[p][:, own], raw[p][:, own], whi[p][:, own].bitcast(F32), ALU.subtract).then_inc(few_lo[p], 1)

                def few_expert(e, more):
                    with dve.Fori(0, 2) as part:
                        half = e * 2 + part

                        def body(i, k, s):
                            bank = (gu.g + k) % DEPTH
                            dve.wait_ge(gate_act, s + (gu.a + 1) + half * HALF)
                            V.tensor_tensor(Wc(FEW_TOK_ACT + P * bank, P), Wc(FEW_GATE + P * bank, P), ps[:, bank, P:2 * P],
                                            ALU.mult).then_inc(few_tok, 1)
                            if not isinstance(s, int) or s > 0:
                                few_keep_act(half, s - 1)
                            few_split_lo(gu, k, s, half)

                        slot_loop(dve, gu, body, peel=1)
                        for s in range(down.n):
                            few_split_lo(down, s, s, half)
                            if s == 0:
                                few_keep_act(half, HALF - 1)
                    dve.wait_ge(y_ready, e + 1)
                    V.tensor_copy(FEW_Y, banks(3)).then_inc(y_kept, 1)
                    if more:
                        keep_gathered(e + 1)
                    dve.wait_ge(spread_out, e + 1)
                    dve.wait_ge(y_added, e + 1)
                    V.tensor_tensor(x[:, :], x[:, :], banks(3, 4), ALU.add).then_inc(y_added, 1)

                with dve.Fori(0, EXPERTS - 1) as e:
                    few_expert(e, True)
                few_expert(EXPERTS - 1, False)
                dve.wait_ge(y_added, EXPERTS + 1)
                V.memset(small[:, 638:639], 0.0).then_inc(acc_drained, QUARTERS)
            with dve.Else():
                split_h(x)
                for tt in range(2):
                    ins = V.tensor_tensor(r3(Wc(tt * 1024, 1024), 8), C("ident").unsqueeze(1).to_broadcast([P, 8, P]),
                                          small[:, 576 + 8 * tt:584 + 8 * tt].unsqueeze(2).to_broadcast([P, 8, P]), ALU.mult)
                    if tt == 0:
                        step(ins)
                ins.then_inc(cw_diag, 1)
                dve.wait_ge(cw_ps, 1)
                cw = W(16, 8)
                for tt in range(2):
                    ins = V.tensor_copy(r3(cw, 8)[:, :, tt * P:(tt + 1) * P], r3(banks(2 * tt), 8))
                    if tt == 0:
                        step(ins)
                ins.then_inc(cw_ready, 1)
                dve.wait_ge(cw_ready, 1)
                c0 = chain[0]
                with dve.Fori(0, EXPERTS) as e:
                    with dve.Fori(0, 2) as part:
                        half = e * 2 + part

                        def body(i, k, s):
                            bank = (gu.g + k) % DEPTH
                            f = Wc(1536 + 256 * bank, 256)
                            chain[0] = s * 2 + c0 + half * (2 * HALF)
                            dve.wait_ge(gate_act, s + (gu.a + 1) + half * HALF)
                            V.tensor_tensor(f, Wc(512 * bank, BLK), ps[:, bank, BLK:2 * BLK], ALU.mult).then_inc(banks_drained, 1)
                            dve.wait_ge(banks_drained, s + (gu.e + 1) + half * HALF)
                            link(V.tensor_tensor(f, f, work[:, bass.ds(e * BLK + 16 * BLK, BLK)], ALU.mult))
                            split_act(s, f)

                        slot_loop(dve, gu, body)
                dve.wait_ge(acc_ready, 4)
                for c in range(QUARTERS):
                    V.scalar_tensor_tensor(out=xs(c), in0=xs(c), scalar=ALPHA, in1=ps[:, 3 + c, :], op0=ALU.mult,
                                           op1=ALU.add).then_inc(acc_drained, 1)
            dve.wait_ge(acc_drained, QUARTERS * 4)
            chain[0], order[0] = 0, last_step
            layer_norm(3, 24, last=True)


SINK_ORDER = [0, 2, 1, 3, 4, 6, 5, 7]


def _block_slots(m):
    k, n = m.shape
    b = m.reshape(k // P, P, n // P, P).transpose(1, 2, 0, 3)
    return b.reshape(P, n // P // 2, SLOT).transpose(1, 0, 2)


def _gu_slots(m):
    k, n = m.shape
    b = m.reshape(k // P, P, 2, n // P // 2, P).transpose(3, 1, 2, 0, 4)
    return b.reshape(n // P // 2, P, SLOT)


def _down_slots(m):
    k, n = m.shape
    b = m.reshape(k // P // 2, 2, P, n // P, P).transpose(0, 2, 1, 3, 4)
    return b.reshape(k // P // 2, P, SLOT)


def _ffn_slots(gu, down):
    g, d = _gu_slots(gu), _down_slots(down)
    parts = []
    for a in range(0, g.shape[0], HALF):
        b = min(a + HALF, g.shape[0])
        parts += [g[a:b], d[a // 2:b // 2]]
    return parts


def _columns(v):
    return v.reshape(-1, P).T


def _channel_major(a):
    return a.reshape(T, NB, P).transpose(2, 1, 0).reshape(P, NB * T)


def _constants():
    i = np.arange(P)
    freq = (np.float32(10000.0) ** (-np.arange(0, 64, 2, dtype=np.float32) / np.float32(64))).astype(np.float32)
    lane = freq[i % 32][:, None]
    rot = np.zeros((P, P), np.float32)
    first = (i % 64) < 32
    rot[i[first] + 32, i[first]] = -1.0
    rot[i[~first] - 32, i[~first]] = 1.0
    cend = 16 * np.arange(NCMP, dtype=np.float32) + 31
    t = np.arange(T)
    cmp_valid = (16 * np.arange(NCMP)[None] + 31) <= t[:, None]
    c = {
        "ident": np.eye(P), "ones": np.ones((P, P)), "ones64": (i[:, None] // 64 == i[None] // 64), "rot": rot,
        "dup0": i[:, None] == (i[None] % 64), "dup1": i[:, None] == 64 + (i[None] % 64),
        "ge": i[:, None] >= i[None], "invf": lane, "eps6": np.full((P, 1), 1e-6), "eps5": np.full((P, 1), 1e-5),
        "cend_cos": np.cos(lane * cend[None]), "cend_sin": np.sin(lane * cend[None]),
        "cmp_mask": np.where(cmp_valid, 0.0, MASKED).reshape(2, P, NCMP).transpose(1, 0, 2).reshape(P, 30),
        "cmp_any": cmp_valid.any(1).reshape(2, P).T, "iota8": np.broadcast_to(np.arange(8), (P, 8)),
        "places": np.broadcast_to(np.arange(1, P + 1), (P, P)),
    }
    consts = np.concatenate([np.asarray(c[n], np.float32) for n in CONST], 1)
    q, k = t[:, None], t[None]
    swa = (k <= q) & (k + P > q)
    by_query = lambda m: np.where(m, 0.0, MASKED).reshape(2, P, T).transpose(1, 0, 2).reshape(P, 512)
    attn = np.concatenate([by_query(swa), by_query(k > q)], 1)
    levels = [np.eye(P)]
    for lv in range(1, HG_LEVELS + 1):
        half = P >> lv
        s_, t_ = i[:, None], i[None]
        levels.append((s_ // (2 * half) == t_ // (2 * half)) & (s_ % (2 * half) < half) & (t_ % (2 * half) >= half))
    pool = np.concatenate([np.broadcast_to(1.0 / np.minimum(t + 1, w), (P, T)) for w in (2, 4, 8, 16)], 1)
    ang = lane * t[None].astype(np.float32)
    nsa = np.concatenate([by_query(k <= q), np.cos(ang), np.sin(ang)], 1)
    stages = [attn, np.concatenate(levels, 1), pool, nsa]
    return consts, np.stack([np.asarray(s, np.float32) for s in stages])


def _stream(v):
    parts = [_block_slots(v["ab_w_in"][0]), _block_slots(v["ab_w_out"][0])]
    for layer in range(2):
        if layer == 1:
            parts += [_block_slots(v["hgrn_w_in"][0]), _block_slots(v["hgrn_w_out"][0])]
        parts += [_block_slots(v["xa_w_kv"][layer]), _block_slots(v["xa_w_q"][layer]), _block_slots(v["xa_w_o"][layer])]
        parts += _ffn_slots(v["ffn_w_up"][layer], v["ffn_w_down"][layer])
    parts += [v["pool_w_2"][0].reshape(4, 2, P, 2, P).transpose(2, 0, 3, 1, 4).reshape(1, P, SLOT)]
    parts += _ffn_slots(v["ffn_w_gu_2"][0], v["ffn_w_down_2"][0])
    parts += [_block_slots(v["nsa_w_in_2"][0][:, :20 * P]), _block_slots(v["nsa_w_out_2"][0])]
    for e in range(EXPERTS):
        parts += _ffn_slots(v["moe_w_gu_2"][0, e], v["moe_w_down_2"][0, e])
    parts += [np.zeros((DEPTH, P, SLOT), np.float32)]
    return np.concatenate(parts)


def kernel(**inputs):
    import concourse.bacc as bacc
    from concourse.bass_utils import run_bass_kernel_spmd

    v = {k: np.asarray(a) for k, a in inputs.items()}
    stream = _stream(v)
    twice = lambda a: np.concatenate([a, a], -1)
    p = {
        "norm_mix": _columns(v["norm_mix"]), "norm_cross": _columns(v["norm_cross"]), "norm_mem": _columns(v["norm_mem"]),
        "norm_ffn": _columns(v["norm_ffn"]), "swa_q": _columns(twice(v["swa_q_norm"][0])), "swa_k": _columns(twice(v["swa_k_norm"][0])),
        "sinks": np.broadcast_to(v["swa_sinks"][0][SINK_ORDER], (P, 8)), "o_norm": _columns(v["hgrn_o_norm"][0]), "lb": _columns(v["hgrn_lb"]),
        "xa_q": _columns(v["xa_q_norm"]), "xa_k": _columns(v["xa_k_norm"]), "conv_w": _columns(v["ffn_conv_w"]),
        "conv_b": _columns(v["ffn_conv_b"]), "ln_g": _columns(v["ln_g_2"]), "ln_b": _columns(v["ln_b_2"]),
        "pool_scale": _columns(v["pool_scale_2"][0]),
        "router": v["moe_router_2"][0].reshape(NB, P, 8).transpose(1, 0, 2).reshape(P, 64),
        "pe_k": _columns(v["nsa_pe_k_2"][0]), "pe_v": _columns(v["nsa_pe_v_2"][0]),
        "w2_k": twice(v["nsa_w2_k_2"][0]), "w2_v": v["nsa_w2_v_2"][0],
    }
    params = np.concatenate([p[n] for n in PARAM], 1)
    w1 = [v[n][0].reshape(16, P, P).transpose(1, 0, 2).reshape(P, 2048) for n in ("nsa_w1_k_2", "nsa_w1_v_2")]
    gates = v["nsa_w_in_2"][0][:, 20 * P:].reshape(NB, P, 48).transpose(1, 0, 2).reshape(P, 384)
    consts, stages = _constants()
    arrays = {
        "stream": stream, "x_in": _channel_major(v["x"][0]), "mem_in": _channel_major(v["mem"][0]),
        "pos_in": np.broadcast_to(v["positions"][0], (P, T)), "params": params, "consts": consts, "stage_consts": stages,
        "w1_in": np.concatenate(w1 + [gates], 1),
    }
    arrays = {k: np.ascontiguousarray(a) for k, a in arrays.items()}
    nc = bacc.Bacc("TRN2", target_bir_lowering=False, num_devices=1)
    args = [nc.dram_tensor(k, a.shape, mybir.dt.from_np(a.dtype), kind="ExternalInput").ap() for k, a in arrays.items()]
    out = nc.dram_tensor("out", (P, NB * T), F32, kind="ExternalOutput").ap()
    build(nc, *args, out)
    r = run_bass_kernel_spmd(nc, [arrays], core_ids=[0])
    got = r.results[0]["out"]
    return got.reshape(P, NB, T).transpose(2, 1, 0).reshape(1, T, D)
```
